# Optimizing a Trainium2 kernel written in Bass

```python
import jax, jax.numpy as jnp
from jax import lax
import numpy as np

D_MODEL = 1024
BATCH = 1
SEQ = 512
DEPTH = 1

GMLP_GROUPS = 4
GMLP_GROUP_DIM = 128
GMLP_WIDTH = GMLP_GROUPS * GMLP_GROUP_DIM
CHUNK = 128
N_HEADS = 8
Q_RANK = 256
KV_RANK = 128
HEAD_V = 64
ATTN_WIDTH = N_HEADS * HEAD_V
IDX_HEADS = 4
IDX_DIM = 64
TOPK_MAX = 256
Q_BLOCK = 128
N_EXPERTS = 32
TOP_K = 4
D_EXPERT = 1024
SWIGLU_LIMIT = 7.0
SWIGLU_ALPHA = 1.702
MOE_BLOCK = 128
EPS = 1e-6

OFF_UV = 0
OFF_CQ = OFF_UV + 2 * GMLP_WIDTH
OFF_CKV = OFF_CQ + Q_RANK
OFF_KIDX = OFF_CKV + KV_RANK
OFF_WIDX = OFF_KIDX + IDX_DIM
OFF_GATE = OFF_WIDX + IDX_HEADS
IN_WIDTH = OFF_GATE + 2 * D_MODEL

kernel_name = "hybrid_gmlp_dsa_moe_block"

def rms_norm(x, g):
    xf = x.astype(jnp.float32)
    y = xf * lax.rsqrt(jnp.mean(xf * xf, axis=-1, keepdims=True) + EPS)
    return (y * g.astype(jnp.float32)).astype(x.dtype)

def gmlp_mixer(uv, v_g, w_s, b_s):
    B, S, _ = uv.shape
    z = jax.nn.gelu(uv)
    u, v = z[..., :GMLP_WIDTH], z[..., GMLP_WIDTH:]
    v = v.reshape(B, S // CHUNK, CHUNK, GMLP_GROUPS, GMLP_GROUP_DIM)
    v = rms_norm(v, v_g)
    causal = jnp.tril(jnp.ones((CHUNK, CHUNK), dtype=bool))
    w = jnp.where(causal[None], w_s, jnp.zeros_like(w_s)).astype(v.dtype)
    sv = jnp.einsum('gts,bcsgd->bctgd', w, v) + b_s.T[None, None, :, :, None].astype(v.dtype)
    return u * sv.reshape(B, S, GMLP_WIDTH)

def dsa_mixer(q, kv, q_idx, k_idx, w_idx, w_uv):
    B, S, H, C = q.shape
    nb = S // Q_BLOCK
    k_top = min(TOPK_MAX, S // 4)
    scale = C ** -0.5
    k_idx_f = k_idx.astype(jnp.float32)
    key_pos = jnp.arange(S)

    def to_blocks(a):
        return jnp.moveaxis(a.reshape((B, nb, Q_BLOCK) + a.shape[2:]), 1, 0)

    def attn_block(args):
        blk, qb, qib, wb = args
        t = blk * Q_BLOCK + jnp.arange(Q_BLOCK)
        logits = jnp.einsum('bqhd,bsd->bqhs', qib.astype(jnp.float32), k_idx_f) * (IDX_DIM ** -0.5)
        score = jnp.einsum('bqhs,bqh->bqs', jax.nn.relu(logits), wb.astype(jnp.float32))
        causal = key_pos[None, :] <= t[:, None]
        score = jnp.where(causal[None], score, -jnp.inf)
        _, idx = lax.top_k(score, k_top)
        valid = idx <= t[None, :, None]
        kv_sel = jax.vmap(lambda kv_b, i_b: kv_b[i_b])(kv, idx).astype(jnp.float32)
        s = jnp.einsum('bqhc,bqkc->bhqk', qb.astype(jnp.float32), kv_sel) * scale
        s = jnp.where(valid[:, None], s, -jnp.inf)
        p = jax.nn.softmax(s, axis=-1)
        o = jnp.einsum('bhqk,bqkc->bqhc', p, kv_sel)
        return o.astype(q.dtype)

    o = lax.map(attn_block, (jnp.arange(nb), to_blocks(q), to_blocks(q_idx), to_blocks(w_idx)))
    o = jnp.moveaxis(o, 0, 1).reshape(B, S, H, C)
    o = jnp.einsum('bshc,hcv->bshv', o, w_uv)
    return o.reshape(B, S, ATTN_WIDTH)

def moe(xn, w_router, b_router, w_exp1, b_exp1, w_exp2, b_exp2):
    B, S, D = xn.shape
    T = B * S
    xt = xn.reshape(T, D)
    logits = (xt @ w_router + b_router).astype(jnp.float32)
    top_val, top_idx = lax.top_k(logits, TOP_K)
    gates = jax.nn.softmax(top_val, axis=-1)
    P = T * TOP_K
    flat_e = top_idx.reshape(P)
    flat_tok = jnp.repeat(jnp.arange(T, dtype=jnp.int32), TOP_K)
    flat_g = gates.reshape(P)
    order = jnp.argsort(flat_e, stable=True)
    se = flat_e[order]
    counts = jnp.bincount(flat_e, length=N_EXPERTS)
    padded = (counts + MOE_BLOCK - 1) // MOE_BLOCK * MOE_BLOCK
    pad_end = jnp.cumsum(padded)
    pad_start = pad_end - padded
    grp_start = jnp.cumsum(counts) - counts
    dest = pad_start[se] + (jnp.arange(P) - grp_start[se])
    n_blocks = -(-P // MOE_BLOCK) + N_EXPERTS
    n_rows = n_blocks * MOE_BLOCK
    row_tok = jnp.full((n_rows,), T, dtype=jnp.int32).at[dest].set(flat_tok[order])
    row_gate = jnp.zeros((n_rows,), jnp.float32).at[dest].set(flat_g[order])
    blk_start = jnp.arange(n_blocks) * MOE_BLOCK
    blk_e = jnp.minimum(jnp.searchsorted(pad_end, blk_start, side='right'), N_EXPERTS - 1)
    x_pad = jnp.concatenate([xt, jnp.zeros((1, D), xt.dtype)], axis=0)

    def expert_block(args):
        tok, g, e = args
        xb = x_pad[tok]
        hb = xb @ w_exp1[e] + b_exp1[e]
        hg = jnp.minimum(hb[:, :D_EXPERT], SWIGLU_LIMIT)
        hu = jnp.clip(hb[:, D_EXPERT:], -SWIGLU_LIMIT, SWIGLU_LIMIT)
        act = (hu + 1.0) * (hg * jax.nn.sigmoid(SWIGLU_ALPHA * hg))
        y = act @ w_exp2[e] + b_exp2[e]
        return y * g[:, None].astype(y.dtype)

    ys = lax.map(expert_block, (row_tok.reshape(n_blocks, MOE_BLOCK),
                                row_gate.reshape(n_blocks, MOE_BLOCK), blk_e))
    out = jax.ops.segment_sum(ys.reshape(n_rows, D), row_tok, num_segments=T + 1)[:T]
    return out.reshape(B, S, D)

def setup_inputs(seed: int = 0) -> dict:
    key = jax.random.key(seed)
    ks = jax.random.split(key, 24)
    f32 = jnp.float32

    def nrm(k, shape, fan_in):
        return jax.random.normal(k, shape, f32) * (fan_in ** -0.5)

    def gain(k, n):
        return 1.0 + 0.1 * jax.random.normal(k, (n,), f32)

    return {
        "x": jax.random.normal(ks[0], (BATCH, SEQ, D_MODEL), f32),
        "norm1_g": gain(ks[1], D_MODEL),
        "w_in": nrm(ks[2], (D_MODEL, IN_WIDTH), D_MODEL),
        "q_lat_g": gain(ks[3], Q_RANK),
        "w_uq": nrm(ks[4], (Q_RANK, N_HEADS, KV_RANK), Q_RANK),
        "q_norm_g": gain(ks[5], KV_RANK),
        "kv_norm_g": gain(ks[6], KV_RANK),
        "w_uv": nrm(ks[7], (N_HEADS, KV_RANK, HEAD_V), KV_RANK),
        "w_q_idx": nrm(ks[8], (Q_RANK, IDX_HEADS, IDX_DIM), Q_RANK),
        "k_idx_g": gain(ks[9], IDX_DIM),
        "gmlp_v_g": gain(ks[10], GMLP_GROUP_DIM),
        "w_spatial": nrm(ks[11], (GMLP_GROUPS, CHUNK, CHUNK), CHUNK),
        "b_spatial": 1.0 + 0.1 * jax.random.normal(ks[12], (GMLP_GROUPS, CHUNK), f32),
        "w_proj_a": nrm(ks[13], (GMLP_WIDTH, D_MODEL), GMLP_WIDTH),
        "w_proj_b": nrm(ks[14], (ATTN_WIDTH, D_MODEL), ATTN_WIDTH),
        "w_out": nrm(ks[15], (D_MODEL, D_MODEL), D_MODEL),
        "norm2_g": gain(ks[16], D_MODEL),
        "w_router": nrm(ks[17], (D_MODEL, N_EXPERTS), D_MODEL),
        "b_router": 0.01 * jax.random.normal(ks[18], (N_EXPERTS,), f32),
        "w_exp1": nrm(ks[19], (N_EXPERTS, D_MODEL, 2 * D_EXPERT), D_MODEL),
        "b_exp1": 0.01 * jax.random.normal(ks[20], (N_EXPERTS, 2 * D_EXPERT), f32),
        "w_exp2": nrm(ks[21], (N_EXPERTS, D_EXPERT, D_MODEL), D_EXPERT),
        "b_exp2": 0.01 * jax.random.normal(ks[22], (N_EXPERTS, D_MODEL), f32),
    }

def reference(x, norm1_g, w_in, q_lat_g, w_uq, q_norm_g, kv_norm_g, w_uv, w_q_idx, k_idx_g,
              gmlp_v_g, w_spatial, b_spatial, w_proj_a, w_proj_b, w_out, norm2_g,
              w_router, b_router, w_exp1, b_exp1, w_exp2, b_exp2):
    for _ in range(DEPTH):
        xn = rms_norm(x, norm1_g)
        h = xn @ w_in
        y_a = gmlp_mixer(h[..., OFF_UV:OFF_CQ], gmlp_v_g, w_spatial, b_spatial)
        c_q = rms_norm(h[..., OFF_CQ:OFF_CKV], q_lat_g)
        q = rms_norm(jnp.einsum('bsr,rhc->bshc', c_q, w_uq), q_norm_g)
        kv = rms_norm(h[..., OFF_CKV:OFF_KIDX], kv_norm_g)
        q_idx = jnp.einsum('bsr,rhd->bshd', c_q, w_q_idx)
        k_idx = rms_norm(h[..., OFF_KIDX:OFF_WIDX], k_idx_g)
        w_idx = h[..., OFF_WIDX:OFF_GATE] * (IDX_HEADS ** -0.5)
        y_b = dsa_mixer(q, kv, q_idx, k_idx, w_idx, w_uv)
        g_a = jax.nn.sigmoid(h[..., OFF_GATE:OFF_GATE + D_MODEL])
        g_b = jax.nn.sigmoid(h[..., OFF_GATE + D_MODEL:IN_WIDTH])
        merged = g_a * (y_a @ w_proj_a) + g_b * (y_b @ w_proj_b)
        x = x + merged @ w_out
        x = x + moe(rms_norm(x, norm2_g), w_router, b_router, w_exp1, b_exp1, w_exp2, b_exp2)
    return x


_drawn_inputs = setup_inputs


def setup_inputs(seed=0):
    import zlib

    import numpy as np

    out = dict(_drawn_inputs(seed))
    spreads = {}
    factors = {'b_exp1': 8.0, 'b_exp2': 8.0}
    for name, (base, spread) in spreads.items():
        noise = np.random.default_rng([zlib.crc32(name.encode()), seed]).standard_normal(out[name].shape)
        drawn = base * np.exp(spread * noise) if base else spread * noise
        out[name] = __import__('jax').numpy.asarray(drawn.astype(out[name].dtype))
    for name, factor in factors.items():
        out[name] = (out[name] * factor).astype(out[name].dtype)
    return out
```

```python
from contextlib import ExitStack

import concourse.bass as bass
from concourse import mybir

P = 128
D = 1024
S = 512
NT = S // P
KD = D // P
G = 4
H = 8
QR = 256
KVR = 128
HV = 64
IH = 4
ID = 64
TOPK = 128
NE = 32
TK = 4
DE = 1024
LIMIT = 7.0
ALPHA = 1.702
EPS = 1e-6
OFF_U, OFF_V, OFF_LAT = 0, 512, 1024
LAT = QR + KVR + ID + IH
C_KV, C_KI, C_WI = QR, QR + KVR, QR + KVR + ID
OFF_GATE = OFF_LAT + LAT
NEG = -1.0e30
TAKEN = -3.0e38
TAKEN_BELOW = -2.0e38
BIG = 4096.0
UNITS = 12
UW = 2048
NEP = NE + 2
OVER = 15

F32 = mybir.dt.float32
BF16 = mybir.dt.bfloat16
I32 = mybir.dt.int32
U32 = mybir.dt.uint32
ALU = mybir.AluOpType
ACT = mybir.ActivationFunctionType
AX = mybir.AxisListType


class Steps:

    def __init__(self, engine, semaphore):
        self.engine, self.semaphore, self.n = engine, semaphore, 0
        self.past = None

    def __call__(self, instruction):
        self.n += 1
        instruction.then_inc(self.semaphore, 1)
        self.engine.wait_ge(self.semaphore, self.n if self.past is None else self.past + self.n)

    def enter(self, turns, per_turn):
        self.first, self.per_turn, self.past = self.n, per_turn, turns * per_turn

    def leave(self, count):
        assert self.n - self.first == self.per_turn, (self.n - self.first, self.per_turn)
        self.n = self.first + count * self.per_turn
        self.past = None


def build(nc, x, norm1_g, w_in, q_lat_g, w_uq, q_norm_g, kv_norm_g, w_uv, w_q_idx, k_idx_g,
          gmlp_v_g, w_spatial, b_spatial, w_proj_a, w_proj_b, w_out, norm2_g,
          w_router, b_router, w_exp1, b_exp1, w_exp2, b_exp2, out):
    xn2_rows = nc.dram_tensor("xn2_rows", (S, D), F32, kind="Internal").ap()
    pair_rows = nc.dram_tensor("pair_rows", (S * TK, D), F32, kind="Internal").ap()
    x_rows = x.rearrange("a (t p) d -> p (a t) d", p=P)
    out_rows = out.rearrange("a (t p) d -> p (a t) d", p=P)

    with ExitStack() as whole:
        def keep(name, shape, dt=F32):
            return whole.enter_context(nc.sbuf_tensor(name, shape, dt))

        def sem(name):
            return whole.enter_context(nc.semaphore(name))

        banks = [whole.enter_context(nc.psum_tensor(f"bank{i}", [P, 512], F32)) for i in range(8)]
        ring = keep("ring", [P, UNITS, UW])
        x_sb = keep("x_sb", [P, NT, D])
        ident = keep("ident", [P, P])
        ones = keep("ones", [P, P])
        cols = keep("cols", [P, 21])
        wr_sb = keep("wr_sb", [P, KD, NE])
        br_sb = keep("br_sb", [P, NE])
        over_flag = keep("over_flag", [P, 1], I32)
        w_landed = [sem(f"w_landed{j}") for j in range(UNITS)]
        N1, N2, QL, QN, VG, KI = 0, 8, 16, 18, 19, 20

        def w1_src(e, k):
            return w_exp1[e, k * P:(k + 1) * P, :]

        def w2_src(e, q):
            return w_exp2[e, 2 * q * P:2 * (q + 1) * P, :].rearrange("(k p) n -> p k n", p=P)

        def unit_dst(j):
            return ring[:, j, :] if j < 8 else ring[:, j, :].rearrange("p (k n) -> p k n", k=2)

        mixers(nc, sem, banks, ring, x_sb, ident, ones, cols, wr_sb, br_sb, w_landed, (N1, N2, QL, QN, VG, KI),
               w1_src, w2_src, unit_dst, x_rows, norm1_g, w_in, q_lat_g, w_uq, q_norm_g, kv_norm_g, w_uv,
               w_q_idx, k_idx_g, gmlp_v_g, w_spatial, b_spatial, w_proj_a, w_proj_b, w_out, norm2_g,
               w_router, b_router)

        n2col = cols[:, N2:N2 + KD]
        tab = keep("tab", [P, NT, 3, NEP])
        rk = keep("rk", [P, NT, NEP])
        bias = keep("bias", [96, 2 * DE + D], BF16)
        eq = keep("eq", [96, NEP])
        slot_iota = keep("slot_iota", [P, P])
        counts = keep("counts", [P, NE])
        routing(nc, sem, banks, x_sb, ident, ones, cols, N2, wr_sb, br_sb, tab, rk, bias, eq, slot_iota,
                counts, over_flag, xn2_rows, b_exp1, b_exp2)
        experts(nc, sem, banks, ring, ident, n2col, tab, rk, bias, eq, slot_iota, counts, over_flag,
                w_landed, unit_dst, xn2_rows, pair_rows, w_exp1, w_exp2)
        beyond = nc.values_load(over_flag[0:1, 0:1], min_val=0, max_val=1)
        with nc.If(beyond > 0):
            further_blocks(nc, sem, banks, ring, ident, n2col, tab, rk, bias, eq, slot_iota, counts, over_flag,
                           unit_dst, xn2_rows, pair_rows, w_exp1, w_exp2)
        combine(nc, sem, ring, x_sb, pair_rows, out_rows)


def mixers(nc, sem, banks, ring, x_sb, ident, ones, cols, wr_sb, br_sb, w_landed, col_of,
           w1_src, w2_src, unit_dst, x_rows, norm1_g, w_in, q_lat_g, w_uq, q_norm_g, kv_norm_g, w_uv,
           w_q_idx, k_idx_g, gmlp_v_g, w_spatial, b_spatial, w_proj_a, w_proj_b, w_out, norm2_g,
           w_router, b_router):
    N1, N2, QL, QN, VG, KI = col_of
    with ExitStack() as ctx:
        def sb(name, shape, dt=F32):
            return ctx.enter_context(nc.sbuf_tensor(name, shape, dt))

        xnT = sb("xnT", [P, KD, S])
        gaT = sb("gaT", [P, KD, S])
        gbT = sb("gbT", [P, KD, S])
        uT = sb("uT", [P, G, S])
        v_sb = sb("v_sb", [P, NT, S])
        lat = sb("lat", [P, 2048])
        cqT = sb("cqT", [P, 2, S])
        kvT = sb("kvT", [P, S])
        kidxT = sb("kidxT", [ID, S])
        kv = sb("kv", [P, NT, KVR])
        wuv = sb("wuv", [P, H, P])
        bspat = sb("bspat", [P, G, P])
        wsT = sb("wsT", [P, G, P])
        kvg = sb("kvg", [P, KVR])
        vecs = sb("vecs", [21, P])
        ss = sb("ss", [P, 48])
        widx = sb("widx", [P, NT, IH])
        top8 = sb("top8", [P, 8])
        mx = sb("mx", [P, NT, H])
        den = sb("den", [P, NT, H])
        qs = sb("qs", [P, NT, H])

        lat_sb = lat[:, 0:NT * LAT].rearrange("p (t n) -> p t n", t=NT)
        qidxT = gbT[0:ID, 0:4, :]
        relu = gbT[:, 4:8, :]
        pT = x_sb[:, 0:2, :].rearrange("p a (b n) -> p (a b) n", b=2)
        mask = x_sb[:, 2:4, :].rearrange("p a (b n) -> p (a b) n", b=2)
        probs = [v_sb[:, :, :], lat[:, :].rearrange("p (h n) -> p h n", h=4)]
        oT = xnT
        ybT = uT
        qT = ring[:, 10:12, :].rearrange("p a (b n) -> p (a b) n", b=4)
        wuq = ring[:, 6, :].rearrange("p (k n) -> p k n", k=2)
        wqi = ring[:, 7, 0:512].rearrange("p (k n) -> p k n", k=2)
        wsp = ring[:, 7, 512:1024].rearrange("p (g n) -> p g n", g=G)
        qsq = ring[:, 7, 1024:2048].rearrange("p (a n) -> p a n", a=2)

        def chunk(u, n):
            return ring[:, u:u + 2, :].rearrange("p a b -> p (a b)")[:, 0:n]

        w_lat = chunk(0, KD * LAT).rearrange("p (k n) -> p k n", k=KD)
        w_v = chunk(2, KD * 512).rearrange("p (k n) -> p k n", k=KD)
        w_u = chunk(4, KD * 512).rearrange("p (k n) -> p k n", k=KD)
        gate_unit = [8, 0, 2, 4]
        w_gate = [chunk(u, KD * 512).rearrange("p (k n) -> p k n", k=KD) for u in gate_unit]
        wpa = chunk(6, G * D).rearrange("p (k n) -> p k n", k=G)
        wpb = chunk(8, G * D).rearrange("p (k n) -> p k n", k=G)
        wout = ring[:, 0:4, :].rearrange("p a (b n) -> p (a b) n", b=2)

        def in_cols(c, n):
            return w_in[:, c:c + n].rearrange("(k p) n -> p k n", p=P)

        x_loaded = sem("x_loaded")
        vecs_loaded = sem("vecs_loaded")
        lat_w_loaded = sem("lat_w_loaded")
        qw_loaded = sem("qw_loaded")
        first_loaded = sem("first_loaded")
        small_loaded = sem("small_loaded")
        v_w_loaded = sem("v_w_loaded")
        u_w_loaded = sem("u_w_loaded")
        gate_w_loaded = [sem(f"gate_w_loaded{i}") for i in range(4)]
        pa_loaded = sem("pa_loaded")
        pb_loaded = sem("pb_loaded")
        out_w_loaded = sem("out_w_loaded")
        x_again = sem("x_again")
        consts_set = sem("consts_set")
        vecs_zeroed = sem("vecs_zeroed")
        wuv_zeroed = sem("wuv_zeroed")
        masked = sem("masked")
        colsT_ready, cols_set = sem("colsT_ready"), sem("cols_set")
        x_squared, x_root, x_scaled = sem("x_squared"), sem("x_root"), sem("x_scaled")
        xT_ready, xT_taken = sem("xT_ready"), sem("xT_taken")
        lat_ready, lat_copied = sem("lat_ready"), sem("lat_copied")
        lat_squared, lat_root, lat_scaled = sem("lat_squared"), sem("lat_root"), sem("lat_scaled")
        latT_ready, latT_taken = sem("latT_ready"), sem("latT_taken")
        qidx_ready, qidx_copied = sem("qidx_ready"), sem("qidx_copied")
        logit_ready, relu_done, score_done = sem("logit_ready"), sem("relu_done"), sem("score_done")
        q_ready, q_copied, q_squared = sem("q_ready"), sem("q_copied"), sem("q_squared")
        qss_ready, qss_copied, q_root, q_scale_set = (sem("qss_ready"), sem("qss_copied"), sem("q_root"),
                                                      sem("q_scale_set"))
        wsT_ready, wsT_copied = sem("wsT_ready"), sem("wsT_copied")
        v_ready, v_gelu, v_squared, v_root, v_scaled = (
            sem("v_ready"), sem("v_gelu"), sem("v_squared"), sem("v_root"), sem("v_scaled"))
        u_ready, u_gelu = sem("u_ready"), sem("u_gelu")
        gate_ready, gate_taken = sem("gate_ready"), sem("gate_taken")
        mix_ready, ya_set = sem("mix_ready"), sem("ya_set")
        pa_ready, pa_taken = sem("pa_ready"), sem("pa_taken")
        mask_set = sem("mask_set")
        s_ready, s_masked, bias_set, exp_done = sem("s_ready"), sem("s_masked"), sem("bias_set"), sem("exp_done")
        inv_set, p_scaled = sem("inv_set"), sem("p_scaled")
        pT_ready, pT_taken = sem("pT_ready"), sem("pT_taken")
        o_ready, o_taken = sem("o_ready"), sem("o_taken")
        yb_ready, yb_taken = sem("yb_ready"), sem("yb_taken")
        pb_ready, merged = sem("pb_ready"), sem("merged")
        x2_ready, x2_taken = sem("x2_ready"), sem("x2_taken")
        dve_step = sem("dve_step")

        QBLOCKS = [3, 2, 1]
        HALVES = [(b, g) for b in range(NT) for g in range(2)]
        PT_BEFORE = [sum(b + 1 for b, _ in HALVES[:i]) for i in range(len(HALVES) + 1)]
        MV = 16

        def act_half(i, act):
            b, g = HALVES[i]
            for kt in range(b + 1):
                j = PT_BEFORE[i] + kt
                act.wait_ge(pT_ready, j + 1)
                if i >= 1:
                    act.wait_ge(o_ready, i)
                act.activation(pT[:, kt, :], banks[4 + j % 2][:, :], ACT.Copy).then_inc(pT_taken, 1)
            act.wait_ge(o_ready, i + 1)
            act.activation(oT[:, 4 * g:4 * g + 4, b * P:(b + 1) * P],
                           banks[6 + g][:, :].rearrange("p (h q) -> p h q", h=4), ACT.Copy).then_inc(o_taken, 1)

        def inverse(dve, i):
            b, g = HALVES[i]
            dve.wait_ge(exp_done, 4 * i + 4)
            dve.reciprocal(den[:, b, 4 * g:4 * g + 4], den[:, b, 4 * g:4 * g + 4]).then_inc(inv_set, 1)

        block = ctx.enter_context(nc.Block())

        @block.sync
        def _(sp):
            for t in range(NT):
                sp.dma_start(x_sb[:, t, :], x_rows[:, t, :]).then_inc(x_loaded, 16)
            sp.wait_ge(vecs_zeroed, 1)
            for at, vec, n in ((N1, norm1_g, 8), (N2, norm2_g, 8), (QL, q_lat_g, 2), (QN, q_norm_g, 1),
                               (VG, gmlp_v_g, 1)):
                sp.dma_start(vecs[at:at + n, :], vec.rearrange("(a p) -> a p", p=P)).then_inc(vecs_loaded, 16)
            sp.dma_start(vecs[KI:KI + 1, 0:ID], k_idx_g.rearrange("(a p) -> a p", a=1)).then_inc(vecs_loaded, 16)
            sp.dma_start(w_lat, in_cols(OFF_LAT, LAT)).then_inc(lat_w_loaded, 16)
            sp.dma_start(kvg[:, :], kv_norm_g.rearrange("(a p) -> a p", a=1).to_broadcast([P, KVR])
                         ).then_inc(first_loaded, 16)
            sp.dma_start(wqi, w_q_idx.rearrange("(k p) h d -> p k (h d)", p=P)).then_inc(qw_loaded, 16)
            sp.dma_start(wuq, w_uq.rearrange("(k p) h d -> p k (h d)", p=P)).then_inc(qw_loaded, 16)
            sp.dma_start(wsp, w_spatial.rearrange("g t s -> t g s")).then_inc(first_loaded, 16)
            sp.dma_start(w_v, in_cols(OFF_V, 512)).then_inc(v_w_loaded, 16)
            sp.dma_start(w_u, in_cols(OFF_U, 512)).then_inc(u_w_loaded, 16)
            sp.dma_start(bspat[:, :, :].rearrange("p g t -> p (g t)"),
                         b_spatial.rearrange("(a g) t -> a (g t)", a=1).to_broadcast([P, G * P])
                         ).then_inc(small_loaded, 16)
            sp.dma_start(br_sb[:, :], b_router.rearrange("(a n) -> a n", a=1).to_broadcast([P, NE])
                         ).then_inc(small_loaded, 16)
            sp.dma_start(wr_sb[:, :, :], w_router.rearrange("(k p) n -> p k n", p=P)).then_inc(small_loaded, 16)
            sp.wait_ge(wuv_zeroed, 1)
            for h in range(H):
                sp.dma_start(wuv[:, h, HV * (h % 2):HV * (h % 2) + HV], w_uv[h]).then_inc(small_loaded, 16)
            for i in range(4):
                if i == 1:
                    sp.wait_ge(lat_ready, NT)
                if i == 2:
                    sp.wait_ge(v_ready, NT)
                if i == 3:
                    sp.wait_ge(u_ready, G)
                sp.dma_start(w_gate[i], in_cols(OFF_GATE + 512 * i, 512)).then_inc(gate_w_loaded[i], 16)
            sp.wait_ge(q_ready, H)
            sp.wait_ge(qss_ready, H)
            sp.wait_ge(wsT_ready, G)
            sp.dma_start(wpa, w_proj_a.rearrange("(k p) n -> p k n", p=P)).then_inc(pa_loaded, 16)
            sp.wait_ge(gate_ready, 4)
            sp.dma_start(wpb, w_proj_b.rearrange("(k p) n -> p k n", p=P)).then_inc(pb_loaded, 16)
            wo_rows = w_out.rearrange("(k p) n -> p k n", p=P)
            for i in range(2):
                sp.wait_ge(gate_ready, 8 + 4 * i)
                sp.dma_start(wout[:, 4 * i:4 * i + 4, :], wo_rows[:, 4 * i:4 * i + 4, :]).then_inc(out_w_loaded, 16)
            sp.wait_ge(gate_ready, 16)
            for j in (4, 5):
                sp.dma_start(unit_dst(j), w1_src(0, j)).then_inc(w_landed[j], 16)
            sp.wait_ge(pa_ready, KD)
            for j in (6, 7):
                sp.dma_start(unit_dst(j), w1_src(0, j)).then_inc(w_landed[j], 16)
            sp.wait_ge(o_ready, len(HALVES))
            sp.wait_ge(s_masked, NT * H)
            sp.wait_ge(pT_ready, PT_BEFORE[-1])
            for t in range(NT):
                sp.dma_start(x_sb[:, t, :], x_rows[:, t, :]).then_inc(x_again, 16)
            for j in (10, 11):
                sp.dma_start(unit_dst(j), w2_src(0, j - 8)).then_inc(w_landed[j], 16)
            sp.wait_ge(pb_ready, KD)
            for j in (8, 9):
                sp.dma_start(unit_dst(j), w2_src(0, j - 8)).then_inc(w_landed[j], 16)
            sp.wait_ge(x2_ready, 2 * NT)
            for j in (0, 1, 2, 3):
                sp.dma_start(unit_dst(j), w1_src(0, j)).then_inc(w_landed[j], 16)
            sp.wait_ge(x_again, 16 * NT)
            sp.wait_ge(small_loaded, 16 * 11)

        @block.gpsimd
        def _(pool):
            pool.memset(vecs[:, :], 0.0).then_inc(vecs_zeroed, 1)
            pool.memset(ident[:, :], 0.0).then_inc(consts_set, 1)
            pool.memset(ones[:, :], 1.0).then_inc(consts_set, 1)
            pool.wait_ge(consts_set, 2)
            pool.affine_select(out=ident[:, :], in_=ident[:, :], compare_op=ALU.not_equal, fill=1.0, base=0,
                               pattern=[[-1, P]], channel_multiplier=1).then_inc(consts_set, 1)
            pool.wait_ge(first_loaded, 16 * 2)
            pool.affine_select(out=wsp, in_=wsp, compare_op=ALU.is_ge, fill=0.0, base=0,
                               pattern=[[0, G], [-1, P]], channel_multiplier=1).then_inc(masked, 1)
            pool.wait_ge(xT_ready, 2 * NT)
            pool.memset(mask[:, 0, 0:P], 0.0).then_inc(masked, 1)
            pool.wait_ge(masked, 2)
            pool.affine_select(out=mask[:, 0, 0:P], in_=mask[:, 0, 0:P], compare_op=ALU.is_ge, fill=NEG,
                               base=0, pattern=[[-1, P]], channel_multiplier=1).then_inc(masked, 1)
            for n, b in enumerate(QBLOCKS):
                pool.wait_ge(score_done, n + 1)
                diag = mask[:, b, b * P:(b + 1) * P]
                pool.affine_select(out=diag, in_=diag, compare_op=ALU.is_ge, fill=NEG,
                                   base=0, pattern=[[-1, P]], channel_multiplier=1).then_inc(masked, 1)
            for i, (b, g) in enumerate(HALVES):
                n = (b + 1) * P
                for h in range(4):
                    hh = 4 * g + h
                    pool.wait_ge(inv_set, i + 1)
                    pool.tensor_scalar(probs[i % 2][:, h, 0:n], probs[i % 2][:, h, 0:n], den[:, b, hh:hh + 1], None,
                                       ALU.mult).then_inc(p_scaled, 1)

        @block.scalar
        def _(act):
            for t in range(NT):
                act.wait_ge(x_loaded, 16 * NT)
                act.activation(gaT[:, 2 * t:2 * t + 2, :].rearrange("p a b -> p (a b)"), x_sb[:, t, :], ACT.Square,
                               accum_out=ss[:, 12 + t:13 + t]).then_inc(x_squared, 1)
            act.wait_ge(x_root, 1)
            act.activation(ss[:, 12:16], ss[:, 12:16], ACT.Sqrt).then_inc(x_root, 1)
            for t in range(NT):
                act.wait_ge(lat_ready, t + 1)
                act.activation(lat_sb[:, t, :], banks[4 + t][:, 0:LAT], ACT.Copy).then_inc(lat_copied, 1)
            act.wait_ge(lat_copied, NT)
            for t in range(NT):
                for j, (a, n) in enumerate(((0, QR), (C_KV, KVR), (C_KI, ID))):
                    act.activation(gaT[:, t, a:a + n], lat_sb[:, t, a:a + n], ACT.Square,
                                   accum_out=ss[:, 4 * j + t:4 * j + t + 1]).then_inc(lat_squared, 1)
            act.wait_ge(lat_root, 3)
            act.activation(ss[:, 0:12], ss[:, 0:12], ACT.Sqrt).then_inc(lat_root, 1)
            for h in range(IH):
                act.wait_ge(qidx_ready, h + 1)
                act.activation(qidxT[:, h, :], banks[4 + h][0:ID, :], ACT.Copy).then_inc(qidx_copied, 1)
            for n, b in enumerate(QBLOCKS):
                if n:
                    act.wait_ge(score_done, n)
                for h in range(IH):
                    act.wait_ge(logit_ready, 4 * n + h + 1)
                    act.activation(relu[:, h, 0:(b + 1) * P], banks[4 * (n % 2) + h][:, 0:(b + 1) * P], ACT.Relu,
                                   scale=ID ** -0.5).then_inc(relu_done, 1)
            for h in range(H):
                act.wait_ge(q_ready, h + 1)
                act.activation(qT[:, h, :], banks[4 + h % 4][:, :], ACT.Copy, scale=cols[:, QN:QN + 1]
                               ).then_inc(q_copied, 1)
                if h >= 2:
                    act.wait_ge(qss_ready, h - 1)
                act.activation(qsq[:, h % 2, :], banks[4 + h % 4][:, :], ACT.Square).then_inc(q_squared, 1)
            act.wait_ge(qss_ready, H)
            act.activation(ss[:, 16:48], banks[0][:, 0:NT * H], ACT.Copy).then_inc(qss_copied, 1)
            act.wait_ge(q_root, 1)
            act.activation(mx[:, :, :].rearrange("p t h -> p (t h)"), den[:, :, :].rearrange("p t h -> p (t h)"),
                           ACT.Sqrt).then_inc(q_root, 1)
            for t in range(NT):
                act.wait_ge(v_ready, t + 1)
                act.activation(v_sb[:, t, :], banks[4 + t][:, :], ACT.Gelu_apprx_tanh).then_inc(v_gelu, 1)
            for g in range(G):
                act.wait_ge(u_ready, g + 1)
                act.activation(uT[:, g, :], banks[g][:, :], ACT.Gelu_apprx_tanh).then_inc(u_gelu, 1)
            act.wait_ge(v_gelu, NT)
            act.wait_ge(q_scale_set, 1)
            act.wait_ge(lat_squared, 3 * NT)
            for t in range(NT):
                for g in range(G):
                    act.activation(gaT[:, t, g * P:(g + 1) * P], v_sb[:, t, g * P:(g + 1) * P], ACT.Square,
                                   accum_out=ss[:, 16 + 4 * t + g:17 + 4 * t + g]).then_inc(v_squared, 1)
            act.wait_ge(v_root, 1)
            act.activation(ss[:, 16:32], ss[:, 16:32], ACT.Sqrt).then_inc(v_root, 1)
            for i in range(16):
                act.wait_ge(gate_ready, i + 1)
                if i == 0:
                    act.wait_ge(v_squared, NT * G)
                if i == 12:
                    act.wait_ge(score_done, 3)
                dst = gaT[:, i, :] if i < 8 else gbT[:, i - 8, :]
                act.activation(dst, banks[(4 + i) % 8][:, :], ACT.Sigmoid).then_inc(gate_taken, 1)
            for i, (b, g) in enumerate(HALVES):
                n = (b + 1) * P
                for h in range(4):
                    hh = 4 * g + h
                    act.wait_ge(bias_set, i + 1)
                    act.activation(probs[i % 2][:, h, 0:n], probs[i % 2][:, h, 0:n], ACT.Exp,
                                   scale=qs[:, b, hh:hh + 1], bias=mx[:, b, hh:hh + 1],
                                   accum_out=den[:, b, hh:hh + 1]).then_inc(exp_done, 1)
                if i >= 1:
                    act_half(i - 1, act)
            act_half(len(HALVES) - 1, act)
            for j in range(4):
                act.wait_ge(yb_ready, j + 1)
                if j == 0:
                    act.wait_ge(pa_ready, KD)
                act.activation(ybT[:, j, :], banks[j][:, :], ACT.Copy).then_inc(yb_taken, 1)

        @block.vector
        def _(dve):
            step = Steps(dve, dve_step)

            def mean(dst, src, n, signal):
                dve.tensor_scalar(dst, src, 1.0 / n, EPS, ALU.mult, ALU.add).then_inc(signal, 1)

            dve.memset(wuv[:, :, :], 0.0).then_inc(wuv_zeroed, 1)
            dve.wait_ge(x_squared, NT)
            mean(ss[:, 12:16], ss[:, 12:16], D, x_root)
            dve.wait_ge(x_root, 2)
            step(dve.reciprocal(ss[:, 12:16], ss[:, 12:16]))
            for t in range(NT):
                dve.tensor_scalar(x_sb[:, t, :], x_sb[:, t, :], ss[:, 12 + t:13 + t], None, ALU.mult
                                  ).then_inc(x_scaled, 1)
            dve.wait_ge(colsT_ready, 1)
            dve.tensor_copy(cols[:, :], banks[7][:, 0:21]).then_inc(cols_set, 1)
            dve.wait_ge(cols_set, 1)
            for j in range(2 * NT):
                t, half = j // 2, j % 2
                dve.wait_ge(xT_ready, j + 1)
                dve.tensor_tensor(xnT[:, 4 * half:4 * half + 4, t * P:(t + 1) * P],
                                  banks[j % 4][:, :].rearrange("p (k q) -> p k q", k=4),
                                  cols[:, N1 + 4 * half:N1 + 4 * half + 4].unsqueeze(2).to_broadcast([P, 4, P]),
                                  ALU.mult).then_inc(xT_taken, 1)
            step(dve.tensor_scalar(cols[:, QN:QN + 1], cols[:, QN:QN + 1], KVR ** -0.5, None, ALU.mult))
            dve.wait_ge(lat_squared, 3 * NT)
            for j, n in enumerate((QR, KVR, ID)):
                mean(ss[:, 4 * j:4 * j + 4], ss[:, 4 * j:4 * j + 4], n, lat_root)
            dve.wait_ge(lat_root, 4)
            step(dve.reciprocal(ss[:, 0:12], ss[:, 0:12]))
            dve.wait_ge(first_loaded, 16 * 2)
            for t in range(NT):
                dve.tensor_scalar(lat_sb[:, t, 0:QR], lat_sb[:, t, 0:QR], ss[:, t:t + 1], None, ALU.mult
                                  ).then_inc(lat_scaled, 1)
            for t in range(NT):
                dve.scalar_tensor_tensor(kv[:, t, :], lat_sb[:, t, C_KV:C_KV + KVR], ss[:, 4 + t:5 + t], kvg[:, :],
                                         ALU.mult, ALU.mult).then_inc(lat_scaled, 1)
            for t in range(NT):
                dve.tensor_scalar(lat_sb[:, t, C_KI:C_KI + ID], lat_sb[:, t, C_KI:C_KI + ID], ss[:, 8 + t:9 + t],
                                  None, ALU.mult).then_inc(lat_scaled, 1)
            step(dve.tensor_scalar(widx[:, :, :], lat_sb[:, :, C_WI:LAT], IH ** -0.5, None, ALU.mult))
            for j in range(2):
                dve.wait_ge(latT_ready, j + 1)
                dve.tensor_scalar(cqT[:, j, :], banks[j][:, :], cols[:, QL + j:QL + j + 1], None, ALU.mult
                                  ).then_inc(latT_taken, 1)
            dve.wait_ge(latT_ready, 3)
            dve.tensor_scalar(kidxT[:, :], banks[2][0:ID, :], cols[0:ID, KI:KI + 1], None, ALU.mult
                              ).then_inc(latT_taken, 1)
            dve.wait_ge(latT_ready, 4)
            dve.tensor_copy(kvT[:, :], banks[3][:, :]).then_inc(latT_taken, 1)
            for n, b in enumerate(QBLOCKS):
                w = (b + 1) * P
                for h in range(IH):
                    dve.wait_ge(relu_done, 4 * n + h + 1)
                    acc = mask[:, b, 0:w]
                    if h == 0:
                        step(dve.tensor_scalar(acc, relu[:, h, 0:w], widx[:, b, h:h + 1], None, ALU.mult))
                    else:
                        ins = dve.scalar_tensor_tensor(acc, relu[:, h, 0:w], widx[:, b, h:h + 1], acc,
                                                       ALU.mult, ALU.add)
                        if h < IH - 1:
                            step(ins)
                        else:
                            ins.then_inc(score_done, 1)
            dve.wait_ge(wsT_ready, G)
            dve.tensor_copy(wsT[:, :, :].rearrange("p g t -> p (g t)"), banks[1][:, :]).then_inc(wsT_copied, 1)
            dve.wait_ge(qss_copied, 1)
            mean(den[:, :, :].rearrange("p t h -> p (t h)"), ss[:, 16:48], KVR, q_root)
            dve.wait_ge(q_root, 2)
            dve.reciprocal(qs[:, :, :].rearrange("p t h -> p (t h)"), mx[:, :, :].rearrange("p t h -> p (t h)")
                           ).then_inc(q_scale_set, 1)
            for n, b in enumerate(QBLOCKS):
                w = (b + 1) * P
                dve.wait_ge(masked, 4 + n)
                work = mask[:, b, 0:w]
                for _ in range(TOPK // 8):
                    step(dve.max(top8[:, :], work))
                    step(dve.match_replace(work, top8[:, :], work, TAKEN))
                dve.tensor_scalar(work, work, TAKEN_BELOW, NEG, ALU.is_gt, ALU.mult).then_inc(mask_set, 1)
            dve.wait_ge(v_squared, NT * G)
            mean(ss[:, 16:32], ss[:, 16:32], P, v_root)
            dve.wait_ge(v_root, 2)
            step(dve.reciprocal(ss[:, 16:32], ss[:, 16:32]))
            for t in range(NT):
                vt = v_sb[:, t, :].rearrange("p (g n) -> p g n", g=G)
                dve.tensor_tensor(vt, vt, ss[:, 16 + 4 * t:20 + 4 * t].unsqueeze(2).to_broadcast([P, G, P]),
                                  ALU.mult).then_inc(v_scaled, 1)
            dve.wait_ge(small_loaded, 16 * 11)
            dve.wait_ge(u_gelu, G)
            for g in range(G):
                dve.wait_ge(mix_ready, g + 1)
                mixed = banks[4 + g][:, :].rearrange("p (t n) -> p t n", t=NT)
                step(dve.scalar_tensor_tensor(mixed, mixed, cols[:, VG:VG + 1],
                                              bspat[:, g:g + 1, :].to_broadcast([P, NT, P]), ALU.mult, ALU.add))
                dve.tensor_tensor(uT[:, g, :], uT[:, g, :], banks[4 + g][:, :], ALU.mult).then_inc(ya_set, 1)
            for c in range(KD):
                dve.wait_ge(pa_ready, c + 1)
                dve.wait_ge(gate_taken, 16)
                dve.tensor_tensor(gaT[:, c, :], gaT[:, c, :], banks[c][:, :], ALU.mult).then_inc(pa_taken, 1)
            dve.wait_ge(mask_set, 3)
            dve.wait_ge(masked, 6)
            for i, (b, g) in enumerate(HALVES):
                n = (b + 1) * P
                if i >= 2:
                    dve.wait_ge(pT_ready, PT_BEFORE[i - 1])
                for h in range(4):
                    hh = 4 * g + h
                    dve.wait_ge(s_ready, 4 * i + h + 1)
                    dve.tensor_tensor_reduce(probs[i % 2][:, h, 0:n], banks[h][:, 0:n], mask[:, b, 0:n], 1.0, TAKEN,
                                             ALU.add, ALU.max, mx[:, b, hh:hh + 1]).then_inc(s_masked, 1)
                dve.wait_ge(s_masked, 4 * i + 4)
                dve.scalar_tensor_tensor(mx[:, b, 4 * g:4 * g + 4], mx[:, b, 4 * g:4 * g + 4], -1.0,
                                         qs[:, b, 4 * g:4 * g + 4], ALU.mult, ALU.mult).then_inc(bias_set, 1)
                if i >= 1:
                    inverse(dve, i - 1)
            inverse(dve, len(HALVES) - 1)
            for c in range(KD):
                dve.wait_ge(pb_ready, c + 1)
                step(dve.tensor_tensor(gbT[:, c, :], gbT[:, c, :], banks[4 + c % 4][:, :], ALU.mult))
                dve.tensor_tensor(gaT[:, c, :], gaT[:, c, :], gbT[:, c, :], ALU.add).then_inc(merged, 1)
            for j in range(2 * NT):
                t, n = j // 2, j % 2
                dve.wait_ge(x2_ready, j + 1)
                dve.wait_ge(x_again, 16 * NT)
                dve.tensor_tensor(x_sb[:, t, 512 * n:512 * n + 512], x_sb[:, t, 512 * n:512 * n + 512],
                                  banks[j % 4][:, :], ALU.add).then_inc(x2_taken, 1)
            dve.wait_ge(x2_taken, 2 * NT)

        @block.tensor
        def _(pe):
            def product(bank, pairs):
                for k, (lhsT, rhs) in enumerate(pairs):
                    last = pe.matmul(bank, lhsT, rhs, start=(k == 0), stop=(k == len(pairs) - 1))
                return last

            pe.wait_ge(consts_set, 3)
            pe.wait_ge(vecs_loaded, 16 * 6)
            pe.transpose(banks[7][:, 0:21], vecs[:, :], ident[0:21, 0:21]).then_inc(colsT_ready, 1)
            for j in range(2 * NT):
                t, half = j // 2, j % 2
                pe.wait_ge(x_scaled, t + 1)
                if j >= 4:
                    pe.wait_ge(xT_taken, j - 3)
                for k in range(4):
                    last = pe.transpose(banks[j % 4][:, k * P:(k + 1) * P],
                                        x_sb[:, t, (4 * half + k) * P:(4 * half + k + 1) * P], ident[:, :])
                last.then_inc(xT_ready, 1)
            pe.wait_ge(lat_w_loaded, 16)
            pe.wait_ge(cols_set, 1)
            for t in range(NT):
                pe.wait_ge(xT_taken, 2 * t + 2)
                product(banks[4 + t][:, 0:LAT], [(xnT[:, k, t * P:(t + 1) * P], w_lat[:, k, :]) for k in range(KD)]
                        ).then_inc(lat_ready, 1)
            pe.wait_ge(xT_taken, 2 * NT)
            for j in range(2):
                pe.wait_ge(lat_scaled, NT)
                for t in range(NT):
                    last = pe.transpose(banks[j][:, t * P:(t + 1) * P], lat_sb[:, t, j * P:(j + 1) * P], ident[:, :])
                last.then_inc(latT_ready, 1)
            pe.wait_ge(lat_scaled, 3 * NT)
            for t in range(NT):
                last = pe.transpose(banks[2][0:ID, t * P:(t + 1) * P], lat_sb[:, t, C_KI:C_KI + ID], ident[:, :])
            last.then_inc(latT_ready, 1)
            for t in range(NT):
                last = pe.transpose(banks[3][:, t * P:(t + 1) * P], kv[:, t, :], ident[:, :])
            last.then_inc(latT_ready, 1)
            pe.wait_ge(qw_loaded, 32)
            pe.wait_ge(latT_taken, 2)
            pe.wait_ge(lat_copied, NT)
            for h in range(IH):
                product(banks[4 + h][0:ID, :], [(wqi[:, k, h * ID:(h + 1) * ID], cqT[:, k, :]) for k in range(2)]
                        ).then_inc(qidx_ready, 1)
            pe.wait_ge(latT_taken, 4)
            for n, b in enumerate(QBLOCKS):
                for h in range(IH):
                    if n == 0:
                        pe.wait_ge(qidx_copied, h + 1)
                    elif n == 1:
                        pe.wait_ge(qidx_copied, IH)
                    else:
                        pe.wait_ge(relu_done, h + 1)
                    product(banks[4 * (n % 2) + h][:, 0:(b + 1) * P],
                            [(qidxT[:, h, b * P:(b + 1) * P], kidxT[:, 0:(b + 1) * P])]).then_inc(logit_ready, 1)
            def query_squares(h):
                pe.wait_ge(q_squared, h + 1)
                if h == 0:
                    pe.wait_ge(relu_done, 12)
                for t in range(NT):
                    last = pe.matmul(banks[0][:, t * H + h:t * H + h + 1], qsq[:, h % 2, t * P:(t + 1) * P],
                                     ones[:, 0:1], start=True, stop=True)
                last.then_inc(qss_ready, 1)

            for h in range(H):
                if h < 4:
                    pe.wait_ge(relu_done, 5 + h)
                else:
                    pe.wait_ge(q_squared, h - 3)
                product(banks[4 + h % 4][:, :], [(wuq[:, k, h * P:(h + 1) * P], cqT[:, k, :]) for k in range(2)]
                        ).then_inc(q_ready, 1)
                if h >= 1:
                    query_squares(h - 1)
            query_squares(H - 1)
            pe.wait_ge(masked, 1)
            for g in range(G):
                pe.transpose(banks[1][:, g * P:(g + 1) * P], wsp[:, g, :], ident[:, :]).then_inc(wsT_ready, 1)
            pe.wait_ge(v_w_loaded, 16)
            for t in range(NT):
                pe.wait_ge(q_squared, 5 + t)
                product(banks[4 + t][:, :], [(xnT[:, k, t * P:(t + 1) * P], w_v[:, k, :]) for k in range(KD)]
                        ).then_inc(v_ready, 1)
            pe.wait_ge(u_w_loaded, 16)
            pe.wait_ge(qss_copied, 1)
            pe.wait_ge(wsT_copied, 1)
            for g in range(G):
                product(banks[g][:, :], [(w_u[:, k, g * P:(g + 1) * P], xnT[:, k, :]) for k in range(KD)]
                        ).then_inc(u_ready, 1)
            for i in range(16):
                if i % 4 == 0:
                    pe.wait_ge(gate_w_loaded[i // 4], 16)
                if i < 4:
                    pe.wait_ge(v_gelu, i + 1)
                elif i < 8:
                    pe.wait_ge(u_gelu, i - 3)
                else:
                    pe.wait_ge(gate_taken, i - 7)
                c = i % 4
                product(banks[(4 + i) % 8][:, :],
                        [(w_gate[i // 4][:, k, c * P:(c + 1) * P], xnT[:, k, :]) for k in range(KD)]
                        ).then_inc(gate_ready, 1)
            for g in range(G):
                pe.wait_ge(gate_taken, 9 + g)
                pe.wait_ge(v_scaled, NT)
                for t in range(NT):
                    last = pe.matmul(banks[4 + g][:, t * P:(t + 1) * P], v_sb[:, t, g * P:(g + 1) * P], wsT[:, g, :],
                                     start=True, stop=True)
                last.then_inc(mix_ready, 1)
            pe.wait_ge(pa_loaded, 16)
            pe.wait_ge(gate_taken, 16)
            pe.wait_ge(ya_set, G)
            for c in range(KD):
                product(banks[c][:, :], [(wpa[:, k, c * P:(c + 1) * P], uT[:, k, :]) for k in range(G)]
                        ).then_inc(pa_ready, 1)

            def scores(i):
                b, g = HALVES[i]
                for h in range(4):
                    if i == 0:
                        pe.wait_ge(pa_taken, h + 1)
                    else:
                        pe.wait_ge(s_masked, 4 * (i - 1) + h + 1)
                    product(banks[h][:, 0:(b + 1) * P],
                            [(qT[:, 4 * g + h, b * P:(b + 1) * P], kvT[:, 0:(b + 1) * P])]).then_inc(s_ready, 1)

            def mix_values(i):
                b, g = HALVES[i]
                pe.wait_ge(p_scaled, 4 * i + 4)
                if i == 0:
                    pe.wait_ge(pa_taken, KD)
                for kt in range(b + 1):
                    j = PT_BEFORE[i] + kt
                    if j >= 2:
                        pe.wait_ge(pT_taken, j - 1)
                    for h in range(4):
                        last = pe.transpose(banks[4 + j % 2][:, h * P:(h + 1) * P],
                                            probs[i % 2][:, h, kt * P:(kt + 1) * P], ident[:, :])
                    last.then_inc(pT_ready, 1)
                if i >= 2:
                    pe.wait_ge(o_taken, i - 1)
                for kt in range(b + 1):
                    pe.wait_ge(pT_taken, PT_BEFORE[i] + kt + 1)
                    last = pe.matmul(banks[6 + g][:, :], kv[:, kt, :], pT[:, kt, :], start=(kt == 0), stop=(kt == b))
                last.then_inc(o_ready, 1)

            for i in range(len(HALVES)):
                scores(i)
                if i >= 1:
                    mix_values(i - 1)
            mix_values(len(HALVES) - 1)
            pe.wait_ge(small_loaded, 16 * 11)
            for j in range(4):
                pe.wait_ge(s_masked, NT * H)
                pe.wait_ge(o_taken, len(HALVES))
                product(banks[j][:, :], [(wuv[:, 2 * j + a, :], oT[:, 2 * j + a, :]) for a in range(2)]
                        ).then_inc(yb_ready, 1)
            pe.wait_ge(pb_loaded, 16)
            pe.wait_ge(yb_taken, 4)
            for c in range(KD):
                if c >= 4:
                    pe.wait_ge(merged, c - 3)
                product(banks[4 + c % 4][:, :], [(wpb[:, k, c * P:(c + 1) * P], ybT[:, k, :]) for k in range(G)]
                        ).then_inc(pb_ready, 1)
            pe.wait_ge(out_w_loaded, 32)
            pe.wait_ge(merged, KD)
            for j in range(2 * NT):
                t, n = j // 2, j % 2
                if j >= 4:
                    pe.wait_ge(x2_taken, j - 3)
                product(banks[j % 4][:, :], [(gaT[:, k, t * P:(t + 1) * P], wout[:, k, 512 * n:512 * n + 512])
                                             for k in range(KD)]).then_inc(x2_ready, 1)


def routing(nc, sem, banks, x_sb, ident, ones, cols, N2, wr_sb, br_sb, tab, rk, bias, eq, slot_iota,
            counts, over_flag, xn2_rows, b_exp1, b_exp2):
    with ExitStack() as ctx:
        def sb(name, shape, dt=F32):
            return ctx.enter_context(nc.sbuf_tensor(name, shape, dt))

        xs = sb("xs", [P, NT, D])
        xn2T = sb("xn2T", [P, KD, S])
        r_ss = sb("r_ss", [P, NT])
        logits = sb("logits", [P, NT, NE])
        top = sb("top", [P, NT, 8])
        top_at = sb("top_at", [P, NT, 8], U32)
        top_col = sb("top_col", [P, NT, 8])
        gate = sb("gate", [P, NT, TK])
        negmax = sb("negmax", [P, NT])
        gsum = sb("gsum", [P, NT])
        e_iota = sb("e_iota", [P, NE])
        hot = sb("hot", [P, NT, TK, NE])
        routed = sb("routed", [P, NT, NE])
        pair_row = sb("pair_row", [P, NT])
        token = sb("token", [P, NT])
        before = sb("before", [P, P])
        bfull = sb("bfull", [96, 2 * DE + D])
        brest = sb("brest", [96, 2 * DE + D])
        over_f = sb("over_f", [P, 1])

        bias_loaded, rows_stored = sem("bias_loaded"), sem("rows_stored")
        r_consts, r_squared, r_root, r_scaled = sem("r_consts"), sem("r_squared"), sem("r_root"), sem("r_scaled")
        r_T_ready, r_T_taken = sem("r_T_ready"), sem("r_T_taken")
        route_ready, route_taken, top_set, exp_set = sem("route_ready"), sem("route_taken"), sem("top_set"), sem("exp_set")
        routed_set, rank_ready, count_ready = sem("routed_set"), sem("rank_ready"), sem("count_ready")
        r_step = sem("r_step")
        block = ctx.enter_context(nc.Block())

        @block.sync
        def _(sp):
            for part in range(3):
                sp.dma_start(bfull[32 * part:32 * part + 32, 0:2 * DE], b_exp1).then_inc(bias_loaded, 16)
                sp.dma_start(bfull[32 * part:32 * part + 32, 2 * DE:2 * DE + D], b_exp2).then_inc(bias_loaded, 16)
            rows = xn2_rows.rearrange("(t p) d -> p t d", p=P)
            for t in range(NT):
                sp.wait_ge(r_scaled, t + 1)
                sp.dma_start(rows[:, t, :], xs[:, t, :]).then_inc(rows_stored, 16)
            sp.wait_ge(rows_stored, 16 * NT)

        @block.gpsimd
        def _(pool):
            pool.iota(e_iota[:, :], pattern=[[1, NE]], base=0, channel_multiplier=0,
                      allow_small_or_imprecise_dtypes=True).then_inc(r_consts, 1)
            pool.iota(slot_iota[:, :], pattern=[[1, P]], base=0, channel_multiplier=0,
                      allow_small_or_imprecise_dtypes=True).then_inc(r_consts, 1)
            pool.iota(token[:, :], pattern=[[P, NT]], base=-int(BIG), channel_multiplier=1,
                      allow_small_or_imprecise_dtypes=True).then_inc(r_consts, 1)
            pool.iota(pair_row[:, :], pattern=[[TK * P, NT]], base=-int(BIG), channel_multiplier=TK,
                      allow_small_or_imprecise_dtypes=True).then_inc(r_consts, 1)
            pool.memset(before[:, :], 1.0).then_inc(r_consts, 1)
            pool.memset(eq[:, :], 0.0).then_inc(r_consts, 1)
            pool.memset(tab[:, :, :, :], 0.0).then_inc(r_consts, 1)
            pool.memset(rk[:, :, :], -1.0).then_inc(r_consts, 1)
            pool.wait_ge(r_consts, 8)
            pool.affine_select(out=before[:, :], in_=before[:, :], compare_op=ALU.is_gt, fill=0.0, base=0,
                               pattern=[[1, P]], channel_multiplier=-1).then_inc(r_consts, 1)
            for part in range(3):
                pool.wait_ge(r_consts, 9 + part)
                pool.affine_select(out=eq[:, :], in_=eq[:, :], compare_op=ALU.not_equal, fill=1.0, base=-32 * part,
                                   pattern=[[-1, NEP]], channel_multiplier=1).then_inc(r_consts, 1)

        @block.scalar
        def _(act):
            for t in range(NT):
                act.activation(xs[:, t, :], x_sb[:, t, :], ACT.Square, accum_out=r_ss[:, t:t + 1]).then_inc(r_squared, 1)
            act.wait_ge(r_root, 1)
            act.activation(r_ss[:, :], r_ss[:, :], ACT.Sqrt).then_inc(r_root, 1)
            for t in range(NT):
                act.wait_ge(top_set, t + 1)
                act.activation(gate[:, t, :], top[:, t, 0:TK], ACT.Exp, bias=negmax[:, t:t + 1],
                               accum_out=gsum[:, t:t + 1]).then_inc(exp_set, 1)

        @block.vector
        def _(dve):
            step = Steps(dve, r_step)
            dve.wait_ge(r_squared, NT)
            dve.tensor_scalar(r_ss[:, :], r_ss[:, :], 1.0 / D, EPS, ALU.mult, ALU.add).then_inc(r_root, 1)
            dve.wait_ge(r_root, 2)
            step(dve.reciprocal(r_ss[:, :], r_ss[:, :]))
            for t in range(NT):
                dve.tensor_scalar(xs[:, t, :], x_sb[:, t, :], r_ss[:, t:t + 1], None, ALU.mult).then_inc(r_scaled, 1)
            for j in range(2 * NT):
                t, half = j // 2, j % 2
                dve.wait_ge(r_T_ready, j + 1)
                dve.tensor_tensor(xn2T[:, 4 * half:4 * half + 4, t * P:(t + 1) * P],
                                  banks[4 + j % 2][:, :].rearrange("p (k q) -> p k q", k=4),
                                  cols[:, N2 + 4 * half:N2 + 4 * half + 4].unsqueeze(2).to_broadcast([P, 4, P]),
                                  ALU.mult).then_inc(r_T_taken, 1)
            dve.wait_ge(r_consts, 12)
            for t in range(NT):
                dve.wait_ge(route_ready, t + 1)
                step(dve.tensor_tensor(logits[:, t, :], banks[t][:, 0:NE], br_sb[:, :], ALU.add))
                step(dve.max(top[:, t, :], logits[:, t, :]))
                dve.tensor_scalar(negmax[:, t:t + 1], top[:, t, 0:1], -1.0, None, ALU.mult).then_inc(top_set, 1)
                step(dve.max_index(top_at[:, t, :], top[:, t, :], logits[:, t, :]))
                step(dve.tensor_copy(top_col[:, t, :], top_at[:, t, :]))
                for k in range(TK):
                    ins = dve.tensor_scalar(hot[:, t, k, :], e_iota[:, :], top_col[:, t, k:k + 1], None, ALU.is_equal)
                step(ins)
                ins = dve.tensor_reduce(routed[:, t, :], hot[:, t, :, :].rearrange("p k e -> p e k"), AX.X, ALU.add)
                ins.then_inc(routed_set, 1)
            for t in range(NT):
                dve.wait_ge(exp_set, t + 1)
                step(dve.reciprocal(gsum[:, t:t + 1], gsum[:, t:t + 1]))
                step(dve.tensor_scalar(gate[:, t, :], gate[:, t, :], gsum[:, t:t + 1], None, ALU.mult))
                dve.wait_ge(routed_set, t + 1)
                dve.tensor_scalar(tab[:, t, 0, 0:NE], routed[:, t, :], token[:, t:t + 1], None, ALU.mult)
                step(dve.tensor_scalar(tab[:, t, 1, 0:NE], routed[:, t, :], pair_row[:, t:t + 1], None, ALU.mult))
                step(dve.tensor_scalar(tab[:, t, 2, 0:NE], hot[:, t, 0, :], gate[:, t, 0:1], None, ALU.mult))
                for k in range(1, TK):
                    dve.scalar_tensor_tensor(tab[:, t, 1, 0:NE], hot[:, t, k, :], float(k), tab[:, t, 1, 0:NE],
                                             ALU.mult, ALU.add)
                    step(dve.scalar_tensor_tensor(tab[:, t, 2, 0:NE], hot[:, t, k, :], gate[:, t, k:k + 1],
                                                  tab[:, t, 2, 0:NE], ALU.mult, ALU.add))
            for t in range(NT):
                dve.wait_ge(rank_ready, t + 1)
                step(dve.scalar_tensor_tensor(rk[:, t, 0:NE], banks[4 + t][:, 0:NE], 1.0, routed[:, t, :],
                                              ALU.add, ALU.mult))
                step(dve.tensor_scalar(rk[:, t, 0:NE], rk[:, t, 0:NE], -1.0, None, ALU.add))
            dve.wait_ge(count_ready, 1)
            step(dve.tensor_copy(counts[:, :], banks[0][:, 64:64 + NE]))
            step(dve.tensor_reduce(over_f[:, :], counts[:, :], AX.X, ALU.max))
            step(dve.tensor_scalar(over_flag[:, :], over_f[:, :], float(P), None, ALU.is_gt))
            dve.wait_ge(bias_loaded, 16 * 6)
            step(dve.tensor_copy(bias[:, :], bfull[:, :]))
            for part in (1, 2):
                rows = slice(32 * part, 96)
                for r in range(part, 3):
                    rows = slice(32 * r, 32 * r + 32)
                    step(dve.tensor_tensor(bfull[rows, :], bfull[rows, :], bias[rows, :], ALU.subtract))
                    step(dve.tensor_copy(bias[rows, :], bfull[rows, :]))

        @block.tensor
        def _(pe):
            for j in range(2 * NT):
                t, half = j // 2, j % 2
                pe.wait_ge(r_scaled, t + 1)
                if j >= 2:
                    pe.wait_ge(r_T_taken, j - 1)
                for k in range(4):
                    last = pe.transpose(banks[4 + j % 2][:, k * P:(k + 1) * P],
                                        xs[:, t, (4 * half + k) * P:(4 * half + k + 1) * P], ident[:, :])
                last.then_inc(r_T_ready, 1)
            for t in range(NT):
                pe.wait_ge(r_T_taken, 2 * t + 2)
                for k in range(KD):
                    last = pe.matmul(banks[t][:, 0:NE], xn2T[:, k, t * P:(t + 1) * P], wr_sb[:, k, :],
                                     start=(k == 0), stop=(k == KD - 1))
                last.then_inc(route_ready, 1)
            pe.wait_ge(r_consts, 12)
            pe.wait_ge(r_T_taken, 2 * NT)
            for t in range(NT):
                pe.wait_ge(routed_set, t + 1)
                for s in range(t + 1):
                    last = pe.matmul(banks[4 + t][:, 0:NE], before[:, :] if s == t else ones[:, :], routed[:, s, :],
                                     start=(s == 0), stop=(s == t))
                last.then_inc(rank_ready, 1)
            for t in range(NT):
                last = pe.matmul(banks[0][:, 64:64 + NE], ones[:, :], routed[:, t, :], start=(t == 0),
                                 stop=(t == NT - 1))
            last.then_inc(count_ready, 1)


def experts(nc, sem, banks, ring, ident, n2col, tab, rk, bias, eq, slot_iota, counts, over_flag,
            w_landed, unit_dst, xn2_rows, pair_rows, w_exp1, w_exp2):
    with ExitStack() as ctx:
        def sb(name, shape, dt=F32):
            return ctx.enter_context(nc.sbuf_tensor(name, shape, dt))

        pick = sb("pick", [P, NT, P])
        sel_h = sb("sel_h", [96, P], BF16)
        sel_y = sb("sel_y", [96, P], BF16)
        row_in = sb("row_in", [P, 1], U32)
        row_out = sb("row_out", [P, 1], U32)
        dest = sb("dest", [P, NEP])
        gates = sb("gates", [P, NEP])
        xg = sb("xg", [P, D])
        xgT = sb("xgT", [P, KD, P])
        hg = sb("hg", [P, DE])
        hu = sb("hu", [P, DE])
        sg = sb("sg", [P, DE])
        act_sb = sb("act_sb", [P, DE])
        actT = sb("actT", [P, KD, P])
        y = sb("y", [P, D])
        onesb = sb("onesb", [96, P], BF16)
        zero = sb("zero", [P, 1])
        carried = sb("carried", [P, 2])

        def w1_rows(e, k):
            return w_exp1[bass.ds(e, 1), k * P:(k + 1) * P, :].rearrange("a p n -> (a p) n")

        def w2_rows(e, q):
            return w_exp2[bass.ds(e, 1), 2 * q * P:2 * (q + 1) * P, :].rearrange("a (k p) n -> p (a k) n", p=P)

        def gather(pool):
            return pool.indirect_dma_start(out=xg[:, :], out_offset=None, in_=xn2_rows,
                                           in_offset=bass.IndirectOffsetOnAxis(ap=row_in[:, 0:1], axis=0),
                                           bounds_check=S - 1, oob_is_err=False)

        def carry_waits(pool, i, signal):
            pool.tensor_tensor(carried[:, i:i + 1], zero[:, :], zero[:, :], ALU.add).then_inc(signal, 1)

        def scatter(pool):
            return pool.indirect_dma_start(out=pair_rows,
                                           out_offset=bass.IndirectOffsetOnAxis(ap=row_out[:, 0:1], axis=0),
                                           in_=y[:, :], in_offset=None, bounds_check=S * TK - 1, oob_is_err=False)

        e_consts = sem("e_consts")
        gather_carried, scatter_carried = sem("gather_carried"), sem("scatter_carried")
        pick_set, slots_ready, slots_taken = sem("pick_set"), sem("slots_ready"), sem("slots_taken")
        gathered, scattered = sem("gathered"), sem("scattered")
        xT_ready, xT_taken = sem("xgT_ready"), sem("xgT_taken")
        selh_set, sely_set = sem("selh_set"), sem("sely_set")
        w1_used, w2_used = sem("w1_used"), sem("w2_used")
        h_ready, hg_set, hu_set, hgu_set = sem("h_ready"), sem("hg_set"), sem("hu_set"), sem("hgu_set")
        sig_done, act_set = sem("sig_done"), sem("act_set")
        aT_ready, aT_taken = sem("aT_ready"), sem("aT_taken")
        y_ready, y_set, row_out_set = sem("y_ready"), sem("y_set"), sem("row_out_set")

        block = ctx.enter_context(nc.Block())


        @block.sync
        def _(sp):
            with sp.Fori(1, NE) as e:
                for k in range(KD):
                    if k < KD - 1:
                        sp.wait_ge(w1_used, e * 7 + (k - 6))
                    else:
                        sp.wait_ge(h_ready, e)
                    sp.dma_start(unit_dst(k), w1_rows(e, k)).then_inc(w_landed[k], 16)
                for q in range(4):
                    if q < 3:
                        sp.wait_ge(w2_used, e * 3 + (q - 2))
                    else:
                        sp.wait_ge(y_ready, e)
                    sp.dma_start(unit_dst(8 + q), w2_rows(e, q)).then_inc(w_landed[8 + q], 16)

        @block.gpsimd
        def _(pool):
            pool.memset(xg[:, :], 0.0).then_inc(e_consts, 1)
            pool.memset(onesb[:, :], 1.0).then_inc(e_consts, 1)
            pool.memset(zero[:, :], 0.0).then_inc(e_consts, 1)
            pool.wait_ge(e_consts, 3)
            for e in range(3):
                pool.wait_ge(slots_taken, e + 1)
                if e:
                    pool.wait_ge(xT_ready, 2 * e)
                gather(pool).then_inc(gathered, 16)
            with pool.Fori(1, NE) as e:
                pool.wait_ge(slots_taken, e + 3)
                pool.wait_ge(xT_ready, e * 2 + 4)
                carry_waits(pool, 0, gather_carried)
                gather(pool).then_inc(gathered, 16)
                pool.wait_ge(row_out_set, e)
                pool.wait_ge(y_set, e * 2)
                carry_waits(pool, 1, scatter_carried)
                scatter(pool).then_inc(scattered, 16)
            pool.wait_ge(row_out_set, NE)
            pool.wait_ge(y_set, 2 * NE)
            scatter(pool).then_inc(scattered, 16)
            pool.wait_ge(gathered, 16 * NEP)
            pool.wait_ge(scattered, 16 * NE)

        @block.scalar
        def _(act):
            def sigmoid(e):
                act.wait_ge(hg_set, e * 2 + 2)
                act.activation(sg[:, :], hg[:, :], ACT.Sigmoid, scale=ALPHA).then_inc(sig_done, 1)

            def copy_activations(e):
                for half in range(2):
                    act.wait_ge(aT_ready, e * 2 + (half + 1))
                    act.activation(actT[:, 4 * half:4 * half + 4, :].rearrange("p k q -> p (k q)"),
                                   banks[6 + half][:, :], ACT.Copy).then_inc(aT_taken, 1)

            def gated_rows(e):
                for n in range(2):
                    act.activation(y[:, 512 * n:512 * n + 512], banks[4 + n][:, :], ACT.Copy,
                                   scale=gates[:, bass.ds(e, 1)]).then_inc(y_set, 1)

            sigmoid(0)
            copy_activations(0)
            with act.Fori(1, NE) as e:
                act.wait_ge(act_set, e)
                sigmoid(e)
                act.wait_ge(y_ready, e)
                act.wait_ge(slots_taken, e + 2)
                act.wait_ge(row_out_set, e)
                gated_rows(e - 1)
                copy_activations(e)
            act.wait_ge(y_ready, NE)
            act.wait_ge(scattered, 16 * (NE - 1))
            gated_rows(NE - 1)

        @block.vector
        def _(dve):
            def pick_tokens(e):
                for t in range(NT):
                    last = dve.tensor_scalar(pick[:, t, :], slot_iota[:, :], rk[:, t, bass.ds(e, 1)], None,
                                             ALU.is_equal)
                last.then_inc(pick_set, 1)

            def take_slots(e):
                dve.tensor_scalar(dest[:, bass.ds(e, 1)], banks[7][:, 1:2], BIG, None, ALU.add)
                dve.tensor_copy(gates[:, bass.ds(e, 1)], banks[7][:, 2:3])
                dve.tensor_scalar(row_in[:, :], banks[7][:, 0:1], BIG, None, ALU.add).then_inc(slots_taken, 1)

            def take_tokens(e):
                for half in range(2):
                    dve.wait_ge(xT_ready, e * 2 + (half + 1))
                    dve.tensor_tensor(xgT[:, 4 * half:4 * half + 4, :],
                                      banks[6 + half][:, :].rearrange("p (k q) -> p k q", k=4),
                                      n2col[:, 4 * half:4 * half + 4].unsqueeze(2).to_broadcast([P, 4, P]), ALU.mult
                                      ).then_inc(xT_taken, 1)

            def select(sel, e, signal):
                dve.tensor_scalar(sel[:, :], onesb[:, :], eq[:, bass.ds(e, 1)], None, ALU.mult).then_inc(signal, 1)

            def clip(e):
                dve.wait_ge(h_ready, e + 1)
                for n in range(2):
                    dve.tensor_scalar(hg[:, 512 * n:512 * n + 512], banks[n][:, :], LIMIT, None, ALU.min
                                      ).then_inc(hg_set, 1)
                for n in range(2):
                    dve.tensor_scalar(hu[:, 512 * n:512 * n + 512], banks[2 + n][:, :], LIMIT, -LIMIT, ALU.min, ALU.max
                                      ).then_inc(hu_set, 1)
                dve.wait_ge(hu_set, e * 2 + 2)
                dve.scalar_tensor_tensor(hu[:, :], hu[:, :], 1.0, hg[:, :], ALU.add, ALU.mult).then_inc(hgu_set, 1)

            def activate(e):
                dve.wait_ge(hgu_set, e + 1)
                dve.wait_ge(sig_done, e + 1)
                dve.tensor_tensor(act_sb[:, :], hu[:, :], sg[:, :], ALU.mult).then_inc(act_set, 1)

            dve.wait_ge(e_consts, 2)
            select(sel_h, 0, selh_set)
            select(sel_y, 0, sely_set)
            for e in range(2):
                if e:
                    dve.wait_ge(gathered, 16 * e)
                    dve.wait_ge(slots_ready, e)
                pick_tokens(e)
                dve.wait_ge(slots_ready, e + 1)
                take_slots(e)
            take_tokens(0)
            pick_tokens(2)
            clip(0)
            dve.wait_ge(gathered, 32)
            dve.wait_ge(slots_ready, 3)
            take_slots(2)
            activate(0)
            select(sel_h, 1, selh_set)
            take_tokens(1)
            dve.tensor_copy(row_out[:, :], dest[:, 0:1]).then_inc(row_out_set, 1)
            with dve.Fori(1, NE) as e:
                pick_tokens(e + 2)
                clip(e)
                dve.wait_ge(gathered, e * 16 + 32)
                dve.wait_ge(slots_ready, e + 3)
                take_slots(e + 2)
                dve.wait_ge(aT_ready, e * 2)
                activate(e)
                select(sel_h, e + 1, selh_set)
                take_tokens(e + 1)
                dve.wait_ge(y_ready, e)
                select(sel_y, e, sely_set)
                dve.wait_ge(gather_carried, e)
                dve.wait_ge(scatter_carried, e)
                dve.wait_ge(scattered, e * 16)
                dve.tensor_copy(row_out[:, :], dest[:, bass.ds(e, 1)]).then_inc(row_out_set, 1)

        @block.tensor
        def _(pe):
            def slots(e):
                pe.wait_ge(pick_set, e + 1)
                for t in range(NT):
                    last = pe.matmul(banks[7][:, 0:3], pick[:, t, :],
                                     tab[:, t, :, bass.ds(e, 1)].rearrange("p a b -> p (a b)"),
                                     start=(t == 0), stop=(t == NT - 1))
                last.then_inc(slots_ready, 1)

            def transpose_half(src, half, signal):
                for k in range(4):
                    last = pe.transpose(banks[6 + half][:, k * P:(k + 1) * P],
                                        src[:, (4 * half + k) * P:(4 * half + k + 1) * P], ident[:, :])
                last.then_inc(signal, 1)

            def products_h(e):
                pe.wait_ge(selh_set, e + 1)
                for n in range(4):
                    pe.matmul(banks[n][:, :], sel_h[:, :], bias[:, 512 * n:512 * n + 512], start=True, stop=False)
                pe.wait_ge(xT_taken, e * 2 + 2)
                for k in range(KD):
                    pe.wait_ge(w_landed[k], e * 16 + 16)
                    for n in range(4):
                        last = pe.matmul(banks[n][:, :], xgT[:, k, :], ring[:, k, 512 * n:512 * n + 512],
                                         start=False, stop=(k == KD - 1))
                    last.then_inc(w1_used if k < KD - 1 else h_ready, 1)

            def products_y(e, ks):
                for k in ks:
                    if k == 0:
                        pe.wait_ge(sely_set, e + 1)
                        for n in range(2):
                            pe.matmul(banks[4 + n][:, :], sel_y[:, :],
                                      bias[:, 2 * DE + 512 * n:2 * DE + 512 * n + 512], start=True, stop=False)
                        pe.wait_ge(aT_taken, e * 2 + 2)
                    if k % 2 == 0:
                        pe.wait_ge(w_landed[8 + k // 2], e * 16 + 16)
                    for n in range(2):
                        last = pe.matmul(banks[4 + n][:, :], actT[:, k, :],
                                         ring[:, 8 + k // 2, 1024 * (k % 2) + 512 * n:1024 * (k % 2) + 512 * n + 512],
                                         start=False, stop=(k == KD - 1))
                    if k == KD - 1:
                        last.then_inc(y_ready, 1)
                    elif k % 2 == 1:
                        last.then_inc(w2_used, 1)

            slots(0)
            pe.wait_ge(slots_taken, 1)
            slots(1)
            pe.wait_ge(gathered, 16)
            transpose_half(xg, 0, xT_ready)
            pe.wait_ge(slots_taken, 2)
            transpose_half(xg, 1, xT_ready)
            products_h(0)
            slots(2)
            pe.wait_ge(gathered, 32)
            transpose_half(xg, 0, xT_ready)
            pe.wait_ge(slots_taken, 3)
            transpose_half(xg, 1, xT_ready)
            pe.wait_ge(act_set, 1)
            pe.wait_ge(xT_taken, 4)
            for half in range(2):
                transpose_half(act_sb, half, aT_ready)
            with pe.Fori(1, NE) as e:
                pe.wait_ge(hu_set, e * 2)
                products_h(e)
                pe.wait_ge(aT_taken, e * 2)
                slots(e + 2)
                pe.wait_ge(gathered, e * 16 + 32)
                transpose_half(xg, 0, xT_ready)
                pe.wait_ge(row_out_set, e)
                products_y(e - 1, range(0, 4))
                pe.wait_ge(slots_taken, e + 3)
                transpose_half(xg, 1, xT_ready)
                products_y(e - 1, range(4, KD))
                pe.wait_ge(act_set, e + 1)
                pe.wait_ge(xT_taken, e * 2 + 4)
                for half in range(2):
                    transpose_half(act_sb, half, aT_ready)
            pe.wait_ge(y_set, 2 * NE - 2)
            products_y(NE - 1, range(KD))


def further_blocks(nc, sem, banks, ring, ident, n2col, tab, rk, bias, eq, slot_iota, counts, over_flag,
                   unit_dst, xn2_rows, pair_rows, w_exp1, w_exp2):
    with ExitStack() as ctx:
        def sb(name, shape, dt=F32):
            return ctx.enter_context(nc.sbuf_tensor(name, shape, dt))

        pick = sb("f_pick", [P, NT, P])
        rank_here = sb("f_rank", [P, NT])
        sel = sb("f_sel", [96, P], BF16)
        row_in = sb("f_row_in", [P, 1], U32)
        row_out = sb("f_row_out", [P, 1], U32)
        gate = sb("f_gate", [P, 1])
        xg = sb("f_xg", [P, D])
        xgT = sb("f_xgT", [P, KD, P])
        hg = sb("f_hg", [P, DE])
        hu = sb("f_hu", [P, DE])
        sg = sb("f_sg", [P, DE])
        act_sb = sb("f_act", [P, DE])
        actT = sb("f_actT", [P, KD, P])
        y = sb("f_y", [P, D])
        onesb = sb("f_onesb", [96, P], BF16)
        more = sb("f_more", [P, 3, NE])
        extra = sb("f_extra", [P, NE])
        upto = sb("f_upto", [P, NE])
        upto2 = sb("f_upto2", [P, NE])
        done = sb("f_done", [P, OVER, NE])
        whose = sb("f_whose", [P, OVER])
        behind = sb("f_behind", [P, OVER])
        first = sb("f_first", [P, OVER])
        number = sb("f_number", [P, OVER])
        whose_i = sb("f_whose_i", [P, OVER], I32)

        f_consts, f_table = sem("f_consts"), sem("f_table")
        f_landed, f_step = sem("f_landed"), sem("f_step")
        f_picked, f_slots, f_rows, f_gathered = sem("f_picked"), sem("f_slots"), sem("f_rows"), sem("f_gathered")
        f_T, f_T_taken = sem("f_T"), sem("f_T_taken")
        f_h, f_hg, f_sig = sem("f_h"), sem("f_hg_set"), sem("f_sig")
        f_act_set, f_y_ready = sem("f_act_set"), sem("f_y_ready")
        f_y_set, f_scattered = sem("f_y_set"), sem("f_scattered")
        f_carried = sem("f_carried")
        zero = sb("f_zero", [P, 1])
        carried = sb("f_carry", [P, 2])
        block = ctx.enter_context(nc.Block())

        def expert_of(engine, j):
            return engine.value_load(whose_i[0:1, bass.ds(j, 1)], min_val=0, max_val=NE - 1)

        @block.sync
        def _(sp):
            sp.wait_ge(f_table, 1)
            with sp.Fori(0, OVER) as j:
                e = expert_of(sp, j)
                sp.wait_ge(f_picked, j + 1)
                for k in range(KD):
                    sp.dma_start(unit_dst(k), w_exp1[bass.ds(e, 1), k * P:(k + 1) * P, :]
                                 .rearrange("a p n -> (a p) n")).then_inc(f_landed, 16)
                for q in range(4):
                    sp.dma_start(unit_dst(8 + q), w_exp2[bass.ds(e, 1), 2 * q * P:2 * (q + 1) * P, :]
                                 .rearrange("a (k p) n -> p (a k) n", p=P)).then_inc(f_landed, 16)

        @block.gpsimd
        def _(pool):
            pool.memset(xg[:, :], 0.0).then_inc(f_consts, 1)
            pool.memset(onesb[:, :], 1.0).then_inc(f_consts, 1)
            pool.memset(zero[:, :], 0.0).then_inc(f_consts, 1)
            pool.iota(number[:, :], pattern=[[1, OVER]], base=0, channel_multiplier=0,
                      allow_small_or_imprecise_dtypes=True).then_inc(f_consts, 1)
            pool.wait_ge(f_consts, 4)
            with pool.Fori(0, OVER) as j:
                pool.wait_ge(f_rows, j + 1)
                pool.tensor_tensor(carried[:, 0:1], zero[:, :], zero[:, :], ALU.add).then_inc(f_carried, 1)
                pool.indirect_dma_start(out=xg[:, :], out_offset=None, in_=xn2_rows,
                                        in_offset=bass.IndirectOffsetOnAxis(ap=row_in[:, 0:1], axis=0),
                                        bounds_check=S - 1, oob_is_err=False).then_inc(f_gathered, 16)
                pool.wait_ge(f_y_set, j * 2 + 2)
                pool.tensor_tensor(carried[:, 1:2], zero[:, :], zero[:, :], ALU.add).then_inc(f_carried, 1)
                pool.indirect_dma_start(out=pair_rows,
                                        out_offset=bass.IndirectOffsetOnAxis(ap=row_out[:, 0:1], axis=0),
                                        in_=y[:, :], in_offset=None, bounds_check=S * TK - 1, oob_is_err=False
                                        ).then_inc(f_scattered, 16)
            pool.wait_ge(f_gathered, 16 * OVER)
            pool.wait_ge(f_scattered, 16 * OVER)

        @block.scalar
        def _(act):
            with act.Fori(0, OVER) as j:
                act.wait_ge(f_hg, j * 2 + 2)
                act.activation(sg[:, :], hg[:, :], ACT.Sigmoid, scale=ALPHA).then_inc(f_sig, 1)
                for half in range(2):
                    act.wait_ge(f_T, j * 4 + (half + 3))
                    act.activation(actT[:, 4 * half:4 * half + 4, :].rearrange("p k q -> p (k q)"),
                                   banks[6 + half][:, :], ACT.Copy).then_inc(f_T_taken, 1)
                act.wait_ge(f_y_ready, j + 1)
                for n in range(2):
                    act.activation(y[:, 512 * n:512 * n + 512], banks[4 + n][:, :], ACT.Copy, scale=gate[:, 0:1]
                                   ).then_inc(f_y_set, 1)

        @block.vector
        def _(dve):
            step = Steps(dve, f_step)
            for c in range(3):
                step(dve.tensor_scalar(more[:, c, :], counts[:, :], float(P * (c + 1)), None, ALU.is_gt))
            step(dve.tensor_reduce(extra[:, :], more[:, :, :].rearrange("p c e -> p e c"), AX.X, ALU.add))
            step(dve.tensor_copy(upto[:, :], extra[:, :]))
            here, there = upto, upto2
            for shift in (1, 2, 4, 8, 16):
                step(dve.tensor_copy(there[:, 0:shift], here[:, 0:shift]))
                step(dve.tensor_tensor(there[:, shift:NE], here[:, shift:NE], here[:, 0:NE - shift], ALU.add))
                here, there = there, here
            dve.wait_ge(f_consts, 4)
            for j in range(OVER):
                step(dve.tensor_scalar(done[:, j, :], here[:, :], float(j), None, ALU.is_le))
            step(dve.tensor_reduce(whose[:, :], done[:, :, :], AX.X, ALU.add))
            for j in range(OVER):
                step(dve.tensor_tensor(done[:, j, :], done[:, j, :], extra[:, :], ALU.mult))
            step(dve.tensor_reduce(behind[:, :], done[:, :, :], AX.X, ALU.add))
            step(dve.tensor_tensor(first[:, :], number[:, :], behind[:, :], ALU.subtract))
            step(dve.tensor_scalar(first[:, :], first[:, :], 1.0, float(P), ALU.add, ALU.mult))
            step(dve.tensor_scalar(behind[:, :], whose[:, :], float(NE), BIG, ALU.is_ge, ALU.mult))
            step(dve.tensor_tensor(first[:, :], first[:, :], behind[:, :], ALU.add))
            step(dve.tensor_scalar(whose[:, :], whose[:, :], float(NE - 1), None, ALU.min))
            dve.tensor_copy(whose_i[:, :], whose[:, :]).then_inc(f_table, 1)
            dve.wait_ge(f_table, 1)
            with dve.Fori(0, OVER) as j:
                step.enter(j, 5)
                e = expert_of(dve, j)
                step(dve.tensor_scalar(rank_here[:, :], rk[:, :, bass.ds(e, 1)].rearrange("p t a -> p (t a)"),
                                       first[:, bass.ds(j, 1)], None, ALU.subtract))
                for t in range(NT):
                    last = dve.tensor_scalar(pick[:, t, :], slot_iota[:, :], rank_here[:, t:t + 1], None,
                                             ALU.is_equal)
                step(last)
                dve.tensor_scalar(sel[:, :], onesb[:, :], eq[:, bass.ds(e, 1)], None, ALU.mult).then_inc(f_picked, 1)
                dve.wait_ge(f_slots, j + 1)
                dve.tensor_copy(gate[:, :], banks[7][:, 2:3])
                dve.tensor_scalar(row_out[:, :], banks[7][:, 1:2], BIG, None, ALU.add)
                dve.tensor_scalar(row_in[:, :], banks[7][:, 0:1], BIG, None, ALU.add).then_inc(f_rows, 1)
                for half in range(2):
                    dve.wait_ge(f_T, j * 4 + (half + 1))
                    dve.tensor_tensor(xgT[:, 4 * half:4 * half + 4, :],
                                      banks[6 + half][:, :].rearrange("p (k q) -> p k q", k=4),
                                      n2col[:, 4 * half:4 * half + 4].unsqueeze(2).to_broadcast([P, 4, P]), ALU.mult
                                      ).then_inc(f_T_taken, 1)
                dve.wait_ge(f_h, j + 1)
                for n in range(2):
                    dve.tensor_scalar(hg[:, 512 * n:512 * n + 512], banks[n][:, :], LIMIT, None, ALU.min
                                      ).then_inc(f_hg, 1)
                for n in range(2):
                    step(dve.tensor_scalar(hu[:, 512 * n:512 * n + 512], banks[2 + n][:, :], LIMIT, -LIMIT, ALU.min,
                                           ALU.max))
                step(dve.scalar_tensor_tensor(hu[:, :], hu[:, :], 1.0, hg[:, :], ALU.add, ALU.mult))
                dve.wait_ge(f_sig, j + 1)
                dve.tensor_tensor(act_sb[:, :], hu[:, :], sg[:, :], ALU.mult).then_inc(f_act_set, 1)
                dve.wait_ge(f_scattered, j * 16 + 16)
                dve.wait_ge(f_carried, j * 2 + 2)
                step.leave(OVER)

        @block.tensor
        def _(pe):
            pe.wait_ge(f_table, 1)
            with pe.Fori(0, OVER) as j:
                e = expert_of(pe, j)
                pe.wait_ge(f_picked, j + 1)
                for t in range(NT):
                    last = pe.matmul(banks[7][:, 0:3], pick[:, t, :],
                                     tab[:, t, :, bass.ds(e, 1)].rearrange("p a b -> p (a b)"),
                                     start=(t == 0), stop=(t == NT - 1))
                last.then_inc(f_slots, 1)
                pe.wait_ge(f_rows, j + 1)
                pe.wait_ge(f_gathered, j * 16 + 16)
                for half in range(2):
                    for k in range(4):
                        last = pe.transpose(banks[6 + half][:, k * P:(k + 1) * P],
                                            xg[:, (4 * half + k) * P:(4 * half + k + 1) * P], ident[:, :])
                    last.then_inc(f_T, 1)
                pe.wait_ge(f_T_taken, j * 4 + 2)
                pe.wait_ge(f_landed, j * (16 * UNITS) + 16 * UNITS)
                for n in range(4):
                    pe.matmul(banks[n][:, :], sel[:, :], bias[:, 512 * n:512 * n + 512], start=True, stop=False)
                    for k in range(KD):
                        last = pe.matmul(banks[n][:, :], xgT[:, k, :], ring[:, k, 512 * n:512 * n + 512],
                                         start=False, stop=(k == KD - 1))
                last.then_inc(f_h, 1)
                pe.wait_ge(f_act_set, j + 1)
                for half in range(2):
                    for k in range(4):
                        last = pe.transpose(banks[6 + half][:, k * P:(k + 1) * P],
                                            act_sb[:, (4 * half + k) * P:(4 * half + k + 1) * P], ident[:, :])
                    last.then_inc(f_T, 1)
                pe.wait_ge(f_T_taken, j * 4 + 4)
                for n in range(2):
                    pe.matmul(banks[4 + n][:, :], sel[:, :], bias[:, 2 * DE + 512 * n:2 * DE + 512 * n + 512],
                              start=True, stop=False)
                    for k in range(KD):
                        last = pe.matmul(banks[4 + n][:, :], actT[:, k, :],
                                         ring[:, 8 + k // 2, 1024 * (k % 2) + 512 * n:1024 * (k % 2) + 512 * n + 512],
                                         start=False, stop=(k == KD - 1))
                last.then_inc(f_y_ready, 1)


def combine(nc, sem, ring, x_sb, pair_rows, out_rows):
    pairs_loaded = [sem(f"pairs_loaded{t}") for t in range(NT)]
    summed, x_summed, out_stored = sem("summed"), sem("x_summed"), sem("out_stored")
    src = pair_rows.rearrange("(t p k) d -> t p (k d)", p=P, k=TK)
    part = [ring[:, 2 * t:2 * t + 2, :].rearrange("p a n -> p (a n)") for t in range(NT)]
    with nc.Block() as block:
        @block.sync
        def _(sp):
            for t in range(NT):
                sp.dma_start(part[t], src[t]).then_inc(pairs_loaded[t], 16)
            for t in range(NT):
                sp.wait_ge(x_summed, t + 1)
                sp.dma_start(out_rows[:, t, :], x_sb[:, t, :]).then_inc(out_stored, 16)
            sp.wait_ge(out_stored, 16 * NT)

        @block.vector
        def _(dve):
            for t in range(NT):
                dve.wait_ge(pairs_loaded[t], 16)
                p = part[t]
                dve.tensor_tensor(p[:, 0:2 * D], p[:, 0:2 * D], p[:, 2 * D:4 * D], ALU.add).then_inc(summed, 1)
                dve.wait_ge(summed, 2 * t + 1)
                dve.tensor_tensor(p[:, 0:D], p[:, 0:D], p[:, D:2 * D], ALU.add).then_inc(summed, 1)
                dve.wait_ge(summed, 2 * t + 2)
                dve.tensor_tensor(x_sb[:, t, :], x_sb[:, t, :], p[:, 0:D], ALU.add).then_inc(x_summed, 1)


_INS = ['x', 'norm1_g', 'w_in', 'q_lat_g', 'w_uq', 'q_norm_g', 'kv_norm_g', 'w_uv', 'w_q_idx', 'k_idx_g',
        'gmlp_v_g', 'w_spatial', 'b_spatial', 'w_proj_a', 'w_proj_b', 'w_out', 'norm2_g',
        'w_router', 'b_router', 'w_exp1', 'b_exp1', 'w_exp2', 'b_exp2']


def kernel(**inputs):
    import numpy as np
    import concourse.bacc as bacc
    from concourse.bass_utils import run_bass_kernel_spmd

    nc = bacc.Bacc("TRN2", target_bir_lowering=False, num_devices=1)
    arrays, args = {}, []
    for name in _INS:
        a = np.ascontiguousarray(inputs[name])
        arrays[f"in_{name}"] = a
        args.append(nc.dram_tensor(f"in_{name}", a.shape, mybir.dt.from_np(a.dtype), kind="ExternalInput").ap())
    shape = inputs["x"].shape
    args.append(nc.dram_tensor("out_y", shape, F32, kind="ExternalOutput").ap())
    build(nc, *args)
    got = run_bass_kernel_spmd(nc, [arrays], core_ids=[0])
    return got.results[0]["out_y"]
```

```python
from contextlib import ExitStack

import concourse.bass as bass
from concourse import mybir

P = 128
D = 1024
S = 512
NT = S // P
KD = D // P
G = 4
H = 8
QR = 256
KVR = 128
HV = 64
IH = 4
ID = 64
TOPK = 128
NE = 32
TK = 4
DE = 1024
LIMIT = 7.0
ALPHA = 1.702
EPS = 1e-6
OFF_U, OFF_V, OFF_LAT = 0, 512, 1024
LAT = QR + KVR + ID + IH
C_KV, C_KI, C_WI = QR, QR + KVR, QR + KVR + ID
OFF_GATE = OFF_LAT + LAT
NEG = -1.0e30
TAKEN = -3.0e38
TAKEN_BELOW = -2.0e38
BIG = 4096.0
UW = 2048
PER_E = 12
RAW = 6
SPLIT = 4
AHEAD = SPLIT - 1
NEP = NE + 2
OVER = 15

F32 = mybir.dt.float32
F32R = mybir.dt.float32r
BF16 = mybir.dt.bfloat16
I32 = mybir.dt.int32
U32 = mybir.dt.uint32
ALU = mybir.AluOpType
ACT = mybir.ActivationFunctionType
AX = mybir.AxisListType


class Steps:

    def __init__(self, engine, semaphore):
        self.engine, self.semaphore, self.n = engine, semaphore, 0
        self.past = None

    def __call__(self, instruction):
        self.n += 1
        instruction.then_inc(self.semaphore, 1)
        self.engine.wait_ge(self.semaphore, self.n if self.past is None else self.past + self.n)

    def enter(self, turns, per_turn):
        self.first, self.per_turn, self.past = self.n, per_turn, turns * per_turn

    def leave(self, count):
        assert self.n - self.first == self.per_turn, (self.n - self.first, self.per_turn)
        self.n = self.first + count * self.per_turn
        self.past = None


def build(nc, x, norm1_g, w_in, q_lat_g, w_uq, q_norm_g, kv_norm_g, w_uv, w_q_idx, k_idx_g,
          gmlp_v_g, w_spatial, b_spatial, w_proj_a, w_proj_b, w_out, norm2_g,
          w_router, b_router, w_exp1, b_exp1, w_exp2, b_exp2, out):
    xn2_rows = nc.dram_tensor("xn2_rows", (S, D), F32, kind="Internal").ap()
    pair_rows = nc.dram_tensor("pair_rows", (S * TK, D), F32, kind="Internal").ap()
    x_rows = x.rearrange("a (t p) d -> p (a t) d", p=P)
    out_rows = out.rearrange("a (t p) d -> p (a t) d", p=P)

    with ExitStack() as whole:
        def keep(name, shape, dt=F32):
            return whole.enter_context(nc.sbuf_tensor(name, shape, dt))

        def sem(name):
            return whole.enter_context(nc.semaphore(name))

        banks = [whole.enter_context(nc.psum_tensor(f"bank{i}", [P, 512], F32)) for i in range(8)]
        ring = keep("ring", [P, RAW, UW])
        x_sb = keep("x_sb", [P, NT, D])
        ident = keep("ident", [P, P])
        ones = keep("ones", [P, P])
        cols = keep("cols", [P, 21])
        wr_sb = keep("wr_sb", [P, KD, NE])
        br_sb = keep("br_sb", [P, NE])
        over_flag = keep("over_flag", [P, 1], I32)
        landed = [sem(f"landed{j}") for j in range(RAW)]
        N1, N2, QL, QN, VG, KI = 0, 8, 16, 18, 19, 20

        mixers(nc, sem, banks, ring, x_sb, ident, ones, cols, wr_sb, br_sb, landed, (N1, N2, QL, QN, VG, KI),
               w_exp1, x_rows, norm1_g, w_in, q_lat_g, w_uq, q_norm_g, kv_norm_g, w_uv,
               w_q_idx, k_idx_g, gmlp_v_g, w_spatial, b_spatial, w_proj_a, w_proj_b, w_out, norm2_g,
               w_router, b_router)

        tab = keep("tab", [P, NT, 3, NEP])
        rk = keep("rk", [P, NT, NEP])
        bias = keep("bias", [96, 2 * DE + D], BF16)
        eq = keep("eq", [96, NEP])
        slot_iota = keep("slot_iota", [P, P])
        counts = keep("counts", [P, NE])
        routing(nc, sem, banks, x_sb, ident, ones, norm2_g, wr_sb, br_sb, tab, rk, bias, eq, slot_iota,
                counts, over_flag, xn2_rows, b_exp1, b_exp2)
        experts(nc, sem, banks, ring, ident, tab, rk, bias, eq, slot_iota, landed, xn2_rows, pair_rows,
                w_exp1, w_exp2)
        beyond = nc.values_load(over_flag[0:1, 0:1], min_val=0, max_val=1)
        with nc.If(beyond > 0):
            further_blocks(nc, sem, banks, ring, ident, tab, rk, bias, eq, slot_iota, counts,
                           xn2_rows, pair_rows, w_exp1, w_exp2)
        combine(nc, sem, x_sb, pair_rows, out_rows)


def mixers(nc, sem, banks, ring, x_sb, ident, ones, cols, wr_sb, br_sb, landed, col_of,
           w_exp1, x_rows, norm1_g, w_in, q_lat_g, w_uq, q_norm_g, kv_norm_g, w_uv,
           w_q_idx, k_idx_g, gmlp_v_g, w_spatial, b_spatial, w_proj_a, w_proj_b, w_out, norm2_g,
           w_router, b_router):
    N1, N2, QL, QN, VG, KI = col_of
    with ExitStack() as ctx:
        def sb(name, shape, dt=F32):
            return ctx.enter_context(nc.sbuf_tensor(name, shape, dt))

        more = sb("more_units", [P, 6, UW])
        xnT = sb("xnT", [P, KD, S])
        gaT = sb("gaT", [P, KD, S])
        gbT = sb("gbT", [P, KD, S])
        uT = sb("uT", [P, G, S])
        v_sb = sb("v_sb", [P, NT, S])
        lat = sb("lat", [P, 2048])
        cqT = sb("cqT", [P, 2, S])
        kvT = sb("kvT", [P, S])
        kidxT = sb("kidxT", [ID, S])
        kv = sb("kv", [P, NT, KVR])
        wuv = sb("wuv", [P, H, P])
        bspat = sb("bspat", [P, G, P])
        wsT = sb("wsT", [P, G, P])
        kvg = sb("kvg", [P, KVR])
        vecs = sb("vecs", [21, P])
        ss = sb("ss", [P, 48])
        widx = sb("widx", [P, NT, IH])
        top8 = sb("top8", [P, 8])
        mx = sb("mx", [P, NT, H])
        den = sb("den", [P, NT, H])
        qs = sb("qs", [P, NT, H])

        lat_sb = lat[:, 0:NT * LAT].rearrange("p (t n) -> p t n", t=NT)
        qidxT = gbT[0:ID, 0:4, :]
        relu = gbT[:, 4:8, :]
        pT = x_sb[:, 0:2, :].rearrange("p a (b n) -> p (a b) n", b=2)
        mask = x_sb[:, 2:4, :].rearrange("p a (b n) -> p (a b) n", b=2)
        probs = [v_sb[:, :, :], lat[:, :].rearrange("p (h n) -> p h n", h=4)]
        oT = xnT
        ybT = uT
        def units(u, n):
            return ring[:, u:u + n, :] if u < RAW else more[:, u - RAW:u - RAW + n, :]

        def chunk(u, n):
            return units(u, 2).rearrange("p a b -> p (a b)")[:, 0:n]

        qT = units(10, 2).rearrange("p a (b n) -> p (a b) n", b=4)
        wuq = units(6, 1)[:, 0, :].rearrange("p (k n) -> p k n", k=2)
        wqi = units(7, 1)[:, 0, 0:512].rearrange("p (k n) -> p k n", k=2)
        wsp = units(7, 1)[:, 0, 512:1024].rearrange("p (g n) -> p g n", g=G)
        qsq = units(7, 1)[:, 0, 1024:2048].rearrange("p (a n) -> p a n", a=2)
        w_lat = chunk(0, KD * LAT).rearrange("p (k n) -> p k n", k=KD)
        w_v = chunk(2, KD * 512).rearrange("p (k n) -> p k n", k=KD)
        w_u = chunk(4, KD * 512).rearrange("p (k n) -> p k n", k=KD)
        gate_unit = [8, 0, 2, 4]
        w_gate = [chunk(u, KD * 512).rearrange("p (k n) -> p k n", k=KD) for u in gate_unit]
        wpa = chunk(6, G * D).rearrange("p (k n) -> p k n", k=G)
        wpb = chunk(8, G * D).rearrange("p (k n) -> p k n", k=G)
        wout = units(0, 4).rearrange("p a (b n) -> p (a b) n", b=2)

        def in_cols(c, n):
            return w_in[:, c:c + n].rearrange("(k p) n -> p k n", p=P)

        x_loaded = sem("x_loaded")
        vecs_loaded = sem("vecs_loaded")
        lat_w_loaded = sem("lat_w_loaded")
        qw_loaded = sem("qw_loaded")
        first_loaded = sem("first_loaded")
        small_loaded = sem("small_loaded")
        v_w_loaded = sem("v_w_loaded")
        u_w_loaded = sem("u_w_loaded")
        gate_w_loaded = [sem(f"gate_w_loaded{i}") for i in range(4)]
        pa_loaded = sem("pa_loaded")
        pb_loaded = sem("pb_loaded")
        out_w_loaded = sem("out_w_loaded")
        x_again = sem("x_again")
        consts_set = sem("consts_set")
        vecs_zeroed = sem("vecs_zeroed")
        wuv_zeroed = sem("wuv_zeroed")
        masked = sem("masked")
        colsT_ready, cols_set = sem("colsT_ready"), sem("cols_set")
        x_squared, x_root, x_scaled = sem("x_squared"), sem("x_root"), sem("x_scaled")
        xT_ready, xT_taken = sem("xT_ready"), sem("xT_taken")
        lat_ready, lat_copied = sem("lat_ready"), sem("lat_copied")
        lat_squared, lat_root, lat_scaled = sem("lat_squared"), sem("lat_root"), sem("lat_scaled")
        latT_ready, latT_taken = sem("latT_ready"), sem("latT_taken")
        qidx_ready, qidx_copied = sem("qidx_ready"), sem("qidx_copied")
        logit_ready, relu_done, score_done = sem("logit_ready"), sem("relu_done"), sem("score_done")
        q_ready, q_copied, q_squared = sem("q_ready"), sem("q_copied"), sem("q_squared")
        qss_ready, qss_copied, q_root, q_scale_set = (sem("qss_ready"), sem("qss_copied"), sem("q_root"),
                                                      sem("q_scale_set"))
        wsT_ready, wsT_copied = sem("wsT_ready"), sem("wsT_copied")
        v_ready, v_gelu, v_squared, v_root, v_scaled = (
            sem("v_ready"), sem("v_gelu"), sem("v_squared"), sem("v_root"), sem("v_scaled"))
        u_ready, u_gelu = sem("u_ready"), sem("u_gelu")
        gate_ready, gate_taken = sem("gate_ready"), sem("gate_taken")
        mix_ready, ya_set = sem("mix_ready"), sem("ya_set")
        pa_ready, pa_taken = sem("pa_ready"), sem("pa_taken")
        mask_set = sem("mask_set")
        s_ready, s_masked, bias_set, exp_done = sem("s_ready"), sem("s_masked"), sem("bias_set"), sem("exp_done")
        inv_set, p_scaled = sem("inv_set"), sem("p_scaled")
        pT_ready, pT_taken = sem("pT_ready"), sem("pT_taken")
        o_ready, o_taken = sem("o_ready"), sem("o_taken")
        yb_ready, yb_taken = sem("yb_ready"), sem("yb_taken")
        pb_ready, merged = sem("pb_ready"), sem("merged")
        x2_ready, x2_taken = sem("x2_ready"), sem("x2_taken")
        dve_step = sem("dve_step")

        QBLOCKS = [3, 2, 1]
        HALVES = [(b, g) for b in range(NT) for g in range(2)]
        PT_BEFORE = [sum(b + 1 for b, _ in HALVES[:i]) for i in range(len(HALVES) + 1)]
        MV = 16

        def act_half(i, act):
            b, g = HALVES[i]
            for kt in range(b + 1):
                j = PT_BEFORE[i] + kt
                act.wait_ge(pT_ready, j + 1)
                if i >= 1:
                    act.wait_ge(o_ready, i)
                act.activation(pT[:, kt, :], banks[4 + j % 2][:, :], ACT.Copy).then_inc(pT_taken, 1)
            act.wait_ge(o_ready, i + 1)
            act.activation(oT[:, 4 * g:4 * g + 4, b * P:(b + 1) * P],
                           banks[6 + g][:, :].rearrange("p (h q) -> p h q", h=4), ACT.Copy).then_inc(o_taken, 1)

        def inverse(dve, i):
            b, g = HALVES[i]
            dve.wait_ge(exp_done, 4 * i + 4)
            dve.reciprocal(den[:, b, 4 * g:4 * g + 4], den[:, b, 4 * g:4 * g + 4]).then_inc(inv_set, 1)

        block = ctx.enter_context(nc.Block())

        @block.sync
        def _(sp):
            for t in range(NT):
                sp.dma_start(x_sb[:, t, :], x_rows[:, t, :]).then_inc(x_loaded, 16)
            sp.wait_ge(vecs_zeroed, 1)
            for at, vec, n in ((N1, norm1_g, 8), (N2, norm2_g, 8), (QL, q_lat_g, 2), (QN, q_norm_g, 1),
                               (VG, gmlp_v_g, 1)):
                sp.dma_start(vecs[at:at + n, :], vec.rearrange("(a p) -> a p", p=P)).then_inc(vecs_loaded, 16)
            sp.dma_start(vecs[KI:KI + 1, 0:ID], k_idx_g.rearrange("(a p) -> a p", a=1)).then_inc(vecs_loaded, 16)
            sp.dma_start(w_lat, in_cols(OFF_LAT, LAT)).then_inc(lat_w_loaded, 16)
            sp.dma_start(kvg[:, :], kv_norm_g.rearrange("(a p) -> a p", a=1).to_broadcast([P, KVR])
                         ).then_inc(first_loaded, 16)
            sp.dma_start(wqi, w_q_idx.rearrange("(k p) h d -> p k (h d)", p=P)).then_inc(qw_loaded, 16)
            sp.dma_start(wuq, w_uq.rearrange("(k p) h d -> p k (h d)", p=P)).then_inc(qw_loaded, 16)
            sp.dma_start(wsp, w_spatial.rearrange("g t s -> t g s")).then_inc(first_loaded, 16)
            sp.dma_start(w_v, in_cols(OFF_V, 512)).then_inc(v_w_loaded, 16)
            sp.dma_start(w_u, in_cols(OFF_U, 512)).then_inc(u_w_loaded, 16)
            sp.dma_start(bspat[:, :, :].rearrange("p g t -> p (g t)"),
                         b_spatial.rearrange("(a g) t -> a (g t)", a=1).to_broadcast([P, G * P])
                         ).then_inc(small_loaded, 16)
            sp.dma_start(br_sb[:, :], b_router.rearrange("(a n) -> a n", a=1).to_broadcast([P, NE])
                         ).then_inc(small_loaded, 16)
            sp.dma_start(wr_sb[:, :, :], w_router.rearrange("(k p) n -> p k n", p=P)).then_inc(small_loaded, 16)
            sp.wait_ge(wuv_zeroed, 1)
            for h in range(H):
                sp.dma_start(wuv[:, h, HV * (h % 2):HV * (h % 2) + HV], w_uv[h]).then_inc(small_loaded, 16)
            for i in range(4):
                if i == 1:
                    sp.wait_ge(lat_ready, NT)
                if i == 2:
                    sp.wait_ge(v_ready, NT)
                if i == 3:
                    sp.wait_ge(u_ready, G)
                sp.dma_start(w_gate[i], in_cols(OFF_GATE + 512 * i, 512)).then_inc(gate_w_loaded[i], 16)
            sp.wait_ge(q_ready, H)
            sp.wait_ge(qss_ready, H)
            sp.wait_ge(wsT_ready, G)
            sp.dma_start(wpa, w_proj_a.rearrange("(k p) n -> p k n", p=P)).then_inc(pa_loaded, 16)
            sp.wait_ge(gate_ready, 4)
            sp.dma_start(wpb, w_proj_b.rearrange("(k p) n -> p k n", p=P)).then_inc(pb_loaded, 16)
            wo_rows = w_out.rearrange("(k p) n -> p k n", p=P)
            for i in range(2):
                sp.wait_ge(gate_ready, 8 + 4 * i)
                sp.dma_start(wout[:, 4 * i:4 * i + 4, :], wo_rows[:, 4 * i:4 * i + 4, :]).then_inc(out_w_loaded, 16)
            sp.wait_ge(gate_ready, 16)
            for j in (4, 5):
                sp.dma_start(ring[:, j, :], w_exp1[0, j * P:(j + 1) * P, :]).then_inc(landed[j], 16)
            sp.wait_ge(o_ready, len(HALVES))
            sp.wait_ge(s_masked, NT * H)
            sp.wait_ge(pT_ready, PT_BEFORE[-1])
            for t in range(NT):
                sp.dma_start(x_sb[:, t, :], x_rows[:, t, :]).then_inc(x_again, 16)
            sp.wait_ge(x2_ready, 2 * NT)
            for j in (0, 1, 2, 3):
                sp.dma_start(ring[:, j, :], w_exp1[0, j * P:(j + 1) * P, :]).then_inc(landed[j], 16)
            sp.wait_ge(x_again, 16 * NT)
            sp.wait_ge(small_loaded, 16 * 11)

        @block.gpsimd
        def _(pool):
            pool.memset(vecs[:, :], 0.0).then_inc(vecs_zeroed, 1)
            pool.memset(ident[:, :], 0.0).then_inc(consts_set, 1)
            pool.memset(ones[:, :], 1.0).then_inc(consts_set, 1)
            pool.wait_ge(consts_set, 2)
            pool.affine_select(out=ident[:, :], in_=ident[:, :], compare_op=ALU.not_equal, fill=1.0, base=0,
                               pattern=[[-1, P]], channel_multiplier=1).then_inc(consts_set, 1)
            pool.wait_ge(first_loaded, 16 * 2)
            pool.affine_select(out=wsp, in_=wsp, compare_op=ALU.is_ge, fill=0.0, base=0,
                               pattern=[[0, G], [-1, P]], channel_multiplier=1).then_inc(masked, 1)
            pool.wait_ge(xT_ready, 2 * NT)
            pool.memset(mask[:, 0, 0:P], 0.0).then_inc(masked, 1)
            pool.wait_ge(masked, 2)
            pool.affine_select(out=mask[:, 0, 0:P], in_=mask[:, 0, 0:P], compare_op=ALU.is_ge, fill=NEG,
                               base=0, pattern=[[-1, P]], channel_multiplier=1).then_inc(masked, 1)
            for n, b in enumerate(QBLOCKS):
                pool.wait_ge(score_done, n + 1)
                diag = mask[:, b, b * P:(b + 1) * P]
                pool.affine_select(out=diag, in_=diag, compare_op=ALU.is_ge, fill=NEG,
                                   base=0, pattern=[[-1, P]], channel_multiplier=1).then_inc(masked, 1)
            for i, (b, g) in enumerate(HALVES):
                n = (b + 1) * P
                for h in range(4):
                    hh = 4 * g + h
                    pool.wait_ge(inv_set, i + 1)
                    pool.tensor_scalar(probs[i % 2][:, h, 0:n], probs[i % 2][:, h, 0:n], den[:, b, hh:hh + 1], None,
                                       ALU.mult).then_inc(p_scaled, 1)

        @block.scalar
        def _(act):
            for t in range(NT):
                act.wait_ge(x_loaded, 16 * NT)
                act.activation(gaT[:, 2 * t:2 * t + 2, :].rearrange("p a b -> p (a b)"), x_sb[:, t, :], ACT.Square,
                               accum_out=ss[:, 12 + t:13 + t]).then_inc(x_squared, 1)
            act.wait_ge(x_root, 1)
            act.activation(ss[:, 12:16], ss[:, 12:16], ACT.Sqrt).then_inc(x_root, 1)
            for t in range(NT):
                act.wait_ge(lat_ready, t + 1)
                act.activation(lat_sb[:, t, :], banks[4 + t][:, 0:LAT], ACT.Copy).then_inc(lat_copied, 1)
            act.wait_ge(lat_copied, NT)
            for t in range(NT):
                for j, (a, n) in enumerate(((0, QR), (C_KV, KVR), (C_KI, ID))):
                    act.activation(gaT[:, t, a:a + n], lat_sb[:, t, a:a + n], ACT.Square,
                                   accum_out=ss[:, 4 * j + t:4 * j + t + 1]).then_inc(lat_squared, 1)
            act.wait_ge(lat_root, 3)
            act.activation(ss[:, 0:12], ss[:, 0:12], ACT.Sqrt).then_inc(lat_root, 1)
            for h in range(IH):
                act.wait_ge(qidx_ready, h + 1)
                act.activation(qidxT[:, h, :], banks[4 + h][0:ID, :], ACT.Copy).then_inc(qidx_copied, 1)
            for n, b in enumerate(QBLOCKS):
                if n:
                    act.wait_ge(score_done, n)
                for h in range(IH):
                    act.wait_ge(logit_ready, 4 * n + h + 1)
                    act.activation(relu[:, h, 0:(b + 1) * P], banks[4 * (n % 2) + h][:, 0:(b + 1) * P], ACT.Relu,
                                   scale=ID ** -0.5).then_inc(relu_done, 1)
            for h in range(H):
                act.wait_ge(q_ready, h + 1)
                act.activation(qT[:, h, :], banks[4 + h % 4][:, :], ACT.Copy, scale=cols[:, QN:QN + 1]
                               ).then_inc(q_copied, 1)
                if h >= 2:
                    act.wait_ge(qss_ready, h - 1)
                act.activation(qsq[:, h % 2, :], banks[4 + h % 4][:, :], ACT.Square).then_inc(q_squared, 1)
            act.wait_ge(qss_ready, H)
            act.activation(ss[:, 16:48], banks[0][:, 0:NT * H], ACT.Copy).then_inc(qss_copied, 1)
            act.wait_ge(q_root, 1)
            act.activation(mx[:, :, :].rearrange("p t h -> p (t h)"), den[:, :, :].rearrange("p t h -> p (t h)"),
                           ACT.Sqrt).then_inc(q_root, 1)
            for t in range(NT):
                act.wait_ge(v_ready, t + 1)
                act.activation(v_sb[:, t, :], banks[4 + t][:, :], ACT.Gelu_apprx_tanh).then_inc(v_gelu, 1)
            for g in range(G):
                act.wait_ge(u_ready, g + 1)
                act.activation(uT[:, g, :], banks[g][:, :], ACT.Gelu_apprx_tanh).then_inc(u_gelu, 1)
            act.wait_ge(v_gelu, NT)
            act.wait_ge(q_scale_set, 1)
            act.wait_ge(lat_squared, 3 * NT)
            for t in range(NT):
                for g in range(G):
                    act.activation(gaT[:, t, g * P:(g + 1) * P], v_sb[:, t, g * P:(g + 1) * P], ACT.Square,
                                   accum_out=ss[:, 16 + 4 * t + g:17 + 4 * t + g]).then_inc(v_squared, 1)
            act.wait_ge(v_root, 1)
            act.activation(ss[:, 16:32], ss[:, 16:32], ACT.Sqrt).then_inc(v_root, 1)
            for i in range(16):
                act.wait_ge(gate_ready, i + 1)
                if i == 0:
                    act.wait_ge(v_squared, NT * G)
                if i == 12:
                    act.wait_ge(score_done, 3)
                dst = gaT[:, i, :] if i < 8 else gbT[:, i - 8, :]
                act.activation(dst, banks[(4 + i) % 8][:, :], ACT.Sigmoid).then_inc(gate_taken, 1)
            for i, (b, g) in enumerate(HALVES):
                n = (b + 1) * P
                for h in range(4):
                    hh = 4 * g + h
                    act.wait_ge(bias_set, i + 1)
                    act.activation(probs[i % 2][:, h, 0:n], probs[i % 2][:, h, 0:n], ACT.Exp,
                                   scale=qs[:, b, hh:hh + 1], bias=mx[:, b, hh:hh + 1],
                                   accum_out=den[:, b, hh:hh + 1]).then_inc(exp_done, 1)
                if i >= 1:
                    act_half(i - 1, act)
            act_half(len(HALVES) - 1, act)
            for j in range(4):
                act.wait_ge(yb_ready, j + 1)
                if j == 0:
                    act.wait_ge(pa_ready, KD)
                act.activation(ybT[:, j, :], banks[j][:, :], ACT.Copy).then_inc(yb_taken, 1)

        @block.vector
        def _(dve):
            step = Steps(dve, dve_step)

            def mean(dst, src, n, signal):
                dve.tensor_scalar(dst, src, 1.0 / n, EPS, ALU.mult, ALU.add).then_inc(signal, 1)

            dve.memset(wuv[:, :, :], 0.0).then_inc(wuv_zeroed, 1)
            dve.wait_ge(x_squared, NT)
            mean(ss[:, 12:16], ss[:, 12:16], D, x_root)
            dve.wait_ge(x_root, 2)
            step(dve.reciprocal(ss[:, 12:16], ss[:, 12:16]))
            for t in range(NT):
                dve.tensor_scalar(x_sb[:, t, :], x_sb[:, t, :], ss[:, 12 + t:13 + t], None, ALU.mult
                                  ).then_inc(x_scaled, 1)
            dve.wait_ge(colsT_ready, 1)
            dve.tensor_copy(cols[:, :], banks[7][:, 0:21]).then_inc(cols_set, 1)
            dve.wait_ge(cols_set, 1)
            for j in range(2 * NT):
                t, half = j // 2, j % 2
                dve.wait_ge(xT_ready, j + 1)
                dve.tensor_tensor(xnT[:, 4 * half:4 * half + 4, t * P:(t + 1) * P],
                                  banks[j % 4][:, :].rearrange("p (k q) -> p k q", k=4),
                                  cols[:, N1 + 4 * half:N1 + 4 * half + 4].unsqueeze(2).to_broadcast([P, 4, P]),
                                  ALU.mult).then_inc(xT_taken, 1)
            step(dve.tensor_scalar(cols[:, QN:QN + 1], cols[:, QN:QN + 1], KVR ** -0.5, None, ALU.mult))
            dve.wait_ge(lat_squared, 3 * NT)
            for j, n in enumerate((QR, KVR, ID)):
                mean(ss[:, 4 * j:4 * j + 4], ss[:, 4 * j:4 * j + 4], n, lat_root)
            dve.wait_ge(lat_root, 4)
            step(dve.reciprocal(ss[:, 0:12], ss[:, 0:12]))
            dve.wait_ge(first_loaded, 16 * 2)
            for t in range(NT):
                dve.tensor_scalar(lat_sb[:, t, 0:QR], lat_sb[:, t, 0:QR], ss[:, t:t + 1], None, ALU.mult
                                  ).then_inc(lat_scaled, 1)
            for t in range(NT):
                dve.scalar_tensor_tensor(kv[:, t, :], lat_sb[:, t, C_KV:C_KV + KVR], ss[:, 4 + t:5 + t], kvg[:, :],
                                         ALU.mult, ALU.mult).then_inc(lat_scaled, 1)
            for t in range(NT):
                dve.tensor_scalar(lat_sb[:, t, C_KI:C_KI + ID], lat_sb[:, t, C_KI:C_KI + ID], ss[:, 8 + t:9 + t],
                                  None, ALU.mult).then_inc(lat_scaled, 1)
            step(dve.tensor_scalar(widx[:, :, :], lat_sb[:, :, C_WI:LAT], IH ** -0.5, None, ALU.mult))
            for j in range(2):
                dve.wait_ge(latT_ready, j + 1)
                dve.tensor_scalar(cqT[:, j, :], banks[j][:, :], cols[:, QL + j:QL + j + 1], None, ALU.mult
                                  ).then_inc(latT_taken, 1)
            dve.wait_ge(latT_ready, 3)
            dve.tensor_scalar(kidxT[:, :], banks[2][0:ID, :], cols[0:ID, KI:KI + 1], None, ALU.mult
                              ).then_inc(latT_taken, 1)
            dve.wait_ge(latT_ready, 4)
            dve.tensor_copy(kvT[:, :], banks[3][:, :]).then_inc(latT_taken, 1)
            for n, b in enumerate(QBLOCKS):
                w = (b + 1) * P
                for h in range(IH):
                    dve.wait_ge(relu_done, 4 * n + h + 1)
                    acc = mask[:, b, 0:w]
                    if h == 0:
                        step(dve.tensor_scalar(acc, relu[:, h, 0:w], widx[:, b, h:h + 1], None, ALU.mult))
                    else:
                        ins = dve.scalar_tensor_tensor(acc, relu[:, h, 0:w], widx[:, b, h:h + 1], acc,
                                                       ALU.mult, ALU.add)
                        if h < IH - 1:
                            step(ins)
                        else:
                            ins.then_inc(score_done, 1)
            dve.wait_ge(wsT_ready, G)
            dve.tensor_copy(wsT[:, :, :].rearrange("p g t -> p (g t)"), banks[1][:, :]).then_inc(wsT_copied, 1)
            dve.wait_ge(qss_copied, 1)
            mean(den[:, :, :].rearrange("p t h -> p (t h)"), ss[:, 16:48], KVR, q_root)
            dve.wait_ge(q_root, 2)
            dve.reciprocal(qs[:, :, :].rearrange("p t h -> p (t h)"), mx[:, :, :].rearrange("p t h -> p (t h)")
                           ).then_inc(q_scale_set, 1)
            for n, b in enumerate(QBLOCKS):
                w = (b + 1) * P
                dve.wait_ge(masked, 4 + n)
                work = mask[:, b, 0:w]
                for _ in range(TOPK // 8):
                    step(dve.max(top8[:, :], work))
                    step(dve.match_replace(work, top8[:, :], work, TAKEN))
                dve.tensor_scalar(work, work, TAKEN_BELOW, NEG, ALU.is_gt, ALU.mult).then_inc(mask_set, 1)
            dve.wait_ge(v_squared, NT * G)
            mean(ss[:, 16:32], ss[:, 16:32], P, v_root)
            dve.wait_ge(v_root, 2)
            step(dve.reciprocal(ss[:, 16:32], ss[:, 16:32]))
            for t in range(NT):
                vt = v_sb[:, t, :].rearrange("p (g n) -> p g n", g=G)
                dve.tensor_tensor(vt, vt, ss[:, 16 + 4 * t:20 + 4 * t].unsqueeze(2).to_broadcast([P, G, P]),
                                  ALU.mult).then_inc(v_scaled, 1)
            dve.wait_ge(small_loaded, 16 * 11)
            dve.wait_ge(u_gelu, G)
            for g in range(G):
                dve.wait_ge(mix_ready, g + 1)
                mixed = banks[4 + g][:, :].rearrange("p (t n) -> p t n", t=NT)
                step(dve.scalar_tensor_tensor(mixed, mixed, cols[:, VG:VG + 1],
                                              bspat[:, g:g + 1, :].to_broadcast([P, NT, P]), ALU.mult, ALU.add))
                dve.tensor_tensor(uT[:, g, :], uT[:, g, :], banks[4 + g][:, :], ALU.mult).then_inc(ya_set, 1)
            for c in range(KD):
                dve.wait_ge(pa_ready, c + 1)
                dve.wait_ge(gate_taken, 16)
                dve.tensor_tensor(gaT[:, c, :], gaT[:, c, :], banks[c][:, :], ALU.mult).then_inc(pa_taken, 1)
            dve.wait_ge(mask_set, 3)
            dve.wait_ge(masked, 6)
            for i, (b, g) in enumerate(HALVES):
                n = (b + 1) * P
                if i >= 2:
                    dve.wait_ge(pT_ready, PT_BEFORE[i - 1])
                for h in range(4):
                    hh = 4 * g + h
                    dve.wait_ge(s_ready, 4 * i + h + 1)
                    dve.tensor_tensor_reduce(probs[i % 2][:, h, 0:n], banks[h][:, 0:n], mask[:, b, 0:n], 1.0, TAKEN,
                                             ALU.add, ALU.max, mx[:, b, hh:hh + 1]).then_inc(s_masked, 1)
                dve.wait_ge(s_masked, 4 * i + 4)
                dve.scalar_tensor_tensor(mx[:, b, 4 * g:4 * g + 4], mx[:, b, 4 * g:4 * g + 4], -1.0,
                                         qs[:, b, 4 * g:4 * g + 4], ALU.mult, ALU.mult).then_inc(bias_set, 1)
                if i >= 1:
                    inverse(dve, i - 1)
            inverse(dve, len(HALVES) - 1)
            for c in range(KD):
                dve.wait_ge(pb_ready, c + 1)
                step(dve.tensor_tensor(gbT[:, c, :], gbT[:, c, :], banks[4 + c % 4][:, :], ALU.mult))
                dve.tensor_tensor(gaT[:, c, :], gaT[:, c, :], gbT[:, c, :], ALU.add).then_inc(merged, 1)
            for j in range(2 * NT):
                t, n = j // 2, j % 2
                dve.wait_ge(x2_ready, j + 1)
                dve.wait_ge(x_again, 16 * NT)
                dve.tensor_tensor(x_sb[:, t, 512 * n:512 * n + 512], x_sb[:, t, 512 * n:512 * n + 512],
                                  banks[j % 4][:, :], ALU.add).then_inc(x2_taken, 1)
            dve.wait_ge(x2_taken, 2 * NT)

        @block.tensor
        def _(pe):
            def product(bank, pairs):
                for k, (lhsT, rhs) in enumerate(pairs):
                    last = pe.matmul(bank, lhsT, rhs, start=(k == 0), stop=(k == len(pairs) - 1))
                return last

            pe.wait_ge(consts_set, 3)
            pe.wait_ge(vecs_loaded, 16 * 6)
            pe.transpose(banks[7][:, 0:21], vecs[:, :], ident[0:21, 0:21]).then_inc(colsT_ready, 1)
            for j in range(2 * NT):
                t, half = j // 2, j % 2
                pe.wait_ge(x_scaled, t + 1)
                if j >= 4:
                    pe.wait_ge(xT_taken, j - 3)
                for k in range(4):
                    last = pe.transpose(banks[j % 4][:, k * P:(k + 1) * P],
                                        x_sb[:, t, (4 * half + k) * P:(4 * half + k + 1) * P], ident[:, :])
                last.then_inc(xT_ready, 1)
            pe.wait_ge(lat_w_loaded, 16)
            pe.wait_ge(cols_set, 1)
            for t in range(NT):
                pe.wait_ge(xT_taken, 2 * t + 2)
                product(banks[4 + t][:, 0:LAT], [(xnT[:, k, t * P:(t + 1) * P], w_lat[:, k, :]) for k in range(KD)]
                        ).then_inc(lat_ready, 1)
            pe.wait_ge(xT_taken, 2 * NT)
            for j in range(2):
                pe.wait_ge(lat_scaled, NT)
                for t in range(NT):
                    last = pe.transpose(banks[j][:, t * P:(t + 1) * P], lat_sb[:, t, j * P:(j + 1) * P], ident[:, :])
                last.then_inc(latT_ready, 1)
            pe.wait_ge(lat_scaled, 3 * NT)
            for t in range(NT):
                last = pe.transpose(banks[2][0:ID, t * P:(t + 1) * P], lat_sb[:, t, C_KI:C_KI + ID], ident[:, :])
            last.then_inc(latT_ready, 1)
            for t in range(NT):
                last = pe.transpose(banks[3][:, t * P:(t + 1) * P], kv[:, t, :], ident[:, :])
            last.then_inc(latT_ready, 1)
            pe.wait_ge(qw_loaded, 32)
            pe.wait_ge(latT_taken, 2)
            pe.wait_ge(lat_copied, NT)
            for h in range(IH):
                product(banks[4 + h][0:ID, :], [(wqi[:, k, h * ID:(h + 1) * ID], cqT[:, k, :]) for k in range(2)]
                        ).then_inc(qidx_ready, 1)
            pe.wait_ge(latT_taken, 4)
            for n, b in enumerate(QBLOCKS):
                for h in range(IH):
                    if n == 0:
                        pe.wait_ge(qidx_copied, h + 1)
                    elif n == 1:
                        pe.wait_ge(qidx_copied, IH)
                    else:
                        pe.wait_ge(relu_done, h + 1)
                    product(banks[4 * (n % 2) + h][:, 0:(b + 1) * P],
                            [(qidxT[:, h, b * P:(b + 1) * P], kidxT[:, 0:(b + 1) * P])]).then_inc(logit_ready, 1)
            def query_squares(h):
                pe.wait_ge(q_squared, h + 1)
                if h == 0:
                    pe.wait_ge(relu_done, 12)
                for t in range(NT):
                    last = pe.matmul(banks[0][:, t * H + h:t * H + h + 1], qsq[:, h % 2, t * P:(t + 1) * P],
                                     ones[:, 0:1], start=True, stop=True)
                last.then_inc(qss_ready, 1)

            for h in range(H):
                if h < 4:
                    pe.wait_ge(relu_done, 5 + h)
                else:
                    pe.wait_ge(q_squared, h - 3)
                product(banks[4 + h % 4][:, :], [(wuq[:, k, h * P:(h + 1) * P], cqT[:, k, :]) for k in range(2)]
                        ).then_inc(q_ready, 1)
                if h >= 1:
                    query_squares(h - 1)
            query_squares(H - 1)
            pe.wait_ge(masked, 1)
            for g in range(G):
                pe.transpose(banks[1][:, g * P:(g + 1) * P], wsp[:, g, :], ident[:, :]).then_inc(wsT_ready, 1)
            pe.wait_ge(v_w_loaded, 16)
            for t in range(NT):
                pe.wait_ge(q_squared, 5 + t)
                product(banks[4 + t][:, :], [(xnT[:, k, t * P:(t + 1) * P], w_v[:, k, :]) for k in range(KD)]
                        ).then_inc(v_ready, 1)
            pe.wait_ge(u_w_loaded, 16)
            pe.wait_ge(qss_copied, 1)
            pe.wait_ge(wsT_copied, 1)
            for g in range(G):
                product(banks[g][:, :], [(w_u[:, k, g * P:(g + 1) * P], xnT[:, k, :]) for k in range(KD)]
                        ).then_inc(u_ready, 1)
            for i in range(16):
                if i % 4 == 0:
                    pe.wait_ge(gate_w_loaded[i // 4], 16)
                if i < 4:
                    pe.wait_ge(v_gelu, i + 1)
                elif i < 8:
                    pe.wait_ge(u_gelu, i - 3)
                else:
                    pe.wait_ge(gate_taken, i - 7)
                c = i % 4
                product(banks[(4 + i) % 8][:, :],
                        [(w_gate[i // 4][:, k, c * P:(c + 1) * P], xnT[:, k, :]) for k in range(KD)]
                        ).then_inc(gate_ready, 1)
            for g in range(G):
                pe.wait_ge(gate_taken, 9 + g)
                pe.wait_ge(v_scaled, NT)
                for t in range(NT):
                    last = pe.matmul(banks[4 + g][:, t * P:(t + 1) * P], v_sb[:, t, g * P:(g + 1) * P], wsT[:, g, :],
                                     start=True, stop=True)
                last.then_inc(mix_ready, 1)
            pe.wait_ge(pa_loaded, 16)
            pe.wait_ge(gate_taken, 16)
            pe.wait_ge(ya_set, G)
            for c in range(KD):
                product(banks[c][:, :], [(wpa[:, k, c * P:(c + 1) * P], uT[:, k, :]) for k in range(G)]
                        ).then_inc(pa_ready, 1)

            def scores(i):
                b, g = HALVES[i]
                for h in range(4):
                    if i == 0:
                        pe.wait_ge(pa_taken, h + 1)
                    else:
                        pe.wait_ge(s_masked, 4 * (i - 1) + h + 1)
                    product(banks[h][:, 0:(b + 1) * P],
                            [(qT[:, 4 * g + h, b * P:(b + 1) * P], kvT[:, 0:(b + 1) * P])]).then_inc(s_ready, 1)

            def mix_values(i):
                b, g = HALVES[i]
                pe.wait_ge(p_scaled, 4 * i + 4)
                if i == 0:
                    pe.wait_ge(pa_taken, KD)
                for kt in range(b + 1):
                    j = PT_BEFORE[i] + kt
                    if j >= 2:
                        pe.wait_ge(pT_taken, j - 1)
                    for h in range(4):
                        last = pe.transpose(banks[4 + j % 2][:, h * P:(h + 1) * P],
                                            probs[i % 2][:, h, kt * P:(kt + 1) * P], ident[:, :])
                    last.then_inc(pT_ready, 1)
                if i >= 2:
                    pe.wait_ge(o_taken, i - 1)
                for kt in range(b + 1):
                    pe.wait_ge(pT_taken, PT_BEFORE[i] + kt + 1)
                    last = pe.matmul(banks[6 + g][:, :], kv[:, kt, :], pT[:, kt, :], start=(kt == 0), stop=(kt == b))
                last.then_inc(o_ready, 1)

            for i in range(len(HALVES)):
                scores(i)
                if i >= 1:
                    mix_values(i - 1)
            mix_values(len(HALVES) - 1)
            pe.wait_ge(small_loaded, 16 * 11)
            for j in range(4):
                pe.wait_ge(s_masked, NT * H)
                pe.wait_ge(o_taken, len(HALVES))
                product(banks[j][:, :], [(wuv[:, 2 * j + a, :], oT[:, 2 * j + a, :]) for a in range(2)]
                        ).then_inc(yb_ready, 1)
            pe.wait_ge(pb_loaded, 16)
            pe.wait_ge(yb_taken, 4)
            for c in range(KD):
                if c >= 4:
                    pe.wait_ge(merged, c - 3)
                product(banks[4 + c % 4][:, :], [(wpb[:, k, c * P:(c + 1) * P], ybT[:, k, :]) for k in range(G)]
                        ).then_inc(pb_ready, 1)
            pe.wait_ge(out_w_loaded, 32)
            pe.wait_ge(merged, KD)
            for j in range(2 * NT):
                t, n = j // 2, j % 2
                if j >= 4:
                    pe.wait_ge(x2_taken, j - 3)
                product(banks[j % 4][:, :], [(gaT[:, k, t * P:(t + 1) * P], wout[:, k, 512 * n:512 * n + 512])
                                             for k in range(KD)]).then_inc(x2_ready, 1)


def routing(nc, sem, banks, x_sb, ident, ones, norm2_g, wr_sb, br_sb, tab, rk, bias, eq, slot_iota,
            counts, over_flag, xn2_rows, b_exp1, b_exp2):
    with ExitStack() as ctx:
        def sb(name, shape, dt=F32):
            return ctx.enter_context(nc.sbuf_tensor(name, shape, dt))

        xs = sb("xs", [P, NT, D])
        xn2T = sb("xn2T", [P, KD, S])
        r_ss = sb("r_ss", [P, NT])
        logits = sb("logits", [P, NT, NE])
        top = sb("top", [P, NT, 8])
        top_at = sb("top_at", [P, NT, 8], U32)
        top_col = sb("top_col", [P, NT, 8])
        gate = sb("gate", [P, NT, TK])
        negmax = sb("negmax", [P, NT])
        gsum = sb("gsum", [P, NT])
        e_iota = sb("e_iota", [P, NE])
        hot = sb("hot", [P, NT, TK, NE])
        routed = sb("routed", [P, NT, NE])
        pair_row = sb("pair_row", [P, NT])
        token = sb("token", [P, NT])
        before = sb("before", [P, P])
        bfull = sb("bfull", [96, 2 * DE + D])
        brest = sb("brest", [96, 2 * DE + D])
        over_f = sb("over_f", [P, 1])

        gain2 = sb("gain2", [P, D])
        gain_loaded = sem("gain_loaded")
        bias_loaded, rows_stored = sem("bias_loaded"), sem("rows_stored")
        r_consts, r_squared, r_root, r_scaled = sem("r_consts"), sem("r_squared"), sem("r_root"), sem("r_scaled")
        r_T_ready, r_T_taken = sem("r_T_ready"), sem("r_T_taken")
        route_ready, route_taken, top_set, exp_set = sem("route_ready"), sem("route_taken"), sem("top_set"), sem("exp_set")
        routed_set, rank_ready, count_ready = sem("routed_set"), sem("rank_ready"), sem("count_ready")
        r_step = sem("r_step")
        block = ctx.enter_context(nc.Block())

        @block.sync
        def _(sp):
            sp.dma_start(gain2[:, :], norm2_g.rearrange("(a n) -> a n", a=1).to_broadcast([P, D])
                         ).then_inc(gain_loaded, 16)
            for part in range(3):
                sp.dma_start(bfull[32 * part:32 * part + 32, 0:2 * DE], b_exp1).then_inc(bias_loaded, 16)
                sp.dma_start(bfull[32 * part:32 * part + 32, 2 * DE:2 * DE + D], b_exp2).then_inc(bias_loaded, 16)
            rows = xn2_rows.rearrange("(t p) d -> p t d", p=P)
            for t in range(NT):
                sp.wait_ge(r_scaled, t + 1)
                sp.dma_start(rows[:, t, :], xs[:, t, :]).then_inc(rows_stored, 16)
            sp.wait_ge(rows_stored, 16 * NT)

        @block.gpsimd
        def _(pool):
            pool.iota(e_iota[:, :], pattern=[[1, NE]], base=0, channel_multiplier=0,
                      allow_small_or_imprecise_dtypes=True).then_inc(r_consts, 1)
            pool.iota(slot_iota[:, :], pattern=[[1, P]], base=0, channel_multiplier=0,
                      allow_small_or_imprecise_dtypes=True).then_inc(r_consts, 1)
            pool.iota(token[:, :], pattern=[[P, NT]], base=-int(BIG), channel_multiplier=1,
                      allow_small_or_imprecise_dtypes=True).then_inc(r_consts, 1)
            pool.iota(pair_row[:, :], pattern=[[TK * P, NT]], base=-int(BIG), channel_multiplier=TK,
                      allow_small_or_imprecise_dtypes=True).then_inc(r_consts, 1)
            pool.memset(before[:, :], 1.0).then_inc(r_consts, 1)
            pool.memset(eq[:, :], 0.0).then_inc(r_consts, 1)
            pool.memset(tab[:, :, :, :], 0.0).then_inc(r_consts, 1)
            pool.memset(rk[:, :, :], -1.0).then_inc(r_consts, 1)
            pool.wait_ge(r_consts, 8)
            pool.affine_select(out=before[:, :], in_=before[:, :], compare_op=ALU.is_gt, fill=0.0, base=0,
                               pattern=[[1, P]], channel_multiplier=-1).then_inc(r_consts, 1)
            for part in range(3):
                pool.wait_ge(r_consts, 9 + part)
                pool.affine_select(out=eq[:, :], in_=eq[:, :], compare_op=ALU.not_equal, fill=1.0, base=-32 * part,
                                   pattern=[[-1, NEP]], channel_multiplier=1).then_inc(r_consts, 1)

        @block.scalar
        def _(act):
            for t in range(NT):
                act.activation(xs[:, t, :], x_sb[:, t, :], ACT.Square, accum_out=r_ss[:, t:t + 1]).then_inc(r_squared, 1)
            act.wait_ge(r_root, 1)
            act.activation(r_ss[:, :], r_ss[:, :], ACT.Sqrt).then_inc(r_root, 1)
            for t in range(NT):
                act.wait_ge(top_set, t + 1)
                act.activation(gate[:, t, :], top[:, t, 0:TK], ACT.Exp, bias=negmax[:, t:t + 1],
                               accum_out=gsum[:, t:t + 1]).then_inc(exp_set, 1)

        @block.vector
        def _(dve):
            step = Steps(dve, r_step)
            dve.wait_ge(r_squared, NT)
            dve.tensor_scalar(r_ss[:, :], r_ss[:, :], 1.0 / D, EPS, ALU.mult, ALU.add).then_inc(r_root, 1)
            dve.wait_ge(r_root, 2)
            step(dve.reciprocal(r_ss[:, :], r_ss[:, :]))
            for t in range(NT):
                if t == 0:
                    dve.wait_ge(gain_loaded, 16)
                dve.scalar_tensor_tensor(xs[:, t, :], x_sb[:, t, :], r_ss[:, t:t + 1], gain2[:, :], ALU.mult, ALU.mult
                                         ).then_inc(r_scaled, 1)
            for j in range(2 * NT):
                t, half = j // 2, j % 2
                dve.wait_ge(r_T_ready, j + 1)
                dve.tensor_copy(xn2T[:, 4 * half:4 * half + 4, t * P:(t + 1) * P],
                                banks[4 + j % 2][:, :].rearrange("p (k q) -> p k q", k=4)).then_inc(r_T_taken, 1)
            dve.wait_ge(r_consts, 12)
            for t in range(NT):
                dve.wait_ge(route_ready, t + 1)
                step(dve.tensor_tensor(logits[:, t, :], banks[t][:, 0:NE], br_sb[:, :], ALU.add))
                step(dve.max(top[:, t, :], logits[:, t, :]))
                dve.tensor_scalar(negmax[:, t:t + 1], top[:, t, 0:1], -1.0, None, ALU.mult).then_inc(top_set, 1)
                step(dve.max_index(top_at[:, t, :], top[:, t, :], logits[:, t, :]))
                step(dve.tensor_copy(top_col[:, t, :], top_at[:, t, :]))
                for k in range(TK):
                    ins = dve.tensor_scalar(hot[:, t, k, :], e_iota[:, :], top_col[:, t, k:k + 1], None, ALU.is_equal)
                step(ins)
                ins = dve.tensor_reduce(routed[:, t, :], hot[:, t, :, :].rearrange("p k e -> p e k"), AX.X, ALU.add)
                ins.then_inc(routed_set, 1)
            for t in range(NT):
                dve.wait_ge(exp_set, t + 1)
                step(dve.reciprocal(gsum[:, t:t + 1], gsum[:, t:t + 1]))
                step(dve.tensor_scalar(gate[:, t, :], gate[:, t, :], gsum[:, t:t + 1], None, ALU.mult))
                dve.wait_ge(routed_set, t + 1)
                dve.tensor_scalar(tab[:, t, 0, 0:NE], routed[:, t, :], token[:, t:t + 1], None, ALU.mult)
                step(dve.tensor_scalar(tab[:, t, 1, 0:NE], routed[:, t, :], pair_row[:, t:t + 1], None, ALU.mult))
                step(dve.tensor_scalar(tab[:, t, 2, 0:NE], hot[:, t, 0, :], gate[:, t, 0:1], None, ALU.mult))
                for k in range(1, TK):
                    dve.scalar_tensor_tensor(tab[:, t, 1, 0:NE], hot[:, t, k, :], float(k), tab[:, t, 1, 0:NE],
                                             ALU.mult, ALU.add)
                    step(dve.scalar_tensor_tensor(tab[:, t, 2, 0:NE], hot[:, t, k, :], gate[:, t, k:k + 1],
                                                  tab[:, t, 2, 0:NE], ALU.mult, ALU.add))
            for t in range(NT):
                dve.wait_ge(rank_ready, t + 1)
                step(dve.scalar_tensor_tensor(rk[:, t, 0:NE], banks[4 + t][:, 0:NE], 1.0, routed[:, t, :],
                                              ALU.add, ALU.mult))
                step(dve.tensor_scalar(rk[:, t, 0:NE], rk[:, t, 0:NE], -1.0, None, ALU.add))
            dve.wait_ge(count_ready, 1)
            step(dve.tensor_copy(counts[:, :], banks[0][:, 64:64 + NE]))
            step(dve.tensor_reduce(over_f[:, :], counts[:, :], AX.X, ALU.max))
            step(dve.tensor_scalar(over_flag[:, :], over_f[:, :], float(P), None, ALU.is_gt))
            dve.wait_ge(bias_loaded, 16 * 6)
            step(dve.tensor_copy(bias[:, :], bfull[:, :]))
            for part in (1, 2):
                rows = slice(32 * part, 96)
                for r in range(part, 3):
                    rows = slice(32 * r, 32 * r + 32)
                    step(dve.tensor_tensor(bfull[rows, :], bfull[rows, :], bias[rows, :], ALU.subtract))
                    step(dve.tensor_copy(bias[rows, :], bfull[rows, :]))

        @block.tensor
        def _(pe):
            for j in range(2 * NT):
                t, half = j // 2, j % 2
                pe.wait_ge(r_scaled, t + 1)
                if j >= 2:
                    pe.wait_ge(r_T_taken, j - 1)
                for k in range(4):
                    last = pe.transpose(banks[4 + j % 2][:, k * P:(k + 1) * P],
                                        xs[:, t, (4 * half + k) * P:(4 * half + k + 1) * P], ident[:, :])
                last.then_inc(r_T_ready, 1)
            for t in range(NT):
                pe.wait_ge(r_T_taken, 2 * t + 2)
                for k in range(KD):
                    last = pe.matmul(banks[t][:, 0:NE], xn2T[:, k, t * P:(t + 1) * P], wr_sb[:, k, :],
                                     start=(k == 0), stop=(k == KD - 1))
                last.then_inc(route_ready, 1)
            pe.wait_ge(r_consts, 12)
            pe.wait_ge(r_T_taken, 2 * NT)
            for t in range(NT):
                pe.wait_ge(routed_set, t + 1)
                for s in range(t + 1):
                    last = pe.matmul(banks[4 + t][:, 0:NE], before[:, :] if s == t else ones[:, :], routed[:, s, :],
                                     start=(s == 0), stop=(s == t))
                last.then_inc(rank_ready, 1)
            for t in range(NT):
                last = pe.matmul(banks[0][:, 64:64 + NE], ones[:, :], routed[:, t, :], start=(t == 0),
                                 stop=(t == NT - 1))
            last.then_inc(count_ready, 1)


def experts(nc, sem, banks, ring, ident, tab, rk, bias, eq, slot_iota, landed, xn2_rows, pair_rows,
            w_exp1, w_exp2):
    with ExitStack() as ctx:
        def sb(name, shape, dt=F32):
            return ctx.enter_context(nc.sbuf_tensor(name, shape, dt))

        wh = sb("wh", [P, SPLIT, UW], F32R)
        wl = sb("wl", [P, SPLIT, UW], F32R)
        pick = sb("pick", [P, NT, P])
        sel_h = sb("sel_h", [96, P], BF16)
        sel_y = sb("sel_y", [96, P], BF16)
        row_in = sb("row_in", [P, 1], U32)
        row_out = sb("row_out", [P, 1], U32)
        dest = sb("dest", [P, NEP])
        gates = sb("gates", [P, NEP])
        xg = sb("xg", [P, D])
        xh = sb("xh", [P, KD, P], F32R)
        xl = sb("xl", [P, KD, P], F32R)
        hg = sb("hg", [P, DE])
        hu = sb("hu", [P, DE])
        sg = sb("sg", [P, DE])
        ah = sb("ah", [P, KD, P], F32R)
        al = sb("al", [P, KD, P], F32R)
        y = sb("y", [P, D])
        onesb = sb("onesb", [96, P], BF16)
        zero = sb("zero", [P, 1])
        carried = sb("carried", [P, 2])

        def gather(pool):
            return pool.indirect_dma_start(out=xg[:, :], out_offset=None, in_=xn2_rows,
                                           in_offset=bass.IndirectOffsetOnAxis(ap=row_in[:, 0:1], axis=0),
                                           bounds_check=S - 1, oob_is_err=False)

        def scatter(pool):
            return pool.indirect_dma_start(out=pair_rows,
                                           out_offset=bass.IndirectOffsetOnAxis(ap=row_out[:, 0:1], axis=0),
                                           in_=y[:, :], in_offset=None, bounds_check=S * TK - 1, oob_is_err=False)

        def carry_waits(pool, i, signal):
            pool.tensor_tensor(carried[:, i:i + 1], zero[:, :], zero[:, :], ALU.add).then_inc(signal, 1)

        e_consts = sem("e_consts")
        gather_carried, scatter_carried = sem("gather_carried"), sem("scatter_carried")
        pick_set, slots_ready, slots_taken = sem("pick_set"), sem("slots_ready"), sem("slots_taken")
        gathered, scattered = sem("gathered"), sem("scattered")
        xT_ready, xh_set, xl_set = sem("xgT_ready"), sem("xh_set"), sem("xl_set")
        selh_set, sely_set = sem("selh_set"), sem("sely_set")
        wh_set, wl_set, unit_used = sem("wh_set"), sem("wl_set"), sem("unit_used")
        hg_set, hu_set, hgu_set = sem("hg_set"), sem("hu_set"), sem("hgu_set")
        sig_done, act_set = sem("sig_done"), sem("act_set")
        aT_ready, ah_set, al_set = sem("aT_ready"), sem("ah_set"), sem("al_set")
        y_set, row_out_set = sem("y_set"), sem("row_out_set")

        FIRST = KD
        def number(e, i):
            return i if type(e) is int and e == 0 else e * PER_E + (i + FIRST - PER_E)

        def slot(i, turn0, n):
            return (i if turn0 else i + FIRST) % n

        block = ctx.enter_context(nc.Block())

        @block.sync
        def _(sp):
            def load(e, i, src, turn0=False):
                sp.wait_ge(wl_set, number(e, i) + (1 - RAW))
                q = slot(i, turn0, RAW)
                dst = ring[:, q, :]
                if src.shape[0] == P and len(src.shape) == 3:
                    dst = dst.rearrange("p (k n) -> p k n", k=2)
                sp.dma_start(dst, src).then_inc(landed[q], 16)

            def w1_rows(e, k):
                return w_exp1[bass.ds(e, 1), k * P:(k + 1) * P, :].rearrange("a p n -> (a p) n")

            def w2_rows(e, q):
                return w_exp2[bass.ds(e, 1), 2 * q * P:2 * (q + 1) * P, :].rearrange("a (k p) n -> p (a k) n", p=P)

            for k in range(RAW, KD):
                load(0, k, w1_rows(0, k), turn0=True)
            with sp.Fori(1, NE) as e:
                for k in range(KD):
                    load(e, k, w1_rows(e, k))
                for q in range(4):
                    load(e, KD + q, w2_rows(e - 1, q))
            for q in range(4):
                load(NE, q, w2_rows(NE - 1, q))

        @block.gpsimd
        def _(pool):
            pool.memset(xg[:, :], 0.0).then_inc(e_consts, 1)
            pool.memset(onesb[:, :], 1.0).then_inc(e_consts, 1)
            pool.memset(zero[:, :], 0.0).then_inc(e_consts, 1)
            pool.wait_ge(e_consts, 3)
            for e in range(3):
                pool.wait_ge(slots_taken, e + 1)
                if e:
                    pool.wait_ge(xT_ready, 2 * e)
                gather(pool).then_inc(gathered, 16)
            with pool.Fori(1, NE) as e:
                pool.wait_ge(slots_taken, e + 3)
                pool.wait_ge(xT_ready, e * 2 + 4)
                carry_waits(pool, 0, gather_carried)
                gather(pool).then_inc(gathered, 16)
                pool.wait_ge(row_out_set, e)
                pool.wait_ge(y_set, e * 2)
                carry_waits(pool, 1, scatter_carried)
                scatter(pool).then_inc(scattered, 16)
            pool.wait_ge(row_out_set, NE)
            pool.wait_ge(y_set, 2 * NE)
            scatter(pool).then_inc(scattered, 16)
            pool.wait_ge(gathered, 16 * NEP)
            pool.wait_ge(scattered, 16 * NE)

        @block.scalar
        def _(act):
            def split_high(e, i, turn0=False):
                q, w = slot(i, turn0, RAW), slot(i, turn0, SPLIT)
                if turn0:
                    act.wait_ge(landed[q], 16 * (i // RAW + 1))
                    if i >= SPLIT:
                        act.wait_ge(unit_used, i + 1 - SPLIT)
                else:
                    act.wait_ge(landed[q], e * 32 + 16 * ((i + FIRST - PER_E) // RAW + 1))
                    act.wait_ge(unit_used, number(e, i) + (1 - SPLIT))
                act.activation(wh[:, w, :], ring[:, q, :], ACT.Copy).then_inc(wh_set, 1)

            def sigmoid(e):
                act.wait_ge(hg_set, e * 2 + 2)
                act.activation(sg[:, :], hg[:, :], ACT.Sigmoid, scale=ALPHA).then_inc(sig_done, 1)

            def upper_half(dst, half, ready, count, signal):
                act.wait_ge(ready, count)
                act.activation(dst[:, 4 * half:4 * half + 4, :].rearrange("p k q -> p (k q)"), banks[6 + half][:, :],
                               ACT.Copy).then_inc(signal, 1)

            def gated_rows(e):
                for n in range(2):
                    act.activation(y[:, 512 * n:512 * n + 512], banks[4 + n][:, :], ACT.Copy,
                                   scale=gates[:, bass.ds(e, 1)]).then_inc(y_set, 1)

            for i in range(AHEAD):
                split_high(0, i, True)
            for half in range(2):
                upper_half(xh, half, xT_ready, half + 1, xh_set)
            for i in range(AHEAD, KD):
                split_high(0, i, True)
            for i in range(AHEAD):
                split_high(1, i)
            sigmoid(0)
            for half in range(2):
                upper_half(xh, half, xT_ready, half + 3, xh_set)
            with act.Fori(1, NE) as e:
                for half in range(2):
                    upper_half(ah, half, aT_ready, e * 2 + (half - 1), ah_set)
                for i in range(AHEAD, KD + AHEAD):
                    split_high(e, i)
                sigmoid(e)
                split_high(e, KD + AHEAD)
                upper_half(xh, 0, xT_ready, e * 2 + 3, xh_set)
                upper_half(xh, 1, xT_ready, e * 2 + 4, xh_set)
                for i in range(PER_E, PER_E + AHEAD):
                    split_high(e, i)
                act.wait_ge(unit_used, number(e, PER_E))
                act.wait_ge(slots_taken, e + 2)
                act.wait_ge(row_out_set, e)
                gated_rows(e - 1)
            for half in range(2):
                upper_half(ah, half, aT_ready, 2 * NE - 1 + half, ah_set)
            split_high(NE, AHEAD)
            act.wait_ge(unit_used, number(NE, 4))
            act.wait_ge(scattered, 16 * (NE - 1))
            gated_rows(NE - 1)

        @block.vector
        def _(dve):
            def pick_tokens(e):
                for t in range(NT):
                    last = dve.tensor_scalar(pick[:, t, :], slot_iota[:, :], rk[:, t, bass.ds(e, 1)], None,
                                             ALU.is_equal)
                last.then_inc(pick_set, 1)

            def take_slots(e):
                dve.tensor_scalar(dest[:, bass.ds(e, 1)], banks[7][:, 1:2], BIG, None, ALU.add)
                dve.tensor_copy(gates[:, bass.ds(e, 1)], banks[7][:, 2:3])
                dve.tensor_scalar(row_in[:, :], banks[7][:, 0:1], BIG, None, ALU.add).then_inc(slots_taken, 1)

            def split_low(e, i, turn0=False):
                q, w = slot(i, turn0, RAW), slot(i, turn0, SPLIT)
                dve.wait_ge(wh_set, number(e, i) + 1)
                dve.tensor_tensor(wl[:, w, :], ring[:, q, :], wh[:, w, :].bitcast(F32), ALU.subtract
                                  ).then_inc(wl_set, 1)

            def lower_half(dst, high, half, ready, count, signal):
                dve.wait_ge(ready, count)
                part = (slice(None), slice(4 * half, 4 * half + 4), slice(None))
                dve.tensor_tensor(dst[part].rearrange("p k q -> p (k q)"), banks[6 + half][:, :],
                                  high[part].bitcast(F32).rearrange("p k q -> p (k q)"), ALU.subtract
                                  ).then_inc(signal, 1)

            def select(sel, e, signal):
                dve.tensor_scalar(sel[:, :], onesb[:, :], eq[:, bass.ds(e, 1)], None, ALU.mult).then_inc(signal, 1)

            def clip_gate(e, h_ready):
                dve.wait_ge(unit_used, h_ready)
                for n in range(2):
                    dve.tensor_scalar(hg[:, 512 * n:512 * n + 512], banks[n][:, :], LIMIT, None, ALU.min
                                      ).then_inc(hg_set, 1)

            def clip_up():
                for n in range(2):
                    dve.tensor_scalar(hu[:, 512 * n:512 * n + 512], banks[2 + n][:, :], LIMIT, -LIMIT, ALU.min, ALU.max
                                      ).then_inc(hu_set, 1)

            def multiply(e):
                dve.wait_ge(hu_set, e * 2 + 2)
                dve.scalar_tensor_tensor(hu[:, :], hu[:, :], 1.0, hg[:, :], ALU.add, ALU.mult).then_inc(hgu_set, 1)

            def activate(e):
                dve.wait_ge(hgu_set, e + 1)
                dve.wait_ge(sig_done, e + 1)
                dve.tensor_tensor(sg[:, :], hu[:, :], sg[:, :], ALU.mult).then_inc(act_set, 1)

            for i in range(AHEAD):
                split_low(0, i, True)
            dve.wait_ge(e_consts, 3)
            select(sel_h, 0, selh_set)
            select(sel_y, 0, sely_set)
            for e in range(2):
                if e:
                    dve.wait_ge(gathered, 16 * e)
                    dve.wait_ge(slots_ready, e)
                pick_tokens(e)
                dve.wait_ge(slots_ready, e + 1)
                take_slots(e)
            for half in range(2):
                lower_half(xl, xh, half, xh_set, half + 1, xl_set)
            pick_tokens(2)
            for i in range(AHEAD, KD):
                split_low(0, i, True)
            for i in range(AHEAD):
                split_low(1, i)
            clip_gate(0, KD)
            clip_up()
            dve.wait_ge(gathered, 32)
            dve.wait_ge(slots_ready, 3)
            take_slots(2)
            multiply(0)
            activate(0)
            select(sel_h, 1, selh_set)
            for half in range(2):
                lower_half(xl, xh, half, xh_set, half + 3, xl_set)
            def turn(e, first=False):
                for half in range(2):
                    lower_half(al, ah, half, ah_set, e * 2 + (half - 1), al_set)
                split_low(e, AHEAD)
                pick_tokens(e + 2)
                for i in range(AHEAD + 1, KD + AHEAD):
                    split_low(e, i)
                    if i == AHEAD + 3:
                        if not first:
                            dve.wait_ge(gather_carried, e - 1)
                            dve.wait_ge(scatter_carried, e - 1)
                            dve.wait_ge(scattered, e * 16 - 16)
                        dve.tensor_copy(row_out[:, :], dest[:, bass.ds(e - 1, 1)]).then_inc(row_out_set, 1)
                clip_gate(e, number(e, KD))
                clip_up()
                dve.wait_ge(gathered, e * 16 + 32)
                dve.wait_ge(slots_ready, e + 3)
                take_slots(e + 2)
                multiply(e)
                split_low(e, KD + AHEAD)
                activate(e)
                select(sel_h, e + 1, selh_set)
                for half in range(2):
                    lower_half(xl, xh, half, xh_set, e * 2 + (half + 3), xl_set)
                for i in range(PER_E, PER_E + AHEAD):
                    split_low(e, i)
                dve.wait_ge(unit_used, number(e, PER_E))
                select(sel_y, e, sely_set)

            turn(1, first=True)
            with dve.Fori(2, NE) as e:
                turn(e)
            for half in range(2):
                lower_half(al, ah, half, ah_set, 2 * NE - 1 + half, al_set)
            split_low(NE, AHEAD)
            dve.wait_ge(scattered, 16 * (NE - 1))
            dve.tensor_copy(row_out[:, :], dest[:, NE - 1:NE]).then_inc(row_out_set, 1)

        @block.tensor
        def _(pe):
            def slots(e):
                pe.wait_ge(pick_set, e + 1)
                for t in range(NT):
                    last = pe.matmul(banks[7][:, 0:3], pick[:, t, :],
                                     tab[:, t, :, bass.ds(e, 1)].rearrange("p a b -> p (a b)"),
                                     start=(t == 0), stop=(t == NT - 1))
                last.then_inc(slots_ready, 1)

            def transpose_half(src, half, signal):
                for k in range(4):
                    last = pe.transpose(banks[6 + half][:, k * P:(k + 1) * P],
                                        src[:, (4 * half + k) * P:(4 * half + k + 1) * P], ident[:, :])
                last.then_inc(signal, 1)

            def start_with_bias(first, count, sel, at):
                for n in range(count):
                    pe.matmul(banks[first + n][:, :], sel[:, :], bias[:, at + 512 * n:at + 512 * n + 512],
                              start=True, stop=False)

            def three_products(bank, high, low, w, cols, stop):
                pe.matmul(bank, high, wh[:, w, cols], start=False, stop=False)
                pe.matmul(bank, high, wl[:, w, cols], start=False, stop=False)
                return pe.matmul(bank, low, wh[:, w, cols], start=False, stop=stop)

            def products_h(e, turn0=False):
                pe.wait_ge(selh_set, e + 1)
                start_with_bias(0, 4, sel_h, 0)
                pe.wait_ge(xl_set, e * 2 + 2)
                for k in range(KD):
                    pe.wait_ge(wl_set, number(e, k) + 1)
                    for n in range(4):
                        last = three_products(banks[n][:, :], xh[:, k, :], xl[:, k, :], slot(k, turn0, SPLIT),
                                              slice(512 * n, 512 * n + 512), k == KD - 1)
                    last.then_inc(unit_used, 1)

            def products_y(e, first, qs):
                for q in qs:
                    if q == 0:
                        pe.wait_ge(sely_set, e)
                        start_with_bias(4, 2, sel_y, 2 * DE)
                        pe.wait_ge(al_set, e * 2)
                    pe.wait_ge(wl_set, number(e, first + q) + 1)
                    for k in (2 * q, 2 * q + 1):
                        for n in range(2):
                            at = 1024 * (k % 2) + 512 * n
                            last = three_products(banks[4 + n][:, :], ah[:, k, :], al[:, k, :],
                                                  slot(first + q, False, SPLIT), slice(at, at + 512), k == KD - 1)
                    last.then_inc(unit_used, 1)

            slots(0)
            pe.wait_ge(slots_taken, 1)
            slots(1)
            pe.wait_ge(gathered, 16)
            transpose_half(xg, 0, xT_ready)
            pe.wait_ge(slots_taken, 2)
            transpose_half(xg, 1, xT_ready)
            products_h(0, True)
            slots(2)
            pe.wait_ge(gathered, 32)
            transpose_half(xg, 0, xT_ready)
            pe.wait_ge(slots_taken, 3)
            transpose_half(xg, 1, xT_ready)
            pe.wait_ge(act_set, 1)
            pe.wait_ge(xl_set, 4)
            for half in range(2):
                transpose_half(sg, half, aT_ready)
            with pe.Fori(1, NE) as e:
                pe.wait_ge(hu_set, e * 2)
                products_h(e)
                pe.wait_ge(al_set, e * 2)
                slots(e + 2)
                pe.wait_ge(gathered, e * 16 + 32)
                transpose_half(xg, 0, xT_ready)
                pe.wait_ge(row_out_set, e)
                products_y(e, KD, range(0, 2))
                pe.wait_ge(slots_taken, e + 3)
                transpose_half(xg, 1, xT_ready)
                products_y(e, KD, range(2, 4))
                pe.wait_ge(act_set, e + 1)
                pe.wait_ge(xl_set, e * 2 + 4)
                for half in range(2):
                    transpose_half(sg, half, aT_ready)
            pe.wait_ge(y_set, 2 * NE - 2)
            products_y(NE, 0, range(4))


def further_blocks(nc, sem, banks, ring, ident, tab, rk, bias, eq, slot_iota, counts, xn2_rows, pair_rows, w_exp1, w_exp2):
    with ExitStack() as ctx:
        def sb(name, shape, dt=F32):
            return ctx.enter_context(nc.sbuf_tensor(name, shape, dt))

        others = sb("f_units", [P, PER_E - RAW, UW])

        def unit(u):
            return ring[:, u, :] if u < RAW else others[:, u - RAW, :]

        pick = sb("f_pick", [P, NT, P])
        rank_here = sb("f_rank", [P, NT])
        sel = sb("f_sel", [96, P], BF16)
        row_in = sb("f_row_in", [P, 1], U32)
        row_out = sb("f_row_out", [P, 1], U32)
        gate = sb("f_gate", [P, 1])
        xg = sb("f_xg", [P, D])
        xgT = sb("f_xgT", [P, KD, P])
        hg = sb("f_hg", [P, DE])
        hu = sb("f_hu", [P, DE])
        sg = sb("f_sg", [P, DE])
        act_sb = sb("f_act", [P, DE])
        actT = sb("f_actT", [P, KD, P])
        y = sb("f_y", [P, D])
        onesb = sb("f_onesb", [96, P], BF16)
        more = sb("f_more", [P, 3, NE])
        extra = sb("f_extra", [P, NE])
        upto = sb("f_upto", [P, NE])
        upto2 = sb("f_upto2", [P, NE])
        done = sb("f_done", [P, OVER, NE])
        whose = sb("f_whose", [P, OVER])
        behind = sb("f_behind", [P, OVER])
        first = sb("f_first", [P, OVER])
        number = sb("f_number", [P, OVER])
        whose_i = sb("f_whose_i", [P, OVER], I32)

        f_consts, f_table = sem("f_consts"), sem("f_table")
        f_landed, f_step = sem("f_landed"), sem("f_step")
        f_picked, f_slots, f_rows, f_gathered = sem("f_picked"), sem("f_slots"), sem("f_rows"), sem("f_gathered")
        f_T, f_T_taken = sem("f_T"), sem("f_T_taken")
        f_h, f_hg, f_sig = sem("f_h"), sem("f_hg_set"), sem("f_sig")
        f_act_set, f_y_ready = sem("f_act_set"), sem("f_y_ready")
        f_y_set, f_scattered = sem("f_y_set"), sem("f_scattered")
        f_carried = sem("f_carried")
        zero = sb("f_zero", [P, 1])
        carried = sb("f_carry", [P, 2])
        block = ctx.enter_context(nc.Block())

        def expert_of(engine, j):
            return engine.value_load(whose_i[0:1, bass.ds(j, 1)], min_val=0, max_val=NE - 1)

        @block.sync
        def _(sp):
            sp.wait_ge(f_table, 1)
            with sp.Fori(0, OVER) as j:
                e = expert_of(sp, j)
                sp.wait_ge(f_picked, j + 1)
                for k in range(KD):
                    sp.dma_start(unit(k), w_exp1[bass.ds(e, 1), k * P:(k + 1) * P, :]
                                 .rearrange("a p n -> (a p) n")).then_inc(f_landed, 16)
                for q in range(4):
                    sp.dma_start(unit(8 + q).rearrange("p (k n) -> p k n", k=2), w_exp2[bass.ds(e, 1), 2 * q * P:2 * (q + 1) * P, :]
                                 .rearrange("a (k p) n -> p (a k) n", p=P)).then_inc(f_landed, 16)

        @block.gpsimd
        def _(pool):
            pool.memset(xg[:, :], 0.0).then_inc(f_consts, 1)
            pool.memset(onesb[:, :], 1.0).then_inc(f_consts, 1)
            pool.memset(zero[:, :], 0.0).then_inc(f_consts, 1)
            pool.iota(number[:, :], pattern=[[1, OVER]], base=0, channel_multiplier=0,
                      allow_small_or_imprecise_dtypes=True).then_inc(f_consts, 1)
            pool.wait_ge(f_consts, 4)
            with pool.Fori(0, OVER) as j:
                pool.wait_ge(f_rows, j + 1)
                pool.tensor_tensor(carried[:, 0:1], zero[:, :], zero[:, :], ALU.add).then_inc(f_carried, 1)
                pool.indirect_dma_start(out=xg[:, :], out_offset=None, in_=xn2_rows,
                                        in_offset=bass.IndirectOffsetOnAxis(ap=row_in[:, 0:1], axis=0),
                                        bounds_check=S - 1, oob_is_err=False).then_inc(f_gathered, 16)
                pool.wait_ge(f_y_set, j * 2 + 2)
                pool.tensor_tensor(carried[:, 1:2], zero[:, :], zero[:, :], ALU.add).then_inc(f_carried, 1)
                pool.indirect_dma_start(out=pair_rows,
                                        out_offset=bass.IndirectOffsetOnAxis(ap=row_out[:, 0:1], axis=0),
                                        in_=y[:, :], in_offset=None, bounds_check=S * TK - 1, oob_is_err=False
                                        ).then_inc(f_scattered, 16)
            pool.wait_ge(f_gathered, 16 * OVER)
            pool.wait_ge(f_scattered, 16 * OVER)

        @block.scalar
        def _(act):
            with act.Fori(0, OVER) as j:
                act.wait_ge(f_hg, j * 2 + 2)
                act.activation(sg[:, :], hg[:, :], ACT.Sigmoid, scale=ALPHA).then_inc(f_sig, 1)
                for half in range(2):
                    act.wait_ge(f_T, j * 4 + (half + 3))
                    act.activation(actT[:, 4 * half:4 * half + 4, :].rearrange("p k q -> p (k q)"),
                                   banks[6 + half][:, :], ACT.Copy).then_inc(f_T_taken, 1)
                act.wait_ge(f_y_ready, j + 1)
                for n in range(2):
                    act.activation(y[:, 512 * n:512 * n + 512], banks[4 + n][:, :], ACT.Copy, scale=gate[:, 0:1]
                                   ).then_inc(f_y_set, 1)

        @block.vector
        def _(dve):
            step = Steps(dve, f_step)
            for c in range(3):
                step(dve.tensor_scalar(more[:, c, :], counts[:, :], float(P * (c + 1)), None, ALU.is_gt))
            step(dve.tensor_reduce(extra[:, :], more[:, :, :].rearrange("p c e -> p e c"), AX.X, ALU.add))
            step(dve.tensor_copy(upto[:, :], extra[:, :]))
            here, there = upto, upto2
            for shift in (1, 2, 4, 8, 16):
                step(dve.tensor_copy(there[:, 0:shift], here[:, 0:shift]))
                step(dve.tensor_tensor(there[:, shift:NE], here[:, shift:NE], here[:, 0:NE - shift], ALU.add))
                here, there = there, here
            dve.wait_ge(f_consts, 4)
            for j in range(OVER):
                step(dve.tensor_scalar(done[:, j, :], here[:, :], float(j), None, ALU.is_le))
            step(dve.tensor_reduce(whose[:, :], done[:, :, :], AX.X, ALU.add))
            for j in range(OVER):
                step(dve.tensor_tensor(done[:, j, :], done[:, j, :], extra[:, :], ALU.mult))
            step(dve.tensor_reduce(behind[:, :], done[:, :, :], AX.X, ALU.add))
            step(dve.tensor_tensor(first[:, :], number[:, :], behind[:, :], ALU.subtract))
            step(dve.tensor_scalar(first[:, :], first[:, :], 1.0, float(P), ALU.add, ALU.mult))
            step(dve.tensor_scalar(behind[:, :], whose[:, :], float(NE), BIG, ALU.is_ge, ALU.mult))
            step(dve.tensor_tensor(first[:, :], first[:, :], behind[:, :], ALU.add))
            step(dve.tensor_scalar(whose[:, :], whose[:, :], float(NE - 1), None, ALU.min))
            dve.tensor_copy(whose_i[:, :], whose[:, :]).then_inc(f_table, 1)
            dve.wait_ge(f_table, 1)
            with dve.Fori(0, OVER) as j:
                step.enter(j, 5)
                e = expert_of(dve, j)
                step(dve.tensor_scalar(rank_here[:, :], rk[:, :, bass.ds(e, 1)].rearrange("p t a -> p (t a)"),
                                       first[:, bass.ds(j, 1)], None, ALU.subtract))
                for t in range(NT):
                    last = dve.tensor_scalar(pick[:, t, :], slot_iota[:, :], rank_here[:, t:t + 1], None,
                                             ALU.is_equal)
                step(last)
                dve.tensor_scalar(sel[:, :], onesb[:, :], eq[:, bass.ds(e, 1)], None, ALU.mult).then_inc(f_picked, 1)
                dve.wait_ge(f_slots, j + 1)
                dve.tensor_copy(gate[:, :], banks[7][:, 2:3])
                dve.tensor_scalar(row_out[:, :], banks[7][:, 1:2], BIG, None, ALU.add)
                dve.tensor_scalar(row_in[:, :], banks[7][:, 0:1], BIG, None, ALU.add).then_inc(f_rows, 1)
                for half in range(2):
                    dve.wait_ge(f_T, j * 4 + (half + 1))
                    dve.tensor_copy(xgT[:, 4 * half:4 * half + 4, :].rearrange("p k q -> p (k q)"),
                                    banks[6 + half][:, :]).then_inc(f_T_taken, 1)
                dve.wait_ge(f_h, j + 1)
                for n in range(2):
                    dve.tensor_scalar(hg[:, 512 * n:512 * n + 512], banks[n][:, :], LIMIT, None, ALU.min
                                      ).then_inc(f_hg, 1)
                for n in range(2):
                    step(dve.tensor_scalar(hu[:, 512 * n:512 * n + 512], banks[2 + n][:, :], LIMIT, -LIMIT, ALU.min,
                                           ALU.max))
                step(dve.scalar_tensor_tensor(hu[:, :], hu[:, :], 1.0, hg[:, :], ALU.add, ALU.mult))
                dve.wait_ge(f_sig, j + 1)
                dve.tensor_tensor(act_sb[:, :], hu[:, :], sg[:, :], ALU.mult).then_inc(f_act_set, 1)
                dve.wait_ge(f_scattered, j * 16 + 16)
                dve.wait_ge(f_carried, j * 2 + 2)
                step.leave(OVER)

        @block.tensor
        def _(pe):
            pe.wait_ge(f_table, 1)
            with pe.Fori(0, OVER) as j:
                e = expert_of(pe, j)
                pe.wait_ge(f_picked, j + 1)
                for t in range(NT):
                    last = pe.matmul(banks[7][:, 0:3], pick[:, t, :],
                                     tab[:, t, :, bass.ds(e, 1)].rearrange("p a b -> p (a b)"),
                                     start=(t == 0), stop=(t == NT - 1))
                last.then_inc(f_slots, 1)
                pe.wait_ge(f_rows, j + 1)
                pe.wait_ge(f_gathered, j * 16 + 16)
                for half in range(2):
                    for k in range(4):
                        last = pe.transpose(banks[6 + half][:, k * P:(k + 1) * P],
                                            xg[:, (4 * half + k) * P:(4 * half + k + 1) * P], ident[:, :])
                    last.then_inc(f_T, 1)
                pe.wait_ge(f_T_taken, j * 4 + 2)
                pe.wait_ge(f_landed, j * (16 * PER_E) + 16 * PER_E)
                for n in range(4):
                    pe.matmul(banks[n][:, :], sel[:, :], bias[:, 512 * n:512 * n + 512], start=True, stop=False)
                    for k in range(KD):
                        last = pe.matmul(banks[n][:, :], xgT[:, k, :], unit(k)[:, 512 * n:512 * n + 512],
                                         start=False, stop=(k == KD - 1))
                last.then_inc(f_h, 1)
                pe.wait_ge(f_act_set, j + 1)
                for half in range(2):
                    for k in range(4):
                        last = pe.transpose(banks[6 + half][:, k * P:(k + 1) * P],
                                            act_sb[:, (4 * half + k) * P:(4 * half + k + 1) * P], ident[:, :])
                    last.then_inc(f_T, 1)
                pe.wait_ge(f_T_taken, j * 4 + 4)
                for n in range(2):
                    pe.matmul(banks[4 + n][:, :], sel[:, :], bias[:, 2 * DE + 512 * n:2 * DE + 512 * n + 512],
                              start=True, stop=False)
                    for k in range(KD):
                        last = pe.matmul(banks[4 + n][:, :], actT[:, k, :],
                                         unit(8 + k // 2)[:, 1024 * (k % 2) + 512 * n:1024 * (k % 2) + 512 * n + 512],
                                         start=False, stop=(k == KD - 1))
                last.then_inc(f_y_ready, 1)


def combine(nc, sem, x_sb, pair_rows, out_rows):
    pairs_loaded = [sem(f"pairs_loaded{t}") for t in range(NT)]
    summed, x_summed, out_stored = sem("summed"), sem("x_summed"), sem("out_stored")
    src = pair_rows.rearrange("(t p k) d -> t p (k d)", p=P, k=TK)
    with nc.sbuf_tensor("pairs", [P, NT, TK * D], F32) as pairs, nc.Block() as block:
        @block.sync
        def _(sp):
            for t in range(NT):
                sp.dma_start(pairs[:, t, :], src[t]).then_inc(pairs_loaded[t], 16)
            for t in range(NT):
                sp.wait_ge(x_summed, t + 1)
                sp.dma_start(out_rows[:, t, :], x_sb[:, t, :]).then_inc(out_stored, 16)
            sp.wait_ge(out_stored, 16 * NT)

        @block.vector
        def _(dve):
            for t in range(NT):
                dve.wait_ge(pairs_loaded[t], 16)
                p = pairs[:, t, :]
                dve.tensor_tensor(p[:, 0:2 * D], p[:, 0:2 * D], p[:, 2 * D:4 * D], ALU.add).then_inc(summed, 1)
                dve.wait_ge(summed, 2 * t + 1)
                dve.tensor_tensor(p[:, 0:D], p[:, 0:D], p[:, D:2 * D], ALU.add).then_inc(summed, 1)
                dve.wait_ge(summed, 2 * t + 2)
                dve.tensor_tensor(x_sb[:, t, :], x_sb[:, t, :], p[:, 0:D], ALU.add).then_inc(x_summed, 1)


_INS = ['x', 'norm1_g', 'w_in', 'q_lat_g', 'w_uq', 'q_norm_g', 'kv_norm_g', 'w_uv', 'w_q_idx', 'k_idx_g',
        'gmlp_v_g', 'w_spatial', 'b_spatial', 'w_proj_a', 'w_proj_b', 'w_out', 'norm2_g',
        'w_router', 'b_router', 'w_exp1', 'b_exp1', 'w_exp2', 'b_exp2']


def kernel(**inputs):
    import numpy as np
    import concourse.bacc as bacc
    from concourse.bass_utils import run_bass_kernel_spmd

    nc = bacc.Bacc("TRN2", target_bir_lowering=False, num_devices=1)
    arrays, args = {}, []
    for name in _INS:
        a = np.ascontiguousarray(inputs[name])
        arrays[f"in_{name}"] = a
        args.append(nc.dram_tensor(f"in_{name}", a.shape, mybir.dt.from_np(a.dtype), kind="ExternalInput").ap())
    shape = inputs["x"].shape
    args.append(nc.dram_tensor("out_y", shape, F32, kind="ExternalOutput").ap())
    build(nc, *args)
    got = run_bass_kernel_spmd(nc, [arrays], core_ids=[0])
    return got.results[0]["out_y"]
```

```python
from contextlib import ExitStack

import concourse.bass as bass
from concourse import mybir

P = 128
D = 1024
S = 512
NT = S // P
KD = D // P
G = 4
H = 8
QR = 256
KVR = 128
HV = 64
IH = 4
ID = 64
TOPK = 128
NE = 32
TK = 4
DE = 1024
LIMIT = 7.0
ALPHA = 1.702
EPS = 1e-6
OFF_U, OFF_V, OFF_LAT = 0, 512, 1024
LAT = QR + KVR + ID + IH
C_KV, C_KI, C_WI = QR, QR + KVR, QR + KVR + ID
OFF_GATE = OFF_LAT + LAT
NEG = -1.0e30
TAKEN = -3.0e38
TAKEN_BELOW = -2.0e38
BIG = 4096.0
UW = 2048
PER_E = 12
RAW = 6
SPLIT = 4
AHEAD = SPLIT - 1
NEP = NE + 2
OVER = 15

F32 = mybir.dt.float32
F32R = mybir.dt.float32r
BF16 = mybir.dt.bfloat16
I32 = mybir.dt.int32
U32 = mybir.dt.uint32
ALU = mybir.AluOpType
ACT = mybir.ActivationFunctionType
AX = mybir.AxisListType


class Steps:

    def __init__(self, engine, semaphore, already=0):
        self.engine, self.semaphore, self.n = engine, semaphore, already
        self.past = None

    def __call__(self, instruction):
        self.n += 1
        instruction.then_inc(self.semaphore, 1)
        self.engine.wait_ge(self.semaphore, self.n if self.past is None else self.past + self.n)

    def enter(self, turns, per_turn):
        self.first, self.per_turn, self.past = self.n, per_turn, turns * per_turn

    def leave(self, count):
        assert self.n - self.first == self.per_turn, (self.n - self.first, self.per_turn)
        self.n = self.first + count * self.per_turn
        self.past = None


def twins(stack, nc, name, shape):
    with nc.sbuf_tensor(name + "_r", shape, F32R) as rounded:
        pass
    return stack.enter_context(nc.sbuf_tensor(name, shape, F32)), rounded


def build(nc, x, norm1_g, w_in, q_lat_g, w_uq, q_norm_g, kv_norm_g, w_uv, w_q_idx, k_idx_g,
          gmlp_v_g, w_spatial, b_spatial, w_proj_a, w_proj_b, w_out, norm2_g,
          w_router, b_router, w_exp1, b_exp1, w_exp2, b_exp2, out):
    xn2_rows = nc.dram_tensor("xn2_rows", (S, D), F32, kind="Internal").ap()
    pair_rows = nc.dram_tensor("pair_rows", (S * TK, D), F32, kind="Internal").ap()
    x_rows = x.rearrange("a (t p) d -> p (a t) d", p=P)
    out_rows = out.rearrange("a (t p) d -> p (a t) d", p=P)

    with ExitStack() as whole:
        def keep(name, shape, dt=F32):
            return whole.enter_context(nc.sbuf_tensor(name, shape, dt))

        def sem(name):
            return whole.enter_context(nc.semaphore(name))

        banks = [whole.enter_context(nc.psum_tensor(f"bank{i}", [P, 512], F32)) for i in range(8)]
        ring, ring_low = twins(whole, nc, "ring", [P, RAW, UW])
        x_sb = keep("x_sb", [P, NT, D])
        ident = keep("ident", [P, P])
        ones = keep("ones", [P, P])
        cols = keep("cols", [P, 21])
        wr_sb = keep("wr_sb", [P, KD, NE])
        br_sb = keep("br_sb", [P, NE])
        over_flag = keep("over_flag", [P, 1], I32)
        rows_sb = keep("rows_sb", [P, NT, D])
        gain2 = keep("gain2", [P, D])
        bias_mem = keep("bias_mem", [P, (2 * DE + D) // 2])
        table_mem = keep("table_mem", [P, NT * 4 * NEP + NEP + 2 * P + 2 * NE + 2 * NT])
        r_ss = keep("r_ss", [P, NT])
        tables = {}
        at = 0
        for name, n in (("tab", NT * 3 * NEP), ("rk", NT * NEP), ("eq", NEP), ("slot_iota", P), ("before", P),
                        ("counts", NE), ("e_iota", NE), ("token", NT), ("pair_row", NT)):
            tables[name] = table_mem[:, at:at + n]
            at += n
        tab = tables["tab"].rearrange("p (t c e) -> p t c e", t=NT, c=3)
        rk = tables["rk"].rearrange("p (t e) -> p t e", t=NT)
        bias = bias_mem[0:96, :].bitcast(BF16)
        eq = tables["eq"][0:96, :]
        slot_iota, counts = tables["slot_iota"], tables["counts"]
        rows_stored = sem("rows_stored")
        landed = [sem(f"landed{j}") for j in range(RAW)]
        N1, N2, QL, QN, VG, KI = 0, 8, 16, 18, 19, 20

        mixers(nc, sem, banks, ring, ring_low, x_sb, ident, ones, cols, wr_sb, br_sb, landed, (N1, N2, QL, QN, VG, KI),
               w_exp1, x_rows, norm1_g, w_in, q_lat_g, w_uq, q_norm_g, kv_norm_g, w_uv,
               w_q_idx, k_idx_g, gmlp_v_g, w_spatial, b_spatial, w_proj_a, w_proj_b, w_out, norm2_g,
               w_router, b_router, rows_sb, gain2, bias_mem, bias, table_mem, tables, tab, rk, r_ss, xn2_rows,
               rows_stored, b_exp1, b_exp2)

        with ExitStack() as split:
            wh = split.enter_context(nc.sbuf_tensor("wh", [P, SPLIT, UW], F32R))
            wl = split.enter_context(nc.sbuf_tensor("wl", [P, SPLIT, UW], F32R))
            xg = split.enter_context(nc.sbuf_tensor("xg", [P, D], F32))
            onesb = split.enter_context(nc.sbuf_tensor("onesb", [96, P], BF16))
            zero = split.enter_context(nc.sbuf_tensor("zero", [P, 1], F32))
            wh_set, wl_set = sem("wh_set"), sem("wl_set")
            routing(nc, sem, banks, ring, wh, wl, landed, wh_set, wl_set, xg, onesb, zero, ones, br_sb, tables,
                    tab, rk, counts, over_flag, rows_stored)
            experts(nc, sem, banks, ring, wh, wl, wh_set, wl_set, xg, onesb, zero, ident, tab, rk, bias, eq, slot_iota, landed,
                    xn2_rows, pair_rows, w_exp1, w_exp2)
        beyond = nc.values_load(over_flag[0:1, 0:1], min_val=0, max_val=1)
        with nc.If(beyond > 0):
            further_blocks(nc, sem, banks, ring, ident, tab, rk, bias, eq, slot_iota, counts,
                           xn2_rows, pair_rows, w_exp1, w_exp2)
        combine(nc, sem, x_sb, pair_rows, out_rows)


def mixers(nc, sem, banks, ring, ring_low, x_sb, ident, ones, cols, wr_sb, br_sb, landed, col_of,
           w_exp1, x_rows, norm1_g, w_in, q_lat_g, w_uq, q_norm_g, kv_norm_g, w_uv,
           w_q_idx, k_idx_g, gmlp_v_g, w_spatial, b_spatial, w_proj_a, w_proj_b, w_out, norm2_g,
           w_router, b_router, rows_sb, gain2, bias_mem, bias, table_mem, tables, tab, rk, r_ss, xn2_rows,
           rows_stored, b_exp1, b_exp2):
    N1, N2, QL, QN, VG, KI = col_of
    with ExitStack() as ctx:
        def sb(name, shape, dt=F32):
            return ctx.enter_context(nc.sbuf_tensor(name, shape, dt))

        early_w, early_w_high = twins(ctx, nc, "early_w", [P, 2, UW])
        xnT, xnT_low = twins(ctx, nc, "xnT", [P, KD, S])
        oT, xnT_high = twins(ctx, nc, "oT", [P, KD, S])
        qT, qT_r = twins(ctx, nc, "qT", [P, H, S])
        gaT, gaT_r = twins(ctx, nc, "gaT", [P, KD, S])
        uT, ya_low = twins(ctx, nc, "uT", [P, G, S])
        v_sb, v_sb_r = twins(ctx, nc, "v_sb", [P, NT, S])
        lat, lat_r = twins(ctx, nc, "lat", [P, 2048])
        kv = sb("kv", [P, NT, KVR])
        wuv = sb("wuv", [P, H, P])
        ss = sb("ss", [P, 48])
        widx = sb("widx", [P, NT, IH])
        top8 = sb("top8", [P, 8])
        mx = sb("mx", [P, NT, H])
        den = sb("den", [P, NT, H])
        qs = sb("qs", [P, NT, H])

        gbT = rows_sb[:, :, :].rearrange("p a (b n) -> p (a b) n", b=2)
        cqT = gain2[:, :].rearrange("p (a n) -> p a n", a=2)
        bspat = bias_mem[:, 0:512].rearrange("p (g n) -> p g n", g=G)
        wsT = bias_mem[:, 512:1024].rearrange("p (g n) -> p g n", g=G)
        kvT = bias_mem[:, 1024:1536]
        kidxT = table_mem[0:ID, 0:S]
        kvg = table_mem[:, S:S + KVR]
        vecs = table_mem[0:21, S + KVR:S + KVR + P]
        lat_sb = lat[:, 0:NT * LAT].rearrange("p (t n) -> p t n", t=NT)
        qidxT = gbT[0:ID, 0:4, :]
        relu = gbT[:, 4:8, :]
        pT = x_sb[:, 0:2, :].rearrange("p a (b n) -> p (a b) n", b=2)
        mask = x_sb[:, 2:4, :].rearrange("p a (b n) -> p (a b) n", b=2)
        probs = [v_sb[:, :, :], lat[:, :].rearrange("p (h n) -> p h n", h=4)]
        xn2T = oT
        ya_high = xnT_high[:, 0:G, :]
        inv_diag = [early_w[:, 1, 1024 + 512 * i:1536 + 512 * i].rearrange("p (h n) -> p h n", h=4) for i in range(2)]
        bfull = early_w[0:96, :, :].rearrange("p a b -> p (a b)")[:, 0:2 * DE + D]
        ybT = uT

        def chunk(u, n):
            return ring[:, u:u + 2, :].rearrange("p a b -> p (a b)")[:, 0:n]

        wuq = early_w[:, 0, :].rearrange("p (k n) -> p k n", k=2)
        wqi = early_w[:, 1, 0:512].rearrange("p (k n) -> p k n", k=2)
        wsp = early_w[:, 1, 512:1024].rearrange("p (g n) -> p g n", g=G)
        qsq = early_w[:, 1, 1024:2048].rearrange("p (a n) -> p a n", a=2)
        w_lat = chunk(0, KD * LAT).rearrange("p (k n) -> p k n", k=KD)
        w_v = chunk(2, KD * 512).rearrange("p (k n) -> p k n", k=KD)
        w_u = chunk(4, KD * 512).rearrange("p (k n) -> p k n", k=KD)
        w_gate = [chunk(u, KD * 512).rearrange("p (k n) -> p k n", k=KD) for u in (0, 2, 4, 0)]
        wpa = chunk(2, G * D).rearrange("p (k n) -> p k n", k=G)
        wpb = chunk(4, G * D).rearrange("p (k n) -> p k n", k=G)
        wout = ring[:, 0:4, :].rearrange("p a (b n) -> p (a b) n", b=2)

        def raw_unit(s):
            return ring[:, (s + 2) % RAW, :]

        def high_unit(s):
            if s < 2:
                return gaT_r[:, 4 * s:4 * s + 4, :].rearrange("p a b -> p (a b)")
            return early_w_high[:, s % 2, :]

        def low_unit(s):
            return ring_low[:, (s + 2) % RAW, :]

        merged_high, merged_low = xnT_low, gaT_r
        out_high = [qT_r[:, 0:4, :].rearrange("p a b -> p (a b)"), qT_r[:, 4:8, :].rearrange("p a b -> p (a b)"),
                    v_sb_r[:, :, :].rearrange("p a b -> p (a b)"), lat_r[:, :]]

        def in_cols(c, n):
            return w_in[:, c:c + n].rearrange("(k p) n -> p k n", p=P)

        x_then_gate_w = [sem(f"x_then_gate_w{i}") for i in range(4)]
        vecs_loaded = sem("vecs_loaded")
        lat_w_loaded = sem("lat_w_loaded")
        qw_loaded = sem("qw_loaded")
        first_loaded = sem("first_loaded")
        small_loaded = sem("small_loaded")
        v_w_loaded = sem("v_w_loaded")
        u_w_loaded = sem("u_w_loaded")
        pa_loaded = sem("pa_loaded")
        pb_loaded = sem("pb_loaded")
        out_w_loaded = sem("out_w_loaded")
        x_again = sem("x_again")
        consts_set = sem("consts_set")
        vecs_zeroed = sem("vecs_zeroed")
        wuv_zeroed = sem("wuv_zeroed")
        masked = sem("masked")
        colsT_ready, cols_set = sem("colsT_ready"), sem("cols_set")
        x_squared, x_root, x_scaled = sem("x_squared"), sem("x_root"), sem("x_scaled")
        xT_ready, xT_taken = sem("xT_ready"), sem("xT_taken")
        lat_ready, lat_copied = sem("lat_ready"), sem("lat_copied")
        lat_squared, lat_root, lat_scaled = sem("lat_squared"), sem("lat_root"), sem("lat_scaled")
        latT_ready, latT_taken = sem("latT_ready"), sem("latT_taken")
        qidx_ready, qidx_copied = sem("qidx_ready"), sem("qidx_copied")
        logit_ready, relu_done, score_done = sem("logit_ready"), sem("relu_done"), sem("score_done")
        q_ready, q_copied, q_squared = sem("q_ready"), sem("q_copied"), sem("q_squared")
        qss_ready, qss_copied, q_root, q_scale_set = (sem("qss_ready"), sem("qss_copied"), sem("q_root"),
                                                      sem("q_scale_set"))
        wsT_ready, wsT_copied = sem("wsT_ready"), sem("wsT_copied")
        v_ready, v_gelu, v_squared, v_root, v_scaled = (
            sem("v_ready"), sem("v_gelu"), sem("v_squared"), sem("v_root"), sem("v_scaled"))
        u_ready, u_gelu = sem("u_ready"), sem("u_gelu")
        gate_ready, gate_taken = sem("gate_ready"), sem("gate_taken")
        mix_ready, ya_set = sem("mix_ready"), sem("ya_set")
        pa_ready, pa_taken = sem("pa_ready"), sem("pa_taken")
        mask_set = sem("mask_set")
        s_ready, s_masked, bias_set, exp_done = sem("s_ready"), sem("s_masked"), sem("bias_set"), sem("exp_done")
        inv_set = sem("inv_set")
        pT_ready, pT_taken = sem("pT_ready"), sem("pT_taken")
        o_ready, o_taken = sem("o_ready"), sem("o_taken")
        yb_ready, yb_taken = sem("yb_ready"), sem("yb_taken")
        pb_ready, merged = sem("pb_ready"), sem("merged")
        x2_ready, x2_taken = sem("x2_ready"), sem("x2_taken")
        r_squared, r_root, r_scaled = sem("r_squared"), sem("r_root"), sem("r_scaled")
        r_T_ready, r_T_taken, route_ready = sem("r_T_ready"), sem("r_T_taken"), sem("route_ready")
        pool_step = sem("pool_step")
        x_high_set, x_low_set, act_high_set, act_low_set = (sem("x_high_set"), sem("x_low_set"), sem("act_high_set"),
                                                          sem("act_low_set"))
        high_set, low_set, first_used = sem("w_high_set"), sem("w_low_set"), sem("first_used")
        dve_step = sem("dve_step")

        QBLOCKS = [3, 2, 1]
        HALVES = [(b, g) for b in range(NT) for g in range(2)]
        PT_BEFORE = [sum(b + 1 for b, _ in HALVES[:i]) for i in range(len(HALVES) + 1)]

        def copy_probs(dve, i):
            b, g = HALVES[i]
            for kt in range(b + 1):
                j = PT_BEFORE[i] + kt
                dve.wait_ge(pT_ready, j + 1)
                if i >= 1:
                    dve.wait_ge(o_ready, i)
                dve.tensor_copy(pT[:, kt, :], banks[4 + j % 2][:, :]).then_inc(pT_taken, 1)

        def copy_outputs(act, i):
            b, g = HALVES[i]
            act.wait_ge(o_ready, i + 1)
            act.activation(oT[:, 4 * g:4 * g + 4, b * P:(b + 1) * P],
                           banks[6 + g][:, :].rearrange("p (h q) -> p h q", h=4), ACT.Copy).then_inc(o_taken, 1)

        def inverse(dve, step, i):
            b, g = HALVES[i]
            dve.wait_ge(exp_done, 4 * i + 4)
            step(dve.reciprocal(den[:, b, 4 * g:4 * g + 4], den[:, b, 4 * g:4 * g + 4]))
            dve.tensor_tensor(inv_diag[i % 2], ident[:, :].unsqueeze(1).to_broadcast([P, 4, P]),
                              den[:, b, 4 * g:4 * g + 4].unsqueeze(2).to_broadcast([P, 4, P]), ALU.mult
                              ).then_inc(inv_set, 1)

        block = ctx.enter_context(nc.Block())

        @block.sync
        def _(sp):
            for t in range(NT):
                sp.dma_start(x_sb[:, t, :], x_rows[:, t, :]).then_inc(x_then_gate_w[t], 16)
                if t != 1:
                    continue
                sp.wait_ge(vecs_zeroed, 1)
                for at, vec, n in ((N1, norm1_g, 8), (N2, norm2_g, 8), (QL, q_lat_g, 2), (QN, q_norm_g, 1),
                                   (VG, gmlp_v_g, 1)):
                    sp.dma_start(vecs[at:at + n, :], vec.rearrange("(a p) -> a p", p=P)).then_inc(vecs_loaded, 16)
                sp.dma_start(vecs[KI:KI + 1, 0:ID], k_idx_g.rearrange("(a p) -> a p", a=1)).then_inc(vecs_loaded, 16)
            sp.dma_start(w_lat, in_cols(OFF_LAT, LAT)).then_inc(lat_w_loaded, 16)
            sp.dma_start(kvg[:, :], kv_norm_g.rearrange("(a p) -> a p", a=1).to_broadcast([P, KVR])
                         ).then_inc(first_loaded, 16)
            sp.dma_start(wqi, w_q_idx.rearrange("(k p) h d -> p k (h d)", p=P)).then_inc(qw_loaded, 16)
            sp.dma_start(wuq, w_uq.rearrange("(k p) h d -> p k (h d)", p=P)).then_inc(qw_loaded, 16)
            sp.dma_start(wsp, w_spatial.rearrange("g t s -> t g s")).then_inc(first_loaded, 16)
            sp.dma_start(w_v, in_cols(OFF_V, 512)).then_inc(v_w_loaded, 16)
            sp.dma_start(w_u, in_cols(OFF_U, 512)).then_inc(u_w_loaded, 16)
            sp.dma_start(bspat[:, :, :].rearrange("p g t -> p (g t)"),
                         b_spatial.rearrange("(a g) t -> a (g t)", a=1).to_broadcast([P, G * P])
                         ).then_inc(small_loaded, 16)
            sp.dma_start(br_sb[:, :], b_router.rearrange("(a n) -> a n", a=1).to_broadcast([P, NE])
                         ).then_inc(small_loaded, 16)
            sp.dma_start(wr_sb[:, :, :], w_router.rearrange("(k p) n -> p k n", p=P)).then_inc(small_loaded, 16)
            sp.wait_ge(wuv_zeroed, 1)
            for h in range(H):
                sp.dma_start(wuv[:, h, HV * (h % 2):HV * (h % 2) + HV], w_uv[h]).then_inc(small_loaded, 16)
            for i in range(4):
                if i == 0:
                    sp.wait_ge(lat_ready, NT)
                elif i == 1:
                    sp.wait_ge(v_ready, NT)
                elif i == 2:
                    sp.wait_ge(u_ready, G)
                else:
                    sp.wait_ge(gate_ready, 4)
                sp.dma_start(w_gate[i], in_cols(OFF_GATE + 512 * i, 512)).then_inc(x_then_gate_w[i], 16)
            sp.wait_ge(qidx_ready, IH)
            sp.wait_ge(q_ready, H)
            sp.dma_start(gain2[:, :], norm2_g.rearrange("(a n) -> a n", a=1).to_broadcast([P, D])
                         ).then_inc(x_again, 16)
            sp.wait_ge(gate_ready, 8)
            sp.dma_start(wpa, w_proj_a.rearrange("(k p) n -> p k n", p=P)).then_inc(pa_loaded, 16)
            sp.wait_ge(gate_ready, 12)
            sp.dma_start(wpb, w_proj_b.rearrange("(k p) n -> p k n", p=P)).then_inc(pb_loaded, 16)
            wo_rows = w_out.rearrange("(k p) n -> p k n", p=P)
            sp.wait_ge(gate_ready, 16)
            sp.dma_start(wout[:, 0:4, :], wo_rows[:, 0:4, :]).then_inc(out_w_loaded, 16)
            sp.wait_ge(pa_ready, KD)
            sp.dma_start(wout[:, 4:8, :], wo_rows[:, 4:8, :]).then_inc(out_w_loaded, 16)
            for part in range(3):
                sp.dma_start(bfull[32 * part:32 * part + 32, 0:2 * DE], b_exp1).then_inc(x_again, 16)
                sp.dma_start(bfull[32 * part:32 * part + 32, 2 * DE:2 * DE + D], b_exp2).then_inc(x_again, 16)
            sp.wait_ge(o_ready, len(HALVES))
            sp.wait_ge(s_masked, NT * H)
            sp.wait_ge(pT_ready, PT_BEFORE[-1])
            for t in range(NT):
                sp.dma_start(x_sb[:, t, :], x_rows[:, t, :]).then_inc(x_again, 16)
            sp.wait_ge(pb_ready, KD)
            for j in (4, 5):
                sp.dma_start(ring[:, j, :], w_exp1[0, j * P:(j + 1) * P, :]).then_inc(landed[j], 16)
            rows = xn2_rows.rearrange("(t p) d -> p t d", p=P)
            for t in range(NT - 1):
                sp.wait_ge(r_scaled, t + 1)
                sp.dma_start(rows[:, t, :], rows_sb[:, t, :]).then_inc(rows_stored, 16)
            sp.wait_ge(x2_ready, 2 * NT)
            for j in (0, 1, 2, 3):
                sp.dma_start(ring[:, j, :], w_exp1[0, j * P:(j + 1) * P, :]).then_inc(landed[j], 16)
            sp.wait_ge(r_scaled, NT)
            sp.dma_start(rows[:, NT - 1, :], rows_sb[:, NT - 1, :]).then_inc(rows_stored, 16)
            sp.wait_ge(x_again, 16 * (NT + 7))
            sp.wait_ge(small_loaded, 16 * 11)

        @block.gpsimd
        def _(pool):
            pool.memset(vecs[:, :], 0.0).then_inc(vecs_zeroed, 1)
            pool.memset(ident[:, :], 0.0).then_inc(consts_set, 1)
            pool.memset(ones[:, :], 1.0).then_inc(consts_set, 1)
            pool.wait_ge(consts_set, 2)
            pool.affine_select(out=ident[:, :], in_=ident[:, :], compare_op=ALU.not_equal, fill=1.0, base=0,
                               pattern=[[-1, P]], channel_multiplier=1).then_inc(consts_set, 1)
            pool.wait_ge(first_loaded, 16 * 2)
            pool.affine_select(out=wsp, in_=wsp, compare_op=ALU.is_ge, fill=0.0, base=0,
                               pattern=[[0, G], [-1, P]], channel_multiplier=1).then_inc(masked, 1)
            pool.wait_ge(xT_ready, 2 * NT)
            pool.memset(mask[:, 0, 0:P], 0.0).then_inc(masked, 1)
            pool.wait_ge(masked, 2)
            pool.affine_select(out=mask[:, 0, 0:P], in_=mask[:, 0, 0:P], compare_op=ALU.is_ge, fill=NEG,
                               base=0, pattern=[[-1, P]], channel_multiplier=1).then_inc(masked, 1)
            for n, b in enumerate(QBLOCKS):
                pool.wait_ge(score_done, n + 1)
                diag = mask[:, b, b * P:(b + 1) * P]
                pool.affine_select(out=diag, in_=diag, compare_op=ALU.is_ge, fill=NEG,
                                   base=0, pattern=[[-1, P]], channel_multiplier=1).then_inc(masked, 1)
            pool.wait_ge(low_set, 2)
            for s in range(2, 14):
                pool.wait_ge(high_set, s + 1)
                pool.tensor_tensor(low_unit(s), raw_unit(s), high_unit(s).bitcast(F32), ALU.subtract
                                   ).then_inc(low_set, 1)
            for q in range(4):
                pool.wait_ge(high_set, 15 + q)
                pool.tensor_tensor(ring_low[:, q, :], ring[:, q, :], out_high[q].bitcast(F32), ALU.subtract
                                   ).then_inc(low_set, 1)
            small = ((tables["e_iota"], [[1, NE]], 0, 0), (tables["slot_iota"], [[1, P]], 0, 0),
                     (tables["token"], [[P, NT]], -int(BIG), 1), (tables["pair_row"], [[TK * P, NT]], -int(BIG), TK))
            for dst, pattern, base, per_partition in small:
                pool.iota(dst, pattern=pattern, base=base, channel_multiplier=per_partition,
                          allow_small_or_imprecise_dtypes=True).then_inc(pool_step, 1)
            pool.memset(tables["before"], 1.0).then_inc(pool_step, 1)
            pool.memset(tables["eq"], 0.0).then_inc(pool_step, 1)
            pool.memset(tab, 0.0).then_inc(pool_step, 1)
            pool.memset(rk, -1.0).then_inc(pool_step, 1)
            pool.wait_ge(pool_step, 8)
            pool.affine_select(out=tables["before"], in_=tables["before"], compare_op=ALU.is_gt, fill=0.0, base=0,
                               pattern=[[1, P]], channel_multiplier=-1).then_inc(pool_step, 1)
            for part in range(3):
                pool.wait_ge(pool_step, 9 + part)
                pool.affine_select(out=tables["eq"][0:96, :], in_=tables["eq"][0:96, :], compare_op=ALU.not_equal,
                                   fill=1.0, base=-32 * part, pattern=[[-1, NEP]], channel_multiplier=1
                                   ).then_inc(pool_step, 1)
            step = Steps(pool, pool_step, 12)
            pool.wait_ge(x_again, 16 * (NT + 7))
            step(pool.tensor_copy(bias[:, :], bfull))
            for part in (1, 2):
                for r in range(part, 3):
                    rows = slice(32 * r, 32 * r + 32)
                    step(pool.tensor_tensor(bfull[rows, :], bfull[rows, :], bias[rows, :], ALU.subtract))
                    step(pool.tensor_copy(bias[rows, :], bfull[rows, :]))

        @block.scalar
        def _(act):
            def split_high(s):
                if s >= 4 and s % 2 == 0:
                    act.wait_ge(first_used, s // 2)
                elif s >= 4:
                    act.wait_ge(u_ready if s == 5 else gate_ready, 4 * max(1, (s - 5) // 2))
                if s % 2 == 0:
                    act.wait_ge(([v_w_loaded, u_w_loaded] + x_then_gate_w + [pa_loaded])[s // 2],
                                32 if 4 <= s < 12 else 16)
                act.activation(high_unit(s), raw_unit(s), ACT.Copy).then_inc(high_set, 1)

            for t in range(NT):
                act.wait_ge(x_then_gate_w[t], 16)
                act.activation(gaT[:, 2 * t:2 * t + 2, :].rearrange("p a b -> p (a b)"), x_sb[:, t, :], ACT.Square,
                               accum_out=ss[:, 12 + t:13 + t]).then_inc(x_squared, 1)
                act.wait_ge(x_root, 2 * t + 1)
                act.activation(ss[:, 12 + t:13 + t], ss[:, 12 + t:13 + t], ACT.Sqrt).then_inc(x_root, 1)
            for t in range(NT):
                act.wait_ge(lat_ready, t + 1)
                act.activation(lat_sb[:, t, :], banks[4 + t][:, 0:LAT], ACT.Copy).then_inc(lat_copied, 1)
                act.wait_ge(lat_copied, t + 1)
                for j, (a, n) in enumerate(((0, QR), (C_KV, KVR), (C_KI, ID))):
                    act.activation(gaT[:, t, a:a + n], lat_sb[:, t, a:a + n], ACT.Square,
                                   accum_out=ss[:, 4 * j + t:4 * j + t + 1]).then_inc(lat_squared, 1)
            act.wait_ge(lat_root, 3)
            act.activation(ss[:, 0:12], ss[:, 0:12], ACT.Sqrt).then_inc(lat_root, 1)
            act.wait_ge(xT_taken, 2 * NT)
            for half in range(2):
                part = slice(4 * half, 4 * half + 4)
                act.activation(xnT_high[:, part, :], xnT[:, part, :], ACT.Copy).then_inc(x_high_set, 1)
            act.wait_ge(lat_squared, 3 * NT)
            split_high(0)
            split_high(1)
            for h in range(IH):
                act.wait_ge(qidx_ready, h + 1)
                act.activation(qidxT[:, h, :], banks[4 + h][0:ID, :], ACT.Copy).then_inc(qidx_copied, 1)
            for n, b in enumerate(QBLOCKS):
                if n:
                    act.wait_ge(score_done, n)
                for h in range(IH):
                    act.wait_ge(logit_ready, 4 * n + h + 1)
                    act.activation(relu[:, h, 0:(b + 1) * P], banks[4 * (n % 2) + h][:, 0:(b + 1) * P], ACT.Relu,
                                   scale=ID ** -0.5).then_inc(relu_done, 1)
            for h in range(H):
                act.wait_ge(q_ready, h + 1)
                act.activation(qT[:, h, :], banks[4 + h % 4][:, :], ACT.Copy, scale=cols[:, QN:QN + 1]
                               ).then_inc(q_copied, 1)
                if h >= 2:
                    act.wait_ge(qss_ready, h - 1)
                act.activation(qsq[:, h % 2, :], banks[4 + h % 4][:, :], ACT.Square).then_inc(q_squared, 1)
            act.wait_ge(qss_ready, H)
            act.activation(ss[:, 16:48], banks[0][:, 0:NT * H], ACT.Copy).then_inc(qss_copied, 1)
            act.wait_ge(q_root, 1)
            act.activation(mx[:, :, :].rearrange("p t h -> p (t h)"), den[:, :, :].rearrange("p t h -> p (t h)"),
                           ACT.Sqrt).then_inc(q_root, 1)
            act.wait_ge(wsT_ready, G)
            split_high(2)
            split_high(3)
            for t in range(NT):
                act.wait_ge(v_ready, t + 1)
                act.activation(v_sb[:, t, :], banks[4 + t][:, :], ACT.Gelu_apprx_tanh).then_inc(v_gelu, 1)
            split_high(4)
            split_high(5)
            for g in range(G):
                act.wait_ge(u_ready, g + 1)
                act.activation(uT[:, g, :], banks[g][:, :], ACT.Gelu_apprx_tanh).then_inc(u_gelu, 1)
            act.wait_ge(v_gelu, NT)
            act.wait_ge(q_scale_set, 1)
            act.wait_ge(lat_squared, 3 * NT)
            for t in range(NT):
                for g in range(G):
                    act.activation(gaT[:, t, g * P:(g + 1) * P], v_sb[:, t, g * P:(g + 1) * P], ACT.Square,
                                   accum_out=ss[:, 16 + 4 * t + g:17 + 4 * t + g]).then_inc(v_squared, 1)
            for i in range(16):
                if i % 4 == 0:
                    split_high(6 + i // 2)
                act.wait_ge(gate_ready, i + 1)
                if i == 0:
                    act.wait_ge(v_squared, NT * G)
                if i == 12:
                    act.wait_ge(score_done, 3)
                dst = gaT[:, i, :] if i < 8 else gbT[:, i - 8, :]
                act.activation(dst, banks[(4 + i) % 8][:, :], ACT.Sigmoid).then_inc(gate_taken, 1)
                if i % 4 == 3:
                    split_high(6 + i // 2)
                if i == 11:
                    act.wait_ge(v_root, 1)
                    act.activation(ss[:, 16:32], ss[:, 16:32], ACT.Sqrt).then_inc(v_root, 1)
            for g in range(G):
                act.wait_ge(ya_set, g + 1)
                act.activation(ya_high[:, g, :], uT[:, g, :], ACT.Copy).then_inc(act_high_set, 1)
            for i, (b, g) in enumerate(HALVES):
                n = (b + 1) * P
                for h in range(4):
                    hh = 4 * g + h
                    act.wait_ge(bias_set, i + 1)
                    act.activation(probs[i % 2][:, h, 0:n], probs[i % 2][:, h, 0:n], ACT.Exp,
                                   scale=qs[:, b, hh:hh + 1], bias=mx[:, b, hh:hh + 1],
                                   accum_out=den[:, b, hh:hh + 1]).then_inc(exp_done, 1)
                if i >= 1:
                    copy_outputs(act, i - 1)
            copy_outputs(act, len(HALVES) - 1)
            for j in range(4):
                act.wait_ge(yb_ready, j + 1)
                if j == 0:
                    act.wait_ge(pa_ready, KD)
                act.activation(ybT[:, j, :], banks[j][:, :], ACT.Copy).then_inc(yb_taken, 1)
            act.wait_ge(out_w_loaded, 32)
            for q in range(4):
                act.activation(out_high[q], ring[:, q, :], ACT.Copy).then_inc(high_set, 1)
            for c in range(KD):
                act.wait_ge(merged, c + 1)
                act.activation(merged_high[:, c, :], gaT[:, c, :], ACT.Copy).then_inc(act_high_set, 1)
            for t in range(NT):
                act.wait_ge(x2_taken, 2 * t + 2)
                act.activation(rows_sb[:, t, :], x_sb[:, t, :], ACT.Square, accum_out=r_ss[:, t:t + 1]
                               ).then_inc(r_squared, 1)
                act.wait_ge(r_root, 2 * t + 1)
                act.activation(r_ss[:, t:t + 1], r_ss[:, t:t + 1], ACT.Sqrt).then_inc(r_root, 1)

        @block.vector
        def _(dve):
            step = Steps(dve, dve_step)

            def mean(dst, src, n, signal):
                dve.tensor_scalar(dst, src, 1.0 / n, EPS, ALU.mult, ALU.add).then_inc(signal, 1)

            dve.memset(wuv[:, :, :], 0.0).then_inc(wuv_zeroed, 1)
            for t in range(NT):
                dve.wait_ge(x_squared, t + 1)
                mean(ss[:, 12 + t:13 + t], ss[:, 12 + t:13 + t], D, x_root)
                dve.wait_ge(x_root, 2 * t + 2)
                step(dve.reciprocal(ss[:, 12 + t:13 + t], ss[:, 12 + t:13 + t]))
                dve.tensor_scalar(x_sb[:, t, :], x_sb[:, t, :], ss[:, 12 + t:13 + t], None, ALU.mult
                                  ).then_inc(x_scaled, 1)
            dve.wait_ge(colsT_ready, 1)
            dve.tensor_copy(cols[:, :], banks[7][:, 0:21]).then_inc(cols_set, 1)
            dve.wait_ge(cols_set, 1)
            for j in range(2 * NT):
                t, half = j // 2, j % 2
                dve.wait_ge(xT_ready, j + 1)
                dve.tensor_tensor(xnT[:, 4 * half:4 * half + 4, t * P:(t + 1) * P],
                                  banks[j % 4][:, :].rearrange("p (k q) -> p k q", k=4),
                                  cols[:, N1 + 4 * half:N1 + 4 * half + 4].unsqueeze(2).to_broadcast([P, 4, P]),
                                  ALU.mult).then_inc(xT_taken, 1)
            step(dve.tensor_scalar(cols[:, QN:QN + 1], cols[:, QN:QN + 1], KVR ** -0.5, None, ALU.mult))
            dve.wait_ge(lat_squared, 3 * NT)
            for j, n in enumerate((QR, KVR, ID)):
                mean(ss[:, 4 * j:4 * j + 4], ss[:, 4 * j:4 * j + 4], n, lat_root)
            dve.wait_ge(lat_root, 4)
            step(dve.reciprocal(ss[:, 0:12], ss[:, 0:12]))
            dve.wait_ge(first_loaded, 16 * 2)
            for t in range(NT):
                dve.tensor_scalar(lat_sb[:, t, 0:QR], lat_sb[:, t, 0:QR], ss[:, t:t + 1], None, ALU.mult
                                  ).then_inc(lat_scaled, 1)
            for t in range(NT):
                dve.scalar_tensor_tensor(kv[:, t, :], lat_sb[:, t, C_KV:C_KV + KVR], ss[:, 4 + t:5 + t], kvg[:, :],
                                         ALU.mult, ALU.mult).then_inc(lat_scaled, 1)
            for t in range(NT):
                dve.tensor_scalar(lat_sb[:, t, C_KI:C_KI + ID], lat_sb[:, t, C_KI:C_KI + ID], ss[:, 8 + t:9 + t],
                                  None, ALU.mult).then_inc(lat_scaled, 1)
            step(dve.tensor_scalar(widx[:, :, :], lat_sb[:, :, C_WI:LAT], IH ** -0.5, None, ALU.mult))
            for j in range(2):
                dve.wait_ge(latT_ready, j + 1)
                dve.tensor_scalar(cqT[:, j, :], banks[j][:, :], cols[:, QL + j:QL + j + 1], None, ALU.mult
                                  ).then_inc(latT_taken, 1)
            dve.wait_ge(latT_ready, 3)
            dve.tensor_scalar(kidxT[:, :], banks[2][0:ID, :], cols[0:ID, KI:KI + 1], None, ALU.mult
                              ).then_inc(latT_taken, 1)
            dve.wait_ge(latT_ready, 4)
            dve.tensor_copy(kvT[:, :], banks[3][:, :]).then_inc(latT_taken, 1)
            dve.wait_ge(lat_ready, NT)
            for half in range(2):
                part = slice(4 * half, 4 * half + 4)
                dve.wait_ge(x_high_set, half + 1)
                dve.tensor_tensor(xnT_low[:, part, :], xnT[:, part, :], xnT_high[:, part, :].bitcast(F32),
                                  ALU.subtract).then_inc(x_low_set, 1)
            for s in range(2):
                dve.wait_ge(high_set, s + 1)
                dve.tensor_tensor(low_unit(s), raw_unit(s), high_unit(s).bitcast(F32), ALU.subtract
                                  ).then_inc(low_set, 1)
            for n, b in enumerate(QBLOCKS):
                w = (b + 1) * P
                for h in range(IH):
                    dve.wait_ge(relu_done, 4 * n + h + 1)
                    acc = mask[:, b, 0:w]
                    if h == 0:
                        step(dve.tensor_scalar(acc, relu[:, h, 0:w], widx[:, b, h:h + 1], None, ALU.mult))
                    else:
                        ins = dve.scalar_tensor_tensor(acc, relu[:, h, 0:w], widx[:, b, h:h + 1], acc,
                                                       ALU.mult, ALU.add)
                        if h < IH - 1:
                            step(ins)
                        else:
                            ins.then_inc(score_done, 1)
            dve.wait_ge(wsT_ready, G)
            dve.tensor_copy(wsT[:, :, :].rearrange("p g t -> p (g t)"), banks[1][:, :]).then_inc(wsT_copied, 1)
            dve.wait_ge(qss_copied, 1)
            mean(den[:, :, :].rearrange("p t h -> p (t h)"), ss[:, 16:48], KVR, q_root)
            dve.wait_ge(q_root, 2)
            dve.reciprocal(qs[:, :, :].rearrange("p t h -> p (t h)"), mx[:, :, :].rearrange("p t h -> p (t h)")
                           ).then_inc(q_scale_set, 1)
            for n, b in enumerate(QBLOCKS):
                w = (b + 1) * P
                dve.wait_ge(masked, 4 + n)
                work = mask[:, b, 0:w]
                for _ in range(TOPK // 8):
                    step(dve.max(top8[:, :], work))
                    step(dve.match_replace(work, top8[:, :], work, TAKEN))
                dve.tensor_scalar(work, work, TAKEN_BELOW, NEG, ALU.is_gt, ALU.mult).then_inc(mask_set, 1)
            dve.wait_ge(v_squared, NT * G)
            mean(ss[:, 16:32], ss[:, 16:32], P, v_root)
            dve.wait_ge(v_root, 2)
            step(dve.reciprocal(ss[:, 16:32], ss[:, 16:32]))
            for t in range(NT):
                vt = v_sb[:, t, :].rearrange("p (g n) -> p g n", g=G)
                dve.tensor_tensor(vt, vt, ss[:, 16 + 4 * t:20 + 4 * t].unsqueeze(2).to_broadcast([P, G, P]),
                                  ALU.mult).then_inc(v_scaled, 1)
            def ya_lower(g):
                dve.wait_ge(act_high_set, g + 1)
                dve.tensor_tensor(ya_low[:, g, :], uT[:, g, :], ya_high[:, g, :].bitcast(F32), ALU.subtract
                                  ).then_inc(act_low_set, 1)

            dve.wait_ge(small_loaded, 16 * 11)
            dve.wait_ge(u_gelu, G)
            for g in range(G):
                dve.wait_ge(mix_ready, g + 1)
                mixed = banks[4 + g][:, :].rearrange("p (t n) -> p t n", t=NT)
                step(dve.scalar_tensor_tensor(mixed, mixed, cols[:, VG:VG + 1],
                                              bspat[:, g:g + 1, :].to_broadcast([P, NT, P]), ALU.mult, ALU.add))
                dve.tensor_tensor(uT[:, g, :], uT[:, g, :], banks[4 + g][:, :], ALU.mult).then_inc(ya_set, 1)
                if g:
                    ya_lower(g - 1)
            ya_lower(G - 1)
            for c in range(KD):
                dve.wait_ge(pa_ready, c + 1)
                dve.wait_ge(gate_taken, 16)
                dve.tensor_tensor(gaT[:, c, :], gaT[:, c, :], banks[c][:, :], ALU.mult).then_inc(pa_taken, 1)
            dve.wait_ge(mask_set, 3)
            dve.wait_ge(masked, 6)
            for i, (b, g) in enumerate(HALVES):
                n = (b + 1) * P
                if i >= 1:
                    inverse(dve, step, i - 1)
                if i >= 2:
                    dve.wait_ge(pT_ready, PT_BEFORE[i - 1])
                for h in range(4):
                    hh = 4 * g + h
                    dve.wait_ge(s_ready, 4 * i + h + 1)
                    dve.tensor_tensor_reduce(probs[i % 2][:, h, 0:n], banks[h][:, 0:n], mask[:, b, 0:n], 1.0, TAKEN,
                                             ALU.add, ALU.max, mx[:, b, hh:hh + 1]).then_inc(s_masked, 1)
                dve.wait_ge(s_masked, 4 * i + 4)
                dve.scalar_tensor_tensor(mx[:, b, 4 * g:4 * g + 4], mx[:, b, 4 * g:4 * g + 4], -1.0,
                                         qs[:, b, 4 * g:4 * g + 4], ALU.mult, ALU.mult).then_inc(bias_set, 1)
                if i >= 1:
                    copy_probs(dve, i - 1)
            inverse(dve, step, len(HALVES) - 1)
            copy_probs(dve, len(HALVES) - 1)
            def merged_lower(c):
                dve.wait_ge(act_high_set, G + c + 1)
                dve.tensor_tensor(merged_low[:, c, :], gaT[:, c, :], merged_high[:, c, :].bitcast(F32), ALU.subtract
                                  ).then_inc(act_low_set, 1)

            for c in range(KD):
                dve.wait_ge(pb_ready, c + 1)
                step(dve.tensor_tensor(gbT[:, c, :], gbT[:, c, :], banks[4 + c % 4][:, :], ALU.mult))
                dve.tensor_tensor(gaT[:, c, :], gaT[:, c, :], gbT[:, c, :], ALU.add).then_inc(merged, 1)
                if c:
                    merged_lower(c - 1)
            merged_lower(KD - 1)
            for j in range(2 * NT):
                t, n = j // 2, j % 2
                dve.wait_ge(x2_ready, j + 1)
                dve.wait_ge(x_again, 16 * (NT + 7))
                dve.tensor_tensor(x_sb[:, t, 512 * n:512 * n + 512], x_sb[:, t, 512 * n:512 * n + 512],
                                  banks[j % 4][:, :], ALU.add).then_inc(x2_taken, 1)
                if n == 0:
                    continue
                dve.wait_ge(r_squared, t + 1)
                mean(r_ss[:, t:t + 1], r_ss[:, t:t + 1], D, r_root)
                dve.wait_ge(r_root, 2 * t + 2)
                step(dve.reciprocal(r_ss[:, t:t + 1], r_ss[:, t:t + 1]))
                dve.scalar_tensor_tensor(rows_sb[:, t, :], x_sb[:, t, :], r_ss[:, t:t + 1], gain2[:, :], ALU.mult,
                                         ALU.mult).then_inc(r_scaled, 1)
                for half in range(2):
                    dve.wait_ge(r_T_ready, 2 * t + half + 1)
                    dve.tensor_copy(xn2T[:, 4 * half:4 * half + 4, t * P:(t + 1) * P],
                                    banks[4 + half][:, :].rearrange("p (k q) -> p k q", k=4)).then_inc(r_T_taken, 1)

        @block.tensor
        def _(pe):
            def product(bank, pairs):
                for k, (lhsT, rhs) in enumerate(pairs):
                    last = pe.matmul(bank, lhsT, rhs, start=(k == 0), stop=(k == len(pairs) - 1))
                return last

            pe.wait_ge(consts_set, 3)
            pe.wait_ge(vecs_loaded, 16 * 6)
            pe.transpose(banks[7][:, 0:21], vecs[:, :], ident[0:21, 0:21]).then_inc(colsT_ready, 1)
            for j in range(2 * NT):
                t, half = j // 2, j % 2
                pe.wait_ge(x_scaled, t + 1)
                if j >= 4:
                    pe.wait_ge(xT_taken, j - 3)
                for k in range(4):
                    last = pe.transpose(banks[j % 4][:, k * P:(k + 1) * P],
                                        x_sb[:, t, (4 * half + k) * P:(4 * half + k + 1) * P], ident[:, :])
                last.then_inc(xT_ready, 1)
            pe.wait_ge(lat_w_loaded, 16)
            pe.wait_ge(cols_set, 1)
            for t in range(NT):
                pe.wait_ge(xT_taken, 2 * t + 2)
                product(banks[4 + t][:, 0:LAT], [(xnT[:, k, t * P:(t + 1) * P], w_lat[:, k, :]) for k in range(KD)]
                        ).then_inc(lat_ready, 1)
            pe.wait_ge(xT_taken, 2 * NT)
            for j in range(2):
                pe.wait_ge(lat_scaled, NT)
                for t in range(NT):
                    last = pe.transpose(banks[j][:, t * P:(t + 1) * P], lat_sb[:, t, j * P:(j + 1) * P], ident[:, :])
                last.then_inc(latT_ready, 1)
            pe.wait_ge(lat_scaled, 3 * NT)
            for t in range(NT):
                last = pe.transpose(banks[2][0:ID, t * P:(t + 1) * P], lat_sb[:, t, C_KI:C_KI + ID], ident[:, :])
            last.then_inc(latT_ready, 1)
            for t in range(NT):
                last = pe.transpose(banks[3][:, t * P:(t + 1) * P], kv[:, t, :], ident[:, :])
            last.then_inc(latT_ready, 1)
            pe.wait_ge(qw_loaded, 32)
            pe.wait_ge(latT_taken, 2)
            pe.wait_ge(lat_copied, NT)
            for h in range(IH):
                product(banks[4 + h][0:ID, :], [(wqi[:, k, h * ID:(h + 1) * ID], cqT[:, k, :]) for k in range(2)]
                        ).then_inc(qidx_ready, 1)
            pe.wait_ge(latT_taken, 4)
            for n, b in enumerate(QBLOCKS):
                for h in range(IH):
                    if n == 0:
                        pe.wait_ge(qidx_copied, h + 1)
                    elif n == 1:
                        pe.wait_ge(qidx_copied, IH)
                    else:
                        pe.wait_ge(relu_done, h + 1)
                    product(banks[4 * (n % 2) + h][:, 0:(b + 1) * P],
                            [(qidxT[:, h, b * P:(b + 1) * P], kidxT[:, 0:(b + 1) * P])]).then_inc(logit_ready, 1)
            def query_squares(h):
                pe.wait_ge(q_squared, h + 1)
                if h == 0:
                    pe.wait_ge(relu_done, 12)
                for t in range(NT):
                    last = pe.matmul(banks[0][:, t * H + h:t * H + h + 1], qsq[:, h % 2, t * P:(t + 1) * P],
                                     ones[:, 0:1], start=True, stop=True)
                last.then_inc(qss_ready, 1)

            for h in range(H):
                if h < 4:
                    pe.wait_ge(relu_done, 5 + h)
                else:
                    pe.wait_ge(q_squared, h - 3)
                product(banks[4 + h % 4][:, :], [(wuq[:, k, h * P:(h + 1) * P], cqT[:, k, :]) for k in range(2)]
                        ).then_inc(q_ready, 1)
                if h >= 1:
                    query_squares(h - 1)
            query_squares(H - 1)
            pe.wait_ge(masked, 1)
            for g in range(G):
                pe.transpose(banks[1][:, g * P:(g + 1) * P], wsp[:, g, :], ident[:, :]).then_inc(wsT_ready, 1)

            def three(bank, a_high, a_low, b_high, b_low, start, stop):
                pe.matmul(bank, a_high, b_high, start=start, stop=False)
                pe.matmul(bank, a_high, b_low, start=False, stop=False)
                return pe.matmul(bank, a_low, b_high, start=False, stop=stop)

            def in_product(first, by_token, ready, bank_free):
                for s in (first, first + 1):
                    pe.wait_ge(low_set, s + 1)
                    high = high_unit(s).rearrange("p (k n) -> p k n", k=4)
                    low = low_unit(s).rearrange("p (k n) -> p k n", k=4)
                    for k in range(4):
                        kx = 4 * (s - first) + k
                        for c in range(4):
                            if s == first and k == 0:
                                bank_free(c)
                            cols = slice(c * P, (c + 1) * P)
                            bank = banks[(4 + 2 * first + c) % 8][:, :]
                            if by_token:
                                last = three(bank, xnT_high[:, kx, cols], xnT_low[:, kx, cols], high[:, k, :],
                                             low[:, k, :], kx == 0, kx == KD - 1)
                            else:
                                last = three(bank, high[:, k, cols], low[:, k, cols], xnT_high[:, kx, :],
                                             xnT_low[:, kx, :], kx == 0, kx == KD - 1)
                            if kx == KD - 1:
                                last.then_inc(ready, 1)
                    if s == first:
                        last.then_inc(first_used, 1)

            pe.wait_ge(x_low_set, 2)
            in_product(0, True, v_ready, lambda c: pe.wait_ge(q_squared, 5 + c))
            pe.wait_ge(qss_copied, 1)
            pe.wait_ge(wsT_copied, 1)
            in_product(2, False, u_ready, lambda c: None)
            in_product(4, False, gate_ready, lambda c: pe.wait_ge(v_gelu, c + 1))
            in_product(6, False, gate_ready, lambda c: pe.wait_ge(u_gelu, c + 1))
            in_product(8, False, gate_ready, lambda c: pe.wait_ge(gate_taken, c + 1))
            in_product(10, False, gate_ready, lambda c: pe.wait_ge(gate_taken, c + 5))
            for g in range(G):
                pe.wait_ge(gate_taken, 9 + g)
                pe.wait_ge(v_scaled, NT)
                for t in range(NT):
                    last = pe.matmul(banks[4 + g][:, t * P:(t + 1) * P], v_sb[:, t, g * P:(g + 1) * P], wsT[:, g, :],
                                     start=True, stop=True)
                last.then_inc(mix_ready, 1)
            for half in range(2):
                for k in range(G):
                    s = 12 + k // 2
                    if half == 0:
                        pe.wait_ge(low_set, s + 1)
                        pe.wait_ge(act_low_set, k + 1)
                    for c in range(4 * half, 4 * half + 4):
                        if half == 0 and k == 0:
                            pe.wait_ge(gate_taken, 13 + c)
                        at = 1024 * (k % 2) + c * P
                        last = three(banks[c][:, :], high_unit(s)[:, at:at + P], low_unit(s)[:, at:at + P],
                                     ya_high[:, k, :], ya_low[:, k, :], k == 0, k == G - 1)
                        if k == G - 1:
                            last.then_inc(pa_ready, 1)

            def scores(i):
                b, g = HALVES[i]
                for h in range(4):
                    if i == 0:
                        pe.wait_ge(pa_taken, h + 1)
                    else:
                        pe.wait_ge(s_masked, 4 * (i - 1) + h + 1)
                    product(banks[h][:, 0:(b + 1) * P],
                            [(qT[:, 4 * g + h, b * P:(b + 1) * P], kvT[:, 0:(b + 1) * P])]).then_inc(s_ready, 1)

            def mix_values(i):
                b, g = HALVES[i]
                pe.wait_ge(inv_set, i + 1)
                if i == 0:
                    pe.wait_ge(pa_taken, KD)
                for kt in range(b + 1):
                    j = PT_BEFORE[i] + kt
                    if j >= 2:
                        pe.wait_ge(pT_taken, j - 1)
                    for h in range(4):
                        last = pe.matmul(banks[4 + j % 2][:, h * P:(h + 1) * P],
                                         probs[i % 2][:, h, kt * P:(kt + 1) * P], inv_diag[i % 2][:, h, :],
                                         start=True, stop=True)
                    last.then_inc(pT_ready, 1)
                if i >= 2:
                    pe.wait_ge(o_taken, i - 1)
                for kt in range(b + 1):
                    pe.wait_ge(pT_taken, PT_BEFORE[i] + kt + 1)
                    last = pe.matmul(banks[6 + g][:, :], kv[:, kt, :], pT[:, kt, :], start=(kt == 0), stop=(kt == b))
                last.then_inc(o_ready, 1)

            for i in range(len(HALVES)):
                scores(i)
                if i >= 1:
                    mix_values(i - 1)
            mix_values(len(HALVES) - 1)
            pe.wait_ge(small_loaded, 16 * 11)
            for j in range(4):
                pe.wait_ge(s_masked, NT * H)
                pe.wait_ge(o_taken, len(HALVES))
                product(banks[j][:, :], [(wuv[:, 2 * j + a, :], oT[:, 2 * j + a, :]) for a in range(2)]
                        ).then_inc(yb_ready, 1)
            pe.wait_ge(pb_loaded, 16)
            pe.wait_ge(yb_taken, 4)
            for c in range(KD):
                if c >= 4:
                    pe.wait_ge(merged, c - 3)
                product(banks[4 + c % 4][:, :], [(wpb[:, k, c * P:(c + 1) * P], ybT[:, k, :]) for k in range(G)]
                        ).then_inc(pb_ready, 1)
            def transposes(t):
                pe.wait_ge(r_scaled, t + 1)
                for half in range(2):
                    if t:
                        pe.wait_ge(r_T_taken, 2 * t + half - 1)
                    for k in range(4):
                        last = pe.transpose(banks[4 + half][:, k * P:(k + 1) * P],
                                            rows_sb[:, t, (4 * half + k) * P:(4 * half + k + 1) * P], ident[:, :])
                    last.then_inc(r_T_ready, 1)

            def route(t):
                pe.wait_ge(r_T_taken, 2 * t + 2)
                for k in range(KD):
                    last = pe.matmul(banks[6][:, t * NE:(t + 1) * NE], xn2T[:, k, t * P:(t + 1) * P], wr_sb[:, k, :],
                                     start=(k == 0), stop=(k == KD - 1))
                last.then_inc(route_ready, 1)

            for j in range(2 * NT):
                t, n = j // 2, j % 2
                if j >= 4:
                    pe.wait_ge(x2_taken, j - 3)
                for k in range(KD):
                    q, at = k // 2, 1024 * (k % 2) + 512 * n
                    if j == 0:
                        pe.wait_ge(low_set, 15 + q)
                        pe.wait_ge(act_low_set, G + k + 1)
                    last = three(banks[j % 4][:, :], merged_high[:, k, t * P:(t + 1) * P],
                                 merged_low[:, k, t * P:(t + 1) * P], out_high[q][:, at:at + 512],
                                 ring_low[:, q, at:at + 512], k == 0, k == KD - 1)
                last.then_inc(x2_ready, 1)
                if n == 0 and t >= 1:
                    transposes(t - 1)
                if n == 1 and t >= 1:
                    route(t - 1)
            transposes(NT - 1)
            route(NT - 1)


def routing(nc, sem, banks, ring, wh, wl, landed, wh_set, wl_set, xg, onesb, zero, ones, br_sb, tables,
            tab, rk, counts, over_flag, rows_stored):
    with ExitStack() as ctx:
        def sb(name, shape, dt=F32):
            return ctx.enter_context(nc.sbuf_tensor(name, shape, dt))

        logits = sb("logits", [P, NT, NE])
        top = sb("top", [P, NT, 8])
        top_at = sb("top_at", [P, NT, 8], U32)
        top_col = sb("top_col", [P, NT, 8])
        gate = sb("gate", [P, NT, TK])
        gsum = sb("gsum", [P, NT])
        hot = sb("hot", [P, NT, TK, NE])
        weighted = sb("weighted", [P, NT, TK, NE])
        routed = sb("routed", [P, NT, NE])
        earlier = sb("earlier", [P, NT + 1, NE])
        over_f = sb("over_f", [P, 1])
        top_set, exp_set = sem("top_set"), sem("exp_set")
        routed_set, rank_ready = sem("routed_set"), sem("rank_ready")
        r_step = sem("r_step")
        block = ctx.enter_context(nc.Block())

        @block.sync
        def _(sp):
            sp.wait_ge(rows_stored, 16 * NT)

        @block.gpsimd
        def _(pool):
            pool.memset(xg[:, :], 0.0)
            pool.memset(onesb[:, :], 1.0)
            pool.memset(zero[:, :], 0.0)
            pool.wait_ge(wh_set, 1)
            pool.tensor_tensor(wl[:, 0, :], ring[:, 0, :], wh[:, 0, :].bitcast(F32), ALU.subtract
                               ).then_inc(wl_set, 1)

        @block.scalar
        def _(act):
            act.wait_ge(landed[0], 16)
            act.activation(wh[:, 0, :], ring[:, 0, :], ACT.Copy).then_inc(wh_set, 1)
            act.wait_ge(top_set, 1)
            act.activation(gate[:, :, :], gate[:, :, :], ACT.Exp).then_inc(exp_set, 1)
            for i in range(1, AHEAD):
                act.wait_ge(landed[i], 16)
                act.activation(wh[:, i, :], ring[:, i, :], ACT.Copy).then_inc(wh_set, 1)

        @block.vector
        def _(dve):
            step = Steps(dve, r_step)

            def per_choice(a):
                return a.unsqueeze(3).to_broadcast([P, NT, a.shape[2], NE])

            def per_expert(a):
                return a.unsqueeze(2).to_broadcast([P, NT, NE])

            step(dve.tensor_tensor(logits[:, :, :], banks[6][:, 0:NT * NE].rearrange("p (t e) -> p t e", t=NT),
                                   br_sb[:, :].unsqueeze(1).to_broadcast([P, NT, NE]), ALU.add))
            for t in range(NT):
                ins = dve.max(top[:, t, :], logits[:, t, :])
            step(ins)
            dve.tensor_tensor(gate[:, :, :], top[:, :, 0:TK], top[:, :, 0:1].to_broadcast([P, NT, TK]), ALU.subtract
                              ).then_inc(top_set, 1)
            for t in range(NT):
                ins = dve.max_index(top_at[:, t, :], top[:, t, :], logits[:, t, :])
            step(ins)
            step(dve.tensor_copy(top_col[:, :, :], top_at[:, :, :]))
            step(dve.tensor_tensor(hot[:, :, :, :],
                                   tables["e_iota"].unsqueeze(1).unsqueeze(1).to_broadcast([P, NT, TK, NE]),
                                   per_choice(top_col[:, :, 0:TK]), ALU.is_equal))
            dve.memset(earlier[:, 0, :], 0.0)
            dve.tensor_reduce(routed[:, :, :], hot[:, :, :, :].rearrange("p t k e -> p t e k"), AX.X, ALU.add
                              ).then_inc(routed_set, 1)
            dve.wait_ge(routed_set, 1)
            for t in range(NT - 1):
                step(dve.tensor_tensor(earlier[:, t + 1, :], earlier[:, t, :], routed[:, t, :], ALU.add))
            dve.tensor_tensor(earlier[:, NT, :], earlier[:, NT - 1, :], routed[:, NT - 1, :], ALU.add
                              ).then_inc(routed_set, 1)
            dve.wait_ge(exp_set, 1)
            step(dve.tensor_reduce(gsum[:, :], gate[:, :, :], AX.X, ALU.add))
            step(dve.reciprocal(gsum[:, :], gsum[:, :]))
            step(dve.tensor_tensor(gate[:, :, :], gate[:, :, :], gsum[:, :].unsqueeze(2).to_broadcast([P, NT, TK]),
                                   ALU.mult))
            step(dve.tensor_tensor(weighted[:, :, :, :], hot[:, :, :, :], per_choice(gate[:, :, :]), ALU.mult))
            dve.tensor_reduce(tab[:, :, 2, 0:NE], weighted[:, :, :, :].rearrange("p t k e -> p t e k"), AX.X, ALU.add)
            dve.tensor_tensor(tab[:, :, 0, 0:NE], routed[:, :, :], per_expert(tables["token"]), ALU.mult)
            step(dve.tensor_tensor(tab[:, :, 1, 0:NE], routed[:, :, :], per_expert(tables["pair_row"]), ALU.mult))
            for k in range(1, TK):
                step(dve.scalar_tensor_tensor(tab[:, :, 1, 0:NE], hot[:, :, k, :], float(k), tab[:, :, 1, 0:NE],
                                              ALU.mult, ALU.add))
            dve.wait_ge(rank_ready, 2)
            step(dve.scalar_tensor_tensor(rk[:, :, 0:NE], banks[4][:, 0:NT * NE].rearrange("p (t e) -> p t e", t=NT),
                                          1.0, routed[:, :, :], ALU.add, ALU.mult))
            step(dve.tensor_scalar(rk[:, :, 0:NE], rk[:, :, 0:NE], -1.0, None, ALU.add))
            step(dve.tensor_copy(counts, banks[5][:, 0:NE]))
            step(dve.tensor_reduce(over_f[:, :], counts, AX.X, ALU.max))
            step(dve.tensor_scalar(over_flag[:, :], over_f[:, :], float(P), None, ALU.is_gt))

        @block.tensor
        def _(pe):
            pe.wait_ge(routed_set, 2)
            pe.matmul(banks[4][:, 0:NT * NE], tables["before"], routed[:, :, :].rearrange("p t e -> p (t e)"),
                      start=True, stop=False)
            pe.matmul(banks[4][:, 0:NT * NE], ones[:, :], earlier[:, 0:NT, :].rearrange("p t e -> p (t e)"),
                      start=False, stop=True).then_inc(rank_ready, 1)
            pe.matmul(banks[5][:, 0:NE], ones[:, :], earlier[:, NT, :], start=True, stop=True
                      ).then_inc(rank_ready, 1)


def experts(nc, sem, banks, ring, wh, wl, wh_set, wl_set, xg, onesb, zero, ident, tab, rk, bias, eq, slot_iota, landed,
            xn2_rows, pair_rows, w_exp1, w_exp2):
    with ExitStack() as ctx:
        def sb(name, shape, dt=F32):
            return ctx.enter_context(nc.sbuf_tensor(name, shape, dt))

        pick = sb("pick", [P, NT, P])
        sel_h = sb("sel_h", [96, P], BF16)
        sel_y = sb("sel_y", [96, P], BF16)
        row_in = sb("row_in", [P, 1], U32)
        row_out = sb("row_out", [P, 1], U32)
        dest = sb("dest", [P, NEP])
        gates = sb("gates", [P, NEP])
        xh = sb("xh", [P, KD, P], F32R)
        xl = sb("xl", [P, KD, P], F32R)
        hg = sb("hg", [P, DE])
        hu = sb("hu", [P, DE])
        sg = sb("sg", [P, DE])
        ah = sb("ah", [P, KD, P], F32R)
        al = sb("al", [P, KD, P], F32R)
        y = sb("y", [P, D])
        carried = sb("carried", [P, 2])

        def gather(pool):
            return pool.indirect_dma_start(out=xg[:, :], out_offset=None, in_=xn2_rows,
                                           in_offset=bass.IndirectOffsetOnAxis(ap=row_in[:, 0:1], axis=0),
                                           bounds_check=S - 1, oob_is_err=False)

        def scatter(pool):
            return pool.indirect_dma_start(out=pair_rows,
                                           out_offset=bass.IndirectOffsetOnAxis(ap=row_out[:, 0:1], axis=0),
                                           in_=y[:, :], in_offset=None, bounds_check=S * TK - 1, oob_is_err=False)

        def carry_waits(pool, i, signal):
            pool.tensor_tensor(carried[:, i:i + 1], zero[:, :], zero[:, :], ALU.add).then_inc(signal, 1)

        gather_carried, scatter_carried = sem("gather_carried"), sem("scatter_carried")
        pick_set, slots_ready, slots_taken = sem("pick_set"), sem("slots_ready"), sem("slots_taken")
        gathered, scattered = sem("gathered"), sem("scattered")
        xT_ready, xh_set, xl_set = sem("xgT_ready"), sem("xh_set"), sem("xl_set")
        selh_set, sely_set = sem("selh_set"), sem("sely_set")
        unit_used = sem("unit_used")
        hg_set, hu_set, hgu_set = sem("hg_set"), sem("hu_set"), sem("hgu_set")
        sig_done, act_set = sem("sig_done"), sem("act_set")
        aT_ready, ah_set, al_set = sem("aT_ready"), sem("ah_set"), sem("al_set")
        y_set, row_out_set = sem("y_set"), sem("row_out_set")

        FIRST = KD
        def number(e, i):
            return i if type(e) is int and e == 0 else e * PER_E + (i + FIRST - PER_E)

        def slot(i, turn0, n):
            return (i if turn0 else i + FIRST) % n

        block = ctx.enter_context(nc.Block())

        @block.sync
        def _(sp):
            def load(e, i, src, turn0=False):
                sp.wait_ge(wl_set, number(e, i) + (1 - RAW))
                q = slot(i, turn0, RAW)
                dst = ring[:, q, :]
                if src.shape[0] == P and len(src.shape) == 3:
                    dst = dst.rearrange("p (k n) -> p k n", k=2)
                sp.dma_start(dst, src).then_inc(landed[q], 16)

            def w1_rows(e, k):
                return w_exp1[bass.ds(e, 1), k * P:(k + 1) * P, :].rearrange("a p n -> (a p) n")

            def w2_rows(e, q):
                return w_exp2[bass.ds(e, 1), 2 * q * P:2 * (q + 1) * P, :].rearrange("a (k p) n -> p (a k) n", p=P)

            for k in range(RAW, KD):
                load(0, k, w1_rows(0, k), turn0=True)
            with sp.Fori(1, NE) as e:
                for k in range(KD):
                    load(e, k, w1_rows(e, k))
                for q in range(4):
                    load(e, KD + q, w2_rows(e - 1, q))
            for q in range(4):
                load(NE, q, w2_rows(NE - 1, q))

        @block.gpsimd
        def _(pool):
            for e in range(3):
                pool.wait_ge(slots_taken, e + 1)
                if e:
                    pool.wait_ge(xT_ready, 2 * e)
                gather(pool).then_inc(gathered, 16)
            with pool.Fori(1, NE) as e:
                pool.wait_ge(slots_taken, e + 3)
                pool.wait_ge(xT_ready, e * 2 + 4)
                carry_waits(pool, 0, gather_carried)
                gather(pool).then_inc(gathered, 16)
                pool.wait_ge(row_out_set, e)
                pool.wait_ge(y_set, e * 2)
                carry_waits(pool, 1, scatter_carried)
                scatter(pool).then_inc(scattered, 16)
            pool.wait_ge(row_out_set, NE)
            pool.wait_ge(y_set, 2 * NE)
            scatter(pool).then_inc(scattered, 16)
            pool.wait_ge(gathered, 16 * NEP)
            pool.wait_ge(scattered, 16 * NE)

        @block.scalar
        def _(act):
            def split_high(e, i, turn0=False):
                q, w = slot(i, turn0, RAW), slot(i, turn0, SPLIT)
                if turn0:
                    act.wait_ge(landed[q], 16 * (i // RAW + 1))
                    if i >= SPLIT:
                        act.wait_ge(unit_used, i + 1 - SPLIT)
                else:
                    act.wait_ge(landed[q], e * 32 + 16 * ((i + FIRST - PER_E) // RAW + 1))
                    act.wait_ge(unit_used, number(e, i) + (1 - SPLIT))
                act.activation(wh[:, w, :], ring[:, q, :], ACT.Copy).then_inc(wh_set, 1)

            def sigmoid(e):
                act.wait_ge(hg_set, e * 2 + 2)
                act.activation(sg[:, :], hg[:, :], ACT.Sigmoid, scale=ALPHA).then_inc(sig_done, 1)

            def upper_half(dst, half, ready, count, signal):
                act.wait_ge(ready, count)
                act.activation(dst[:, 4 * half:4 * half + 4, :].rearrange("p k q -> p (k q)"), banks[6 + half][:, :],
                               ACT.Copy).then_inc(signal, 1)

            def gated_rows(e):
                for n in range(2):
                    act.activation(y[:, 512 * n:512 * n + 512], banks[4 + n][:, :], ACT.Copy,
                                   scale=gates[:, bass.ds(e, 1)]).then_inc(y_set, 1)

            for half in range(2):
                upper_half(xh, half, xT_ready, half + 1, xh_set)
            for i in range(AHEAD, KD):
                split_high(0, i, True)
            for i in range(AHEAD):
                split_high(1, i)
            act.wait_ge(unit_used, KD)
            for half in range(2):
                upper_half(xh, half, xT_ready, half + 3, xh_set)
            sigmoid(0)
            with act.Fori(1, NE) as e:
                split_high(e, AHEAD)
                for half in range(2):
                    upper_half(ah, half, aT_ready, e * 2 + (half - 1), ah_set)
                for i in range(AHEAD + 1, KD + AHEAD):
                    split_high(e, i)
                sigmoid(e)
                split_high(e, KD + AHEAD)
                upper_half(xh, 0, xT_ready, e * 2 + 3, xh_set)
                upper_half(xh, 1, xT_ready, e * 2 + 4, xh_set)
                for i in range(PER_E, PER_E + AHEAD):
                    split_high(e, i)
                act.wait_ge(unit_used, number(e, PER_E))
                act.wait_ge(slots_taken, e + 2)
                act.wait_ge(row_out_set, e)
                gated_rows(e - 1)
            for half in range(2):
                upper_half(ah, half, aT_ready, 2 * NE - 1 + half, ah_set)
            split_high(NE, AHEAD)
            act.wait_ge(unit_used, number(NE, 4))
            act.wait_ge(scattered, 16 * (NE - 1))
            gated_rows(NE - 1)

        @block.vector
        def _(dve):
            def pick_tokens(e):
                for t in range(NT):
                    last = dve.tensor_scalar(pick[:, t, :], slot_iota[:, :], rk[:, t, bass.ds(e, 1)], None,
                                             ALU.is_equal)
                last.then_inc(pick_set, 1)

            def take_slots(e):
                dve.tensor_scalar(dest[:, bass.ds(e, 1)], banks[7][:, 1:2], BIG, None, ALU.add)
                dve.tensor_copy(gates[:, bass.ds(e, 1)], banks[7][:, 2:3])
                dve.tensor_scalar(row_in[:, :], banks[7][:, 0:1], BIG, None, ALU.add).then_inc(slots_taken, 1)

            def split_low(e, i, turn0=False):
                q, w = slot(i, turn0, RAW), slot(i, turn0, SPLIT)
                dve.wait_ge(wh_set, number(e, i) + 1)
                dve.tensor_tensor(wl[:, w, :], ring[:, q, :], wh[:, w, :].bitcast(F32), ALU.subtract
                                  ).then_inc(wl_set, 1)

            def lower_half(dst, high, half, ready, count, signal):
                dve.wait_ge(ready, count)
                part = (slice(None), slice(4 * half, 4 * half + 4), slice(None))
                dve.tensor_tensor(dst[part].rearrange("p k q -> p (k q)"), banks[6 + half][:, :],
                                  high[part].bitcast(F32).rearrange("p k q -> p (k q)"), ALU.subtract
                                  ).then_inc(signal, 1)

            def select(sel, e, signal):
                dve.tensor_scalar(sel[:, :], onesb[:, :], eq[:, bass.ds(e, 1)], None, ALU.mult).then_inc(signal, 1)

            def clip_gate(e, h_ready):
                dve.wait_ge(unit_used, h_ready)
                for n in range(2):
                    dve.tensor_scalar(hg[:, 512 * n:512 * n + 512], banks[n][:, :], LIMIT, None, ALU.min
                                      ).then_inc(hg_set, 1)

            def clip_up():
                for n in range(2):
                    dve.tensor_scalar(hu[:, 512 * n:512 * n + 512], banks[2 + n][:, :], LIMIT, -LIMIT, ALU.min, ALU.max
                                      ).then_inc(hu_set, 1)

            def multiply(e):
                dve.wait_ge(hu_set, e * 2 + 2)
                dve.scalar_tensor_tensor(hu[:, :], hu[:, :], 1.0, hg[:, :], ALU.add, ALU.mult).then_inc(hgu_set, 1)

            def activate(e):
                dve.wait_ge(hgu_set, e + 1)
                dve.wait_ge(sig_done, e + 1)
                dve.tensor_tensor(sg[:, :], hu[:, :], sg[:, :], ALU.mult).then_inc(act_set, 1)

            select(sel_h, 0, selh_set)
            select(sel_y, 0, sely_set)
            pick_tokens(0)
            dve.wait_ge(slots_ready, 1)
            take_slots(0)
            pick_tokens(1)
            for i in range(1, AHEAD):
                split_low(0, i, True)
            dve.wait_ge(slots_ready, 2)
            dve.wait_ge(gathered, 16)
            take_slots(1)
            for half in range(2):
                lower_half(xl, xh, half, xh_set, half + 1, xl_set)
            pick_tokens(2)
            for i in range(AHEAD, KD):
                split_low(0, i, True)
                if i == 5:
                    dve.wait_ge(gathered, 32)
                    dve.wait_ge(slots_ready, 3)
                    take_slots(2)
            for i in range(AHEAD - 1):
                split_low(1, i)
            clip_gate(0, KD)
            select(sel_h, 1, selh_set)
            clip_up()
            for half in range(2):
                lower_half(xl, xh, half, xh_set, half + 3, xl_set)
            multiply(0)
            activate(0)
            split_low(1, AHEAD - 1)
            def turn(e, first=False):
                split_low(e, AHEAD)
                pick_tokens(e + 2)
                for half in range(2):
                    lower_half(al, ah, half, ah_set, e * 2 + (half - 1), al_set)
                for i in range(AHEAD + 1, KD + AHEAD):
                    split_low(e, i)
                    if i == AHEAD + 3:
                        if not first:
                            dve.wait_ge(gather_carried, e - 1)
                            dve.wait_ge(scatter_carried, e - 1)
                            dve.wait_ge(scattered, e * 16 - 16)
                        dve.tensor_copy(row_out[:, :], dest[:, bass.ds(e - 1, 1)]).then_inc(row_out_set, 1)
                clip_gate(e, number(e, KD))
                select(sel_h, e + 1, selh_set)
                clip_up()
                dve.wait_ge(gathered, e * 16 + 32)
                dve.wait_ge(slots_ready, e + 3)
                take_slots(e + 2)
                multiply(e)
                split_low(e, KD + AHEAD)
                activate(e)
                for half in range(2):
                    lower_half(xl, xh, half, xh_set, e * 2 + (half + 3), xl_set)
                for i in range(PER_E, PER_E + AHEAD):
                    split_low(e, i)
                dve.wait_ge(unit_used, number(e, PER_E))
                select(sel_y, e, sely_set)

            turn(1, first=True)
            with dve.Fori(2, NE) as e:
                turn(e)
            for half in range(2):
                lower_half(al, ah, half, ah_set, 2 * NE - 1 + half, al_set)
            split_low(NE, AHEAD)
            dve.wait_ge(scattered, 16 * (NE - 1))
            dve.tensor_copy(row_out[:, :], dest[:, NE - 1:NE]).then_inc(row_out_set, 1)

        @block.tensor
        def _(pe):
            def slots(e):
                pe.wait_ge(pick_set, e + 1)
                for t in range(NT):
                    last = pe.matmul(banks[7][:, 0:3], pick[:, t, :],
                                     tab[:, t, :, bass.ds(e, 1)].rearrange("p a b -> p (a b)"),
                                     start=(t == 0), stop=(t == NT - 1))
                last.then_inc(slots_ready, 1)

            def transpose_half(src, half, signal):
                for k in range(4):
                    last = pe.transpose(banks[6 + half][:, k * P:(k + 1) * P],
                                        src[:, (4 * half + k) * P:(4 * half + k + 1) * P], ident[:, :])
                last.then_inc(signal, 1)

            def start_with_bias(first, count, sel, at):
                for n in range(count):
                    pe.matmul(banks[first + n][:, :], sel[:, :], bias[:, at + 512 * n:at + 512 * n + 512],
                              start=True, stop=False)

            def three_products(bank, high, low, w, cols, stop):
                pe.matmul(bank, high, wh[:, w, cols], start=False, stop=False)
                pe.matmul(bank, high, wl[:, w, cols], start=False, stop=False)
                return pe.matmul(bank, low, wh[:, w, cols], start=False, stop=stop)

            def products_h(e, turn0=False):
                pe.wait_ge(selh_set, e + 1)
                start_with_bias(0, 4, sel_h, 0)
                pe.wait_ge(xl_set, e * 2 + 2)
                for k in range(KD):
                    if not turn0 and k == 2:
                        pe.wait_ge(act_set, e)
                        for half in range(2):
                            transpose_half(sg, half, aT_ready)
                    if turn0 and k == 4:
                        slots(2)
                    if turn0 and k == 6:
                        pe.wait_ge(gathered, 32)
                        transpose_half(xg, 0, xT_ready)
                        pe.wait_ge(slots_taken, 3)
                        transpose_half(xg, 1, xT_ready)
                    pe.wait_ge(wl_set, number(e, k) + 1)
                    for n in range(4):
                        last = three_products(banks[n][:, :], xh[:, k, :], xl[:, k, :], slot(k, turn0, SPLIT),
                                              slice(512 * n, 512 * n + 512), k == KD - 1)
                    last.then_inc(unit_used, 1)

            def products_y(e, first, qs):
                for q in qs:
                    if q == 0:
                        pe.wait_ge(sely_set, e)
                        start_with_bias(4, 2, sel_y, 2 * DE)
                        pe.wait_ge(al_set, e * 2)
                    pe.wait_ge(wl_set, number(e, first + q) + 1)
                    for k in (2 * q, 2 * q + 1):
                        for n in range(2):
                            at = 1024 * (k % 2) + 512 * n
                            last = three_products(banks[4 + n][:, :], ah[:, k, :], al[:, k, :],
                                                  slot(first + q, False, SPLIT), slice(at, at + 512), k == KD - 1)
                    last.then_inc(unit_used, 1)

            slots(0)
            pe.wait_ge(slots_taken, 1)
            slots(1)
            pe.wait_ge(gathered, 16)
            transpose_half(xg, 0, xT_ready)
            pe.wait_ge(slots_taken, 2)
            transpose_half(xg, 1, xT_ready)
            products_h(0, True)
            with pe.Fori(1, NE) as e:
                pe.wait_ge(hu_set, e * 2)
                products_h(e)
                pe.wait_ge(al_set, e * 2)
                slots(e + 2)
                pe.wait_ge(gathered, e * 16 + 32)
                transpose_half(xg, 0, xT_ready)
                pe.wait_ge(row_out_set, e)
                products_y(e, KD, range(0, 2))
                pe.wait_ge(slots_taken, e + 3)
                transpose_half(xg, 1, xT_ready)
                products_y(e, KD, range(2, 4))
            pe.wait_ge(act_set, NE)
            pe.wait_ge(xl_set, 2 * NE + 2)
            for half in range(2):
                transpose_half(sg, half, aT_ready)
            pe.wait_ge(y_set, 2 * NE - 2)
            products_y(NE, 0, range(4))


def further_blocks(nc, sem, banks, ring, ident, tab, rk, bias, eq, slot_iota, counts, xn2_rows, pair_rows, w_exp1, w_exp2):
    with ExitStack() as ctx:
        def sb(name, shape, dt=F32):
            return ctx.enter_context(nc.sbuf_tensor(name, shape, dt))

        others = sb("f_units", [P, PER_E - RAW, UW])

        def unit(u):
            return ring[:, u, :] if u < RAW else others[:, u - RAW, :]

        pick = sb("f_pick", [P, NT, P])
        rank_here = sb("f_rank", [P, NT])
        sel = sb("f_sel", [96, P], BF16)
        row_in = sb("f_row_in", [P, 1], U32)
        row_out = sb("f_row_out", [P, 1], U32)
        gate = sb("f_gate", [P, 1])
        xg = sb("f_xg", [P, D])
        xgT = sb("f_xgT", [P, KD, P])
        hg = sb("f_hg", [P, DE])
        hu = sb("f_hu", [P, DE])
        sg = sb("f_sg", [P, DE])
        act_sb = sb("f_act", [P, DE])
        actT = sb("f_actT", [P, KD, P])
        y = sb("f_y", [P, D])
        onesb = sb("f_onesb", [96, P], BF16)
        more = sb("f_more", [P, 3, NE])
        extra = sb("f_extra", [P, NE])
        upto = sb("f_upto", [P, NE])
        upto2 = sb("f_upto2", [P, NE])
        done = sb("f_done", [P, OVER, NE])
        whose = sb("f_whose", [P, OVER])
        behind = sb("f_behind", [P, OVER])
        first = sb("f_first", [P, OVER])
        number = sb("f_number", [P, OVER])
        whose_i = sb("f_whose_i", [P, OVER], I32)

        f_consts, f_table = sem("f_consts"), sem("f_table")
        f_landed, f_step = sem("f_landed"), sem("f_step")
        f_picked, f_slots, f_rows, f_gathered = sem("f_picked"), sem("f_slots"), sem("f_rows"), sem("f_gathered")
        f_T, f_T_taken = sem("f_T"), sem("f_T_taken")
        f_h, f_hg, f_sig = sem("f_h"), sem("f_hg_set"), sem("f_sig")
        f_act_set, f_y_ready = sem("f_act_set"), sem("f_y_ready")
        f_y_set, f_scattered = sem("f_y_set"), sem("f_scattered")
        f_carried = sem("f_carried")
        zero = sb("f_zero", [P, 1])
        carried = sb("f_carry", [P, 2])
        block = ctx.enter_context(nc.Block())

        def expert_of(engine, j):
            return engine.value_load(whose_i[0:1, bass.ds(j, 1)], min_val=0, max_val=NE - 1)

        @block.sync
        def _(sp):
            sp.wait_ge(f_table, 1)
            with sp.Fori(0, OVER) as j:
                e = expert_of(sp, j)
                sp.wait_ge(f_picked, j + 1)
                for k in range(KD):
                    sp.dma_start(unit(k), w_exp1[bass.ds(e, 1), k * P:(k + 1) * P, :]
                                 .rearrange("a p n -> (a p) n")).then_inc(f_landed, 16)
                for q in range(4):
                    sp.dma_start(unit(8 + q).rearrange("p (k n) -> p k n", k=2), w_exp2[bass.ds(e, 1), 2 * q * P:2 * (q + 1) * P, :]
                                 .rearrange("a (k p) n -> p (a k) n", p=P)).then_inc(f_landed, 16)

        @block.gpsimd
        def _(pool):
            pool.memset(xg[:, :], 0.0).then_inc(f_consts, 1)
            pool.memset(onesb[:, :], 1.0).then_inc(f_consts, 1)
            pool.memset(zero[:, :], 0.0).then_inc(f_consts, 1)
            pool.iota(number[:, :], pattern=[[1, OVER]], base=0, channel_multiplier=0,
                      allow_small_or_imprecise_dtypes=True).then_inc(f_consts, 1)
            pool.wait_ge(f_consts, 4)
            with pool.Fori(0, OVER) as j:
                pool.wait_ge(f_rows, j + 1)
                pool.tensor_tensor(carried[:, 0:1], zero[:, :], zero[:, :], ALU.add).then_inc(f_carried, 1)
                pool.indirect_dma_start(out=xg[:, :], out_offset=None, in_=xn2_rows,
                                        in_offset=bass.IndirectOffsetOnAxis(ap=row_in[:, 0:1], axis=0),
                                        bounds_check=S - 1, oob_is_err=False).then_inc(f_gathered, 16)
                pool.wait_ge(f_y_set, j * 2 + 2)
                pool.tensor_tensor(carried[:, 1:2], zero[:, :], zero[:, :], ALU.add).then_inc(f_carried, 1)
                pool.indirect_dma_start(out=pair_rows,
                                        out_offset=bass.IndirectOffsetOnAxis(ap=row_out[:, 0:1], axis=0),
                                        in_=y[:, :], in_offset=None, bounds_check=S * TK - 1, oob_is_err=False
                                        ).then_inc(f_scattered, 16)
            pool.wait_ge(f_gathered, 16 * OVER)
            pool.wait_ge(f_scattered, 16 * OVER)

        @block.scalar
        def _(act):
            with act.Fori(0, OVER) as j:
                act.wait_ge(f_hg, j * 2 + 2)
                act.activation(sg[:, :], hg[:, :], ACT.Sigmoid, scale=ALPHA).then_inc(f_sig, 1)
                for half in range(2):
                    act.wait_ge(f_T, j * 4 + (half + 3))
                    act.activation(actT[:, 4 * half:4 * half + 4, :].rearrange("p k q -> p (k q)"),
                                   banks[6 + half][:, :], ACT.Copy).then_inc(f_T_taken, 1)
                act.wait_ge(f_y_ready, j + 1)
                for n in range(2):
                    act.activation(y[:, 512 * n:512 * n + 512], banks[4 + n][:, :], ACT.Copy, scale=gate[:, 0:1]
                                   ).then_inc(f_y_set, 1)

        @block.vector
        def _(dve):
            step = Steps(dve, f_step)
            for c in range(3):
                step(dve.tensor_scalar(more[:, c, :], counts[:, :], float(P * (c + 1)), None, ALU.is_gt))
            step(dve.tensor_reduce(extra[:, :], more[:, :, :].rearrange("p c e -> p e c"), AX.X, ALU.add))
            step(dve.tensor_copy(upto[:, :], extra[:, :]))
            here, there = upto, upto2
            for shift in (1, 2, 4, 8, 16):
                step(dve.tensor_copy(there[:, 0:shift], here[:, 0:shift]))
                step(dve.tensor_tensor(there[:, shift:NE], here[:, shift:NE], here[:, 0:NE - shift], ALU.add))
                here, there = there, here
            dve.wait_ge(f_consts, 4)
            for j in range(OVER):
                step(dve.tensor_scalar(done[:, j, :], here[:, :], float(j), None, ALU.is_le))
            step(dve.tensor_reduce(whose[:, :], done[:, :, :], AX.X, ALU.add))
            for j in range(OVER):
                step(dve.tensor_tensor(done[:, j, :], done[:, j, :], extra[:, :], ALU.mult))
            step(dve.tensor_reduce(behind[:, :], done[:, :, :], AX.X, ALU.add))
            step(dve.tensor_tensor(first[:, :], number[:, :], behind[:, :], ALU.subtract))
            step(dve.tensor_scalar(first[:, :], first[:, :], 1.0, float(P), ALU.add, ALU.mult))
            step(dve.tensor_scalar(behind[:, :], whose[:, :], float(NE), BIG, ALU.is_ge, ALU.mult))
            step(dve.tensor_tensor(first[:, :], first[:, :], behind[:, :], ALU.add))
            step(dve.tensor_scalar(whose[:, :], whose[:, :], float(NE - 1), None, ALU.min))
            dve.tensor_copy(whose_i[:, :], whose[:, :]).then_inc(f_table, 1)
            dve.wait_ge(f_table, 1)
            with dve.Fori(0, OVER) as j:
                step.enter(j, 5)
                e = expert_of(dve, j)
                step(dve.tensor_scalar(rank_here[:, :], rk[:, :, bass.ds(e, 1)].rearrange("p t a -> p (t a)"),
                                       first[:, bass.ds(j, 1)], None, ALU.subtract))
                for t in range(NT):
                    last = dve.tensor_scalar(pick[:, t, :], slot_iota[:, :], rank_here[:, t:t + 1], None,
                                             ALU.is_equal)
                step(last)
                dve.tensor_scalar(sel[:, :], onesb[:, :], eq[:, bass.ds(e, 1)], None, ALU.mult).then_inc(f_picked, 1)
                dve.wait_ge(f_slots, j + 1)
                dve.tensor_copy(gate[:, :], banks[7][:, 2:3])
                dve.tensor_scalar(row_out[:, :], banks[7][:, 1:2], BIG, None, ALU.add)
                dve.tensor_scalar(row_in[:, :], banks[7][:, 0:1], BIG, None, ALU.add).then_inc(f_rows, 1)
                for half in range(2):
                    dve.wait_ge(f_T, j * 4 + (half + 1))
                    dve.tensor_copy(xgT[:, 4 * half:4 * half + 4, :].rearrange("p k q -> p (k q)"),
                                    banks[6 + half][:, :]).then_inc(f_T_taken, 1)
                dve.wait_ge(f_h, j + 1)
                for n in range(2):
                    dve.tensor_scalar(hg[:, 512 * n:512 * n + 512], banks[n][:, :], LIMIT, None, ALU.min
                                      ).then_inc(f_hg, 1)
                for n in range(2):
                    step(dve.tensor_scalar(hu[:, 512 * n:512 * n + 512], banks[2 + n][:, :], LIMIT, -LIMIT, ALU.min,
                                           ALU.max))
                step(dve.scalar_tensor_tensor(hu[:, :], hu[:, :], 1.0, hg[:, :], ALU.add, ALU.mult))
                dve.wait_ge(f_sig, j + 1)
                dve.tensor_tensor(act_sb[:, :], hu[:, :], sg[:, :], ALU.mult).then_inc(f_act_set, 1)
                dve.wait_ge(f_scattered, j * 16 + 16)
                dve.wait_ge(f_carried, j * 2 + 2)
                step.leave(OVER)

        @block.tensor
        def _(pe):
            pe.wait_ge(f_table, 1)
            with pe.Fori(0, OVER) as j:
                e = expert_of(pe, j)
                pe.wait_ge(f_picked, j + 1)
                for t in range(NT):
                    last = pe.matmul(banks[7][:, 0:3], pick[:, t, :],
                                     tab[:, t, :, bass.ds(e, 1)].rearrange("p a b -> p (a b)"),
                                     start=(t == 0), stop=(t == NT - 1))
                last.then_inc(f_slots, 1)
                pe.wait_ge(f_rows, j + 1)
                pe.wait_ge(f_gathered, j * 16 + 16)
                for half in range(2):
                    for k in range(4):
                        last = pe.transpose(banks[6 + half][:, k * P:(k + 1) * P],
                                            xg[:, (4 * half + k) * P:(4 * half + k + 1) * P], ident[:, :])
                    last.then_inc(f_T, 1)
                pe.wait_ge(f_T_taken, j * 4 + 2)
                pe.wait_ge(f_landed, j * (16 * PER_E) + 16 * PER_E)
                for n in range(4):
                    pe.matmul(banks[n][:, :], sel[:, :], bias[:, 512 * n:512 * n + 512], start=True, stop=False)
                    for k in range(KD):
                        last = pe.matmul(banks[n][:, :], xgT[:, k, :], unit(k)[:, 512 * n:512 * n + 512],
                                         start=False, stop=(k == KD - 1))
                last.then_inc(f_h, 1)
                pe.wait_ge(f_act_set, j + 1)
                for half in range(2):
                    for k in range(4):
                        last = pe.transpose(banks[6 + half][:, k * P:(k + 1) * P],
                                            act_sb[:, (4 * half + k) * P:(4 * half + k + 1) * P], ident[:, :])
                    last.then_inc(f_T, 1)
                pe.wait_ge(f_T_taken, j * 4 + 4)
                for n in range(2):
                    pe.matmul(banks[4 + n][:, :], sel[:, :], bias[:, 2 * DE + 512 * n:2 * DE + 512 * n + 512],
                              start=True, stop=False)
                    for k in range(KD):
                        last = pe.matmul(banks[4 + n][:, :], actT[:, k, :],
                                         unit(8 + k // 2)[:, 1024 * (k % 2) + 512 * n:1024 * (k % 2) + 512 * n + 512],
                                         start=False, stop=(k == KD - 1))
                last.then_inc(f_y_ready, 1)


def combine(nc, sem, x_sb, pair_rows, out_rows):
    W = D // 2
    PIECES = [(t, slice(half * W, (half + 1) * W)) for t in range(NT) for half in range(2)]
    pairs_loaded = [sem(f"pairs_loaded{i}") for i in range(len(PIECES))]
    summed, x_summed, out_stored = sem("summed"), sem("x_summed"), sem("out_stored")
    src = pair_rows.rearrange("(t p k) d -> t p k d", p=P, k=TK)
    with nc.sbuf_tensor("pairs", [P, len(PIECES), TK, W], F32) as pairs, nc.Block() as block:
        @block.sync
        def _(sp):
            for i, (t, cols) in enumerate(PIECES):
                sp.dma_start(pairs[:, i, :, :], src[t][:, :, cols]).then_inc(pairs_loaded[i], 16)
            for i, (t, cols) in enumerate(PIECES):
                sp.wait_ge(x_summed, i + 1)
                sp.dma_start(out_rows[:, t, cols], x_sb[:, t, cols]).then_inc(out_stored, 16)
            sp.wait_ge(out_stored, 16 * len(PIECES))

        @block.vector
        def _(dve):
            for i, (t, cols) in enumerate(PIECES):
                dve.wait_ge(pairs_loaded[i], 16)
                p = pairs[:, i, :, :]
                dve.tensor_tensor(p[:, 0:2, :], p[:, 0:2, :], p[:, 2:4, :], ALU.add).then_inc(summed, 1)
                dve.wait_ge(summed, 2 * i + 1)
                dve.tensor_tensor(p[:, 0, :], p[:, 0, :], p[:, 1, :], ALU.add).then_inc(summed, 1)
                dve.wait_ge(summed, 2 * i + 2)
                dve.tensor_tensor(x_sb[:, t, cols], x_sb[:, t, cols], p[:, 0, :], ALU.add).then_inc(x_summed, 1)


_INS = ['x', 'norm1_g', 'w_in', 'q_lat_g', 'w_uq', 'q_norm_g', 'kv_norm_g', 'w_uv', 'w_q_idx', 'k_idx_g',
        'gmlp_v_g', 'w_spatial', 'b_spatial', 'w_proj_a', 'w_proj_b', 'w_out', 'norm2_g',
        'w_router', 'b_router', 'w_exp1', 'b_exp1', 'w_exp2', 'b_exp2']


def kernel(**inputs):
    import numpy as np
    import concourse.bacc as bacc
    from concourse.bass_utils import run_bass_kernel_spmd

    nc = bacc.Bacc("TRN2", target_bir_lowering=False, num_devices=1)
    arrays, args = {}, []
    for name in _INS:
        a = np.ascontiguousarray(inputs[name])
        arrays[f"in_{name}"] = a
        args.append(nc.dram_tensor(f"in_{name}", a.shape, mybir.dt.from_np(a.dtype), kind="ExternalInput").ap())
    shape = inputs["x"].shape
    args.append(nc.dram_tensor("out_y", shape, F32, kind="ExternalOutput").ap())
    build(nc, *args)
    got = run_bass_kernel_spmd(nc, [arrays], core_ids=[0])
    return got.results[0]["out_y"]
```
